# Optimizing a Trainium2 kernel written in Bass

```python
import math
import jax
import jax.numpy as jnp
from jax import lax
import numpy as np

D_MODEL = 1024
BATCH = 1
SEQ = 512
DEPTH = 1

CHUNK = 64
Q_BLOCK = 128
ROPE_THETA = 10000.0
NORM_EPS = 1e-6

DA_HEADS = 4
DA_QK_DIM = 64
DA_V_DIM = 2 * DA_QK_DIM
DA_WIDTH = DA_HEADS * DA_V_DIM

HG_HEADS = 4
HG_DIM = 128
HG_WIDTH = HG_HEADS * HG_DIM

RW_HEADS = 8
RW_DIM = 64
RW_WIDTH = RW_HEADS * RW_DIM
RW_DECAY_LORA = 64
RW_A_LORA = 64
RW_V_LORA = 32
RW_GATE_LORA = 128
RW_GN_EPS = 64e-5
RW_COLS = (RW_WIDTH, RW_WIDTH, RW_WIDTH, RW_DECAY_LORA, RW_A_LORA, RW_GATE_LORA)
RW_SHIFT_WIDTH = sum(RW_COLS)
RW_SPLIT_IDX = tuple(np.cumsum(RW_COLS)[:-1].tolist())

N_BRANCHES = 3
FFN_HIDDEN = -(-8 * D_MODEL // (3 * 256)) * 256
ADA_WIDTH = 6 * D_MODEL

COL_SIZES = (
    2 * DA_HEADS * DA_QK_DIM, 2 * DA_HEADS * DA_QK_DIM, DA_WIDTH,
    HG_WIDTH, HG_WIDTH, HG_WIDTH, HG_WIDTH,
    RW_SHIFT_WIDTH,
    N_BRANCHES * D_MODEL,
)
IN_COLS = sum(COL_SIZES)
SPLIT_IDX = tuple(np.cumsum(COL_SIZES)[:-1].tolist())

kernel_name = "chunk_causal_hybrid_diffattn_hgrn2_rwkv7"

def rms_norm(x, w, eps=NORM_EPS):
    xf = x.astype(jnp.float32)
    y = xf * lax.rsqrt(jnp.mean(xf * xf, axis=-1, keepdims=True) + eps)
    return (y * w.astype(jnp.float32)).astype(x.dtype)

def rope_tables(positions):
    inv_freq = ROPE_THETA ** (-jnp.arange(0, DA_QK_DIM, 2, dtype=jnp.float32) / DA_QK_DIM)
    ang = positions.astype(jnp.float32)[..., None] * inv_freq
    return jnp.cos(ang), jnp.sin(ang)

def apply_rope(x, cos, sin):
    cos = cos[:, :, None, None, :]
    sin = sin[:, :, None, None, :]
    x1, x2 = jnp.split(x, 2, axis=-1)
    return jnp.concatenate([x1 * cos - x2 * sin, x2 * cos + x1 * sin], axis=-1)

def diff_attention(q, k, v, cos, sin, lam_vecs, subln_w, layer_idx):
    Bn, Sn = q.shape[0], q.shape[1]
    q = apply_rope(q.reshape(Bn, Sn, DA_HEADS, 2, DA_QK_DIM).astype(jnp.float32), cos, sin) * (DA_QK_DIM ** -0.5)
    k = apply_rope(k.reshape(Bn, Sn, DA_HEADS, 2, DA_QK_DIM).astype(jnp.float32), cos, sin)
    v = v.reshape(Bn, Sn, DA_HEADS, DA_V_DIM).astype(jnp.float32)
    lam_init = 0.8 - 0.6 * math.exp(-0.3 * layer_idx)
    lv = lam_vecs.astype(jnp.float32)
    lam = jnp.exp(jnp.sum(lv[0] * lv[1])) - jnp.exp(jnp.sum(lv[2] * lv[3])) + lam_init
    outs = []
    for blk in range(Sn // Q_BLOCK):
        start = blk * Q_BLOCK
        end = start + Q_BLOCK
        s = jnp.einsum('bqhme,bkhme->bhmqk', q[:, start:end], k[:, :end])
        q_chunk = (start + jnp.arange(Q_BLOCK)) // CHUNK
        k_chunk = jnp.arange(end) // CHUNK
        allowed = k_chunk[None, :] <= q_chunk[:, None]
        p = jax.nn.softmax(jnp.where(allowed, s, -jnp.inf), axis=-1)
        pd = p[:, :, 0] - lam * p[:, :, 1]
        outs.append(jnp.einsum('bhqk,bkhd->bqhd', pd, v[:, :end]))
    o = jnp.concatenate(outs, axis=1)
    o = rms_norm(o, subln_w) * (1.0 - lam_init)
    return o.reshape(Bn, Sn, DA_WIDTH)

def hgrn2(f_pre, i_in, q_in, g_in, lb, norm_w):
    Bn, Sn = f_pre.shape[0], f_pre.shape[1]
    nc = Sn // CHUNK
    z = f_pre.astype(jnp.float32)
    lb = lb.astype(jnp.float32)
    log_f = jnp.logaddexp(jnp.log(lb), jnp.log1p(-lb) + jax.nn.log_sigmoid(z))
    key = (1.0 - lb) * jax.nn.sigmoid(-z)

    def to_chunks(t):
        return t.astype(jnp.float32).reshape(Bn, nc, CHUNK, HG_HEADS, HG_DIM).transpose(1, 0, 3, 2, 4)

    causal = jnp.tril(jnp.ones((CHUNK, CHUNK), dtype=bool))

    def chunk_step(state, inp):
        qc, kc, vc, lfc = inp
        b = jnp.cumsum(lfc, axis=2)
        rel = jnp.where(causal[:, :, None], b[:, :, :, None, :] - b[:, :, None, :, :], -jnp.inf)
        scores = jnp.einsum('bhqd,bhkd,bhqkd->bhqk', qc, kc, jnp.exp(rel))
        o_intra = jnp.einsum('bhqk,bhkv->bhqv', scores, vc)
        o_inter = jnp.einsum('bhqd,bhdv->bhqv', qc * jnp.exp(b), state)
        b_last = b[:, :, -1:, :]
        new_state = jnp.exp(b_last)[:, :, 0, :, None] * state + jnp.einsum(
            'bhkd,bhkv->bhdv', kc * jnp.exp(b_last - b), vc)
        return new_state, o_intra + o_inter

    s0 = jnp.zeros((Bn, HG_HEADS, HG_DIM, HG_DIM), jnp.float32)
    _, o = lax.scan(chunk_step, s0, (to_chunks(q_in), to_chunks(key), to_chunks(i_in), to_chunks(log_f)))
    o = o.transpose(1, 0, 3, 2, 4).reshape(Bn, Sn, HG_HEADS, HG_DIM)
    g = jax.nn.silu(g_in.astype(jnp.float32)).reshape(Bn, Sn, HG_HEADS, HG_DIM)
    return (rms_norm(o, norm_w) * g).reshape(Bn, Sn, HG_WIDTH)

def rwkv7(u, mu, w0, w2, a0, a2, g2, k_k, k_a, r_k, gn_w, gn_b, v_first, v_res):
    Bn, Sn = u.shape[0], u.shape[1]
    u = u.astype(jnp.float32)
    u_prev = jnp.pad(u, ((0, 0), (1, 0), (0, 0)))[:, :-1]
    u = u + (u_prev - u) * mu
    r, k, v, w_lo, a_lo, g_lo = jnp.split(u, RW_SPLIT_IDX, axis=-1)
    w = -jax.nn.softplus(-(w0 + jnp.tanh(w_lo) @ w2)) - 0.5
    decay = jnp.exp(-jnp.exp(w))
    a = jax.nn.sigmoid(a0 + a_lo @ a2)
    g = jax.nn.sigmoid(g_lo) @ g2
    if v_res is None:
        v_first = v
    else:
        v0, v1, v2 = v_res
        v = v + (v_first - v) * jax.nn.sigmoid(v0 + (v @ v1) @ v2)

    def heads(t):
        return t.reshape(Bn, Sn, RW_HEADS, RW_DIM)

    kk = heads(k * k_k)
    kk = kk * lax.rsqrt(jnp.maximum(jnp.sum(kk * kk, axis=-1, keepdims=True), 1e-24))
    k = k * (1.0 + (a - 1.0) * k_a)
    r_h, k_h, v_h, w_h, a_h = heads(r), heads(k), heads(v), heads(decay), heads(a)

    def step(state, inp):
        r_t, w_t, k_t, v_t, kk_t, a_t = inp
        sa = jnp.einsum('bhvk,bhk->bhv', state, -kk_t)
        state = (state * w_t[:, :, None, :] + sa[..., None] * (kk_t * a_t)[:, :, None, :]
                 + v_t[..., None] * k_t[:, :, None, :])
        return state, jnp.einsum('bhvk,bhk->bhv', state, r_t)

    s0 = jnp.zeros((Bn, RW_HEADS, RW_DIM, RW_DIM), jnp.float32)
    xs = tuple(t.transpose(1, 0, 2, 3) for t in (r_h, w_h, k_h, v_h, kk, a_h))
    _, o = lax.scan(step, s0, xs)
    o = o.transpose(1, 0, 2, 3)
    mean = jnp.mean(o, axis=-1, keepdims=True)
    var = jnp.mean(jnp.square(o - mean), axis=-1, keepdims=True)
    o = (o - mean) * lax.rsqrt(var + RW_GN_EPS) * gn_w.reshape(RW_HEADS, RW_DIM) + gn_b.reshape(RW_HEADS, RW_DIM)
    o = o + jnp.sum(r_h * k_h * r_k, axis=-1, keepdims=True) * v_h
    return o.reshape(Bn, Sn, RW_WIDTH) * g, v_first

def setup_inputs(seed: int = 0) -> dict:
    key = jax.random.key(seed)
    keys = jax.random.split(key, 40)
    counter = [0]

    def nk():
        counter[0] += 1
        return keys[counter[0] - 1]

    def normal(shape, scale):
        return jax.random.normal(nk(), shape, jnp.float32) * scale

    L, D = DEPTH, D_MODEL
    x = normal((BATCH, SEQ, D), 1.0)
    c = normal((BATCH, D), 1.0)
    offset = jax.random.randint(nk(), (BATCH, 1), 0, 1024, dtype=jnp.int32)
    positions = offset + jnp.arange(SEQ, dtype=jnp.int32)[None, :]
    return {
        "x": x,
        "c": c,
        "positions": positions,
        "ada_w": normal((L, D, ADA_WIDTH), 0.5 * D ** -0.5),
        "ada_b": normal((L, ADA_WIDTH), 0.01),
        "norm_mix_w": 1.0 + normal((L, D), 0.05),
        "norm_ffn_w": 1.0 + normal((L, D), 0.05),
        "w_in": normal((L, D, IN_COLS), D ** -0.5),
        "da_lambda": normal((L, 4, DA_QK_DIM), 0.1),
        "da_subln_w": 1.0 + normal((L, DA_V_DIM), 0.05),
        "hg_lb": normal((L, HG_WIDTH), 0.5),
        "hg_norm_w": 1.0 + normal((L, HG_DIM), 0.05),
        "rw_mu": jax.random.uniform(nk(), (L, RW_SHIFT_WIDTH), jnp.float32, 0.0, 1.0),
        "rw_w0": jax.random.uniform(nk(), (L, RW_WIDTH), jnp.float32, -6.0, -1.0),
        "rw_w2": normal((L, RW_DECAY_LORA, RW_WIDTH), RW_DECAY_LORA ** -0.5),
        "rw_a0": normal((L, RW_WIDTH), 0.1),
        "rw_a2": normal((L, RW_A_LORA, RW_WIDTH), RW_A_LORA ** -0.5),
        "rw_g2": normal((L, RW_GATE_LORA, RW_WIDTH), RW_GATE_LORA ** -0.5),
        "rw_k_k": 0.85 + normal((L, RW_WIDTH), 0.05),
        "rw_k_a": 1.0 + normal((L, RW_WIDTH), 0.05),
        "rw_r_k": normal((L, RW_HEADS, RW_DIM), 0.1),
        "rw_gn_w": 1.0 + normal((L, RW_WIDTH), 0.05),
        "rw_gn_b": normal((L, RW_WIDTH), 0.01),
        "rw_v0": normal((L - 1, RW_WIDTH), 0.1),
        "rw_v1": normal((L - 1, RW_WIDTH, RW_V_LORA), RW_WIDTH ** -0.5),
        "rw_v2": normal((L - 1, RW_V_LORA, RW_WIDTH), RW_V_LORA ** -0.5),
        "w_branch_a": normal((L, DA_WIDTH, D), DA_WIDTH ** -0.5),
        "w_branch_b": normal((L, HG_WIDTH, D), HG_WIDTH ** -0.5),
        "w_branch_c": normal((L, RW_WIDTH, D), RW_WIDTH ** -0.5),
        "w_out": normal((L, D, D), D ** -0.5),
        "ffn_w_in": normal((L, D, 2 * FFN_HIDDEN), D ** -0.5),
        "ffn_w_out": normal((L, FFN_HIDDEN, D), FFN_HIDDEN ** -0.5),
        "final_norm_w": 1.0 + normal((D,), 0.05),
    }

def reference(x, c, positions, ada_w, ada_b, norm_mix_w, norm_ffn_w, w_in, da_lambda, da_subln_w,
              hg_lb, hg_norm_w, rw_mu, rw_w0, rw_w2, rw_a0, rw_a2, rw_g2, rw_k_k, rw_k_a, rw_r_k,
              rw_gn_w, rw_gn_b, rw_v0, rw_v1, rw_v2, w_branch_a, w_branch_b, w_branch_c, w_out,
              ffn_w_in, ffn_w_out, final_norm_w):
    dt = x.dtype
    cos, sin = rope_tables(positions)
    lb_all = jnp.cumsum(jax.nn.softmax(hg_lb.astype(jnp.float32), axis=0), axis=0)
    lb_all = lb_all - lb_all[0]
    c_act = jax.nn.silu(c.astype(jnp.float32))
    v_first = None
    for l in range(DEPTH):
        ada = c_act @ ada_w[l].astype(jnp.float32) + ada_b[l].astype(jnp.float32)
        shift1, scale1, gate1, shift2, scale2, gate2 = [t[:, None, :] for t in jnp.split(ada, 6, axis=-1)]

        h = rms_norm(x, norm_mix_w[l]).astype(jnp.float32) * (1.0 + scale1) + shift1
        u = h.astype(dt) @ w_in[l]
        da_q, da_k, da_v, hg_f, hg_i, hg_q, hg_g, rw_u, gates = jnp.split(u, SPLIT_IDX, axis=-1)
        o_a = diff_attention(da_q, da_k, da_v, cos, sin, da_lambda[l], da_subln_w[l], l)
        o_b = hgrn2(hg_f, hg_i, hg_q, hg_g, lb_all[l], hg_norm_w[l])
        v_res = None if l == 0 else (rw_v0[l - 1], rw_v1[l - 1], rw_v2[l - 1])
        o_c, v_first = rwkv7(rw_u, rw_mu[l], rw_w0[l], rw_w2[l], rw_a0[l], rw_a2[l], rw_g2[l],
                             rw_k_k[l], rw_k_a[l], rw_r_k[l], rw_gn_w[l], rw_gn_b[l], v_first, v_res)
        g_a, g_b, g_c = jnp.split(jax.nn.sigmoid(gates.astype(jnp.float32)), N_BRANCHES, axis=-1)
        merged = g_a * (o_a @ w_branch_a[l]) + g_b * (o_b @ w_branch_b[l]) + g_c * (o_c @ w_branch_c[l])
        mix = merged.astype(dt) @ w_out[l]
        x = x + (gate1 * mix).astype(dt)

        h = rms_norm(x, norm_ffn_w[l]).astype(jnp.float32) * (1.0 + scale2) + shift2
        gate_h, up_h = jnp.split(h.astype(dt) @ ffn_w_in[l], 2, axis=-1)
        ffn = (jax.nn.silu(gate_h) * up_h) @ ffn_w_out[l]
        x = x + (gate2 * ffn).astype(dt)
    return rms_norm(x, final_norm_w)


_drawn_inputs = setup_inputs


def setup_inputs(seed=0):
    import zlib

    import numpy as np

    out = dict(_drawn_inputs(seed))
    spreads = {}
    factors = {'ada_b': 4.685,
     'norm_mix_w': 3.206,
     'norm_ffn_w': 11.448,
     'da_lambda': 5.679,
     'da_subln_w': 49.309,
     'hg_norm_w': 29.911,
     'rw_w2': 7.924,
     'rw_a0': 8.0,
     'rw_k_k': 200.0,
     'rw_k_a': 7.813,
     'rw_gn_w': 64.0,
     'rw_gn_b': 200.0}
    for name, (base, spread) in spreads.items():
        noise = np.random.default_rng([zlib.crc32(name.encode()), seed]).standard_normal(out[name].shape)
        drawn = base * np.exp(spread * noise) if base else spread * noise
        out[name] = jnp.asarray(drawn.astype(out[name].dtype))
    for name, factor in factors.items():
        out[name] = (out[name] * factor).astype(out[name].dtype)
    return out
```

```python
from contextlib import ExitStack

import concourse.bass as bass
from concourse import mybir

F32 = mybir.dt.float32
F32R = mybir.dt.float32r
U8 = mybir.dt.uint8
I32 = mybir.dt.int32
ALU = mybir.AluOpType
ACT = mybir.ActivationFunctionType
AX_X = mybir.AxisListType.X

P = 128
D = 1024
T = 512
KC = D // P
TB = T // P
FFN = 2816
EPS = 1e-6
GN_EPS = 64e-5
DECAY = 0.6065306597126334
LAM_INIT = 0.2
TWO_PI = 6.283185307179586
TURN = (6.28125, 0.0019350051879882812, 3.0198680e-07)
ROUND = 12582912.0
LEVELS = 7

DA_Q, DA_K, DA_V, HG_F, HG_I, HG_Q, HG_G, RW_U, GATES = 0, 512, 1024, 1536, 2048, 2560, 3072, 3584, 5376

V_MU, V_W0, V_A0, V_KK, V_KA, V_RK, V_GNW, V_GNB, V_HGN, V_SUB, V_NM, V_NF, V_C, V_ADAB = (
    0, 14, 18, 22, 26, 30, 34, 38, 42, 43, 44, 52, 60, 68)
NVEC = 116

C_ID, C_PERM, C_ONES, C_BLK, C_MASK, C_MA, C_MB, C_LOW = 0, 128, 256, 384, 512, 1024, 1152, 1280
C_FREQ, C_EPS, C_GEPS, C_HPI, C_SEL, C_SELT = 1408, 1409, 1410, 1411, 1412, 1444
NCONST = C_SELT + 512

RAW = 3
RING = 2
BANKS = 8


def panel_stream(w_in, ada_w, wbr, w_out, f_in, f_out):
    def stationary(w, col, kc=KC):
        return w.rearrange("(k p) n -> p k n", p=P)[:, 0:kc, col:col + 256]

    def moving(w, half, col):
        return w.rearrange("(k p) n -> p k n", p=P)[:, 4 * half:4 * half + 4, col:col + 512]

    out = [("ada", stationary(ada_w, 256 * n)) for n in range(8)]
    mixers = [("w", stationary(w_in, RW_U + 256 * n)) for n in range(7)]
    mixers += [("w", stationary(w_in, base + 256 * n)) for base in (HG_F, HG_Q, HG_G) for n in range(2)]
    mixers += [("w", moving(w_in, half, HG_I)) for half in range(2)]
    mixers += [("w", stationary(w_in, DA_Q + 256 * n)) for n in range(4)]
    mixers += [("w", moving(w_in, half, DA_V)) for half in range(2)]
    late = [("ada", stationary(ada_w, 256 * n)) for n in range(8, 24)]
    for panel in mixers:
        out.append(panel)
        if late:
            out.append(late.pop(0))
    for j in range(4):
        out += [("w", stationary(w_in, GATES + D * g + 256 * j)) for g in range(3)]
        out += [("w", stationary(w, 256 * j, 4)) for w in wbr]
    out += [("w", moving(w_out, half, 512 * n)) for n in range(2) for half in range(2)]
    for j in range(FFN // 256):
        out += [("w", stationary(f_in, 256 * j)), ("w", stationary(f_in, FFN + 256 * j))]
    fo = f_out.rearrange("(k p) n -> p k n", p=P)
    out += [("w", fo[:, 2 * j:2 * j + 2, :]) for j in range(FFN // 256)]
    assert not late
    return out


class Banks:

    def __init__(self):
        self.of, self.count, self.next, self.used = {}, [0] * BANKS, 0, BANKS

    def rotate(self, n):
        self.used, self.next = n, 0

    def add(self, *name, bank=None):
        if bank is None:
            bank = self.next
            self.next = (bank + 1) % self.used
        self.of[name] = (bank, self.count[bank])
        self.count[bank] += 1


def bank_plan():
    b = Banks()
    b.add("vectors")
    for n in range(8):
        b.add("ada", n)
    for kc in range(KC):
        b.add("h", 0, kc)
    late = list(range(8, 24))

    def late_ada():
        if late:
            b.add("ada", late.pop(0))

    for n in range(7):
        b.add("rw", 2 * n)
        b.add("rw", 2 * n + 1)
        late_ada()
    for what in ("rw w", "rw a", "rw kk"):
        for c in range(4):
            b.add(what, c)
    b.add("rw bonus")
    for c in range(TB):
        for x in range(3):
            b.add("rw tok", c, x)
        for g in range(2):
            for hl in range(4):
                b.add("rw sc", c, g, hl)
            b.add("rw n", c, g)
        for i in range(1, LEVELS):
            for g in range(2):
                b.add("rw t", c, g, i)
            for g in range(2):
                if i < LEVELS - 1:
                    b.add("rw p", c, g, i)
                b.add("rw pt", c, g, i)
        for what in ("rw r", "rw u", "rw o") + (("rw m",) if c < TB - 1 else ()):
            for g in range(2):
                b.add(what, c, g)
    for what in ("rw mean", "rw var", "rw bv", "rw g"):
        for c in range(4):
            b.add(what, c)
    for n in range(6):
        b.add("hg", 2 * n)
        b.add("hg", 2 * n + 1)
        late_ada()
    for tb in range(TB):
        b.add("hg v", tb)
    late_ada()
    late_ada()
    for lev in range(LEVELS + 1):
        for c in range(TB):
            b.add("hg sc", lev, c)
    for c in range(TB):
        b.add("hg tok", c)
        b.add("hg o", c)
        if c < TB - 1:
            b.add("hg s", c)
    for h in range(4):
        b.add("hg ss", h)
    for n in range(4):
        b.add("da", 2 * n)
        b.add("da", 2 * n + 1)
        late_ada()
    for tb in range(TB):
        b.add("da v", tb)
    for n in range(8):
        b.add("da rot", n)
    b.rotate(6)
    for h in range(4):
        b.add("da o", h, bank=6 + h % 2)
        for i in range(TB):
            for m in range(2):
                b.add("da s", h, i, m)
            b.add("da pt", h, i)
        b.add("da ss", h)
    b.rotate(8)
    for j in range(4):
        for g in range(3):
            for m in range(2):
                b.add("gate", j, g, m)
        for g in range(3):
            for m in range(2):
                b.add("branch", j, g, m)
    for n in range(2):
        for tb in range(TB):
            b.add("out", n, tb)
    for kc in range(KC):
        b.add("h", 1, kc)
    for j in range(FFN // 256):
        for which in range(2):
            for m in range(2):
                b.add("ffn", j, which, m)
    for tb in range(TB):
        for n in range(2):
            b.add("down", tb, n)
    assert not late
    return b


def panel_ends():
    ends = [("bank", ("rw", 2 * n + 1)) for n in range(7)]
    ends += [("bank", ("hg", 2 * n + 1)) for n in range(6)]
    ends += [("panel used", 1), ("bank", ("hg v", TB - 1))]
    ends += [("bank", ("da", 2 * n + 1)) for n in range(4)]
    ends += [("panel used", 2), ("bank", ("da v", TB - 1))]
    for j in range(4):
        ends += [("bank", ("gate", j, g, 1)) for g in range(3)]
        ends += [("bank", ("branch", j, g, 1)) for g in range(3)]
    for n in range(2):
        ends += [("panel used", 3 + n), ("bank", ("out", n, TB - 1))]
    for j in range(FFN // 256):
        ends += [("bank", ("ffn", j, which, 1)) for which in range(2)]
    ends += [("down k", 2 * j + 2) for j in range(FFN // 256)]
    return ends


def build(nc, x, ada_w, w_in, wba, wbb, wbc, w_out, f_in, f_out, w2, a2, g2,
          vecs, consts, levels, gate_b, final_w, lam, positions, out):
    panels = panel_stream(w_in, ada_w, (wba, wbb, wbc), w_out, f_in, f_out)
    plan = bank_plan()
    with ExitStack() as ctx:
        def sb(name, shape, dt=F32):
            return ctx.enter_context(nc.sbuf_tensor(name, shape, dt))

        raw = sb("raw", [P, RAW, 2048])
        whi = sb("whi", [P, RING, 2048], F32R)
        wlo = sb("wlo", [P, RING, 2048], F32R)
        hhi = sb("hhi", [P, KC, T], F32R)
        hlo = sb("hlo", [P, KC, T], F32R)
        cst = sb("cst", [P, NCONST])
        lev_mask = sb("lev_mask", [P, 2 * LEVELS + 1, P], U8)
        vrow = sb("vrow", [NVEC, P])
        vc = sb("vc", [P, NVEC])
        ca = sb("ca", [P, KC])
        small = sb("small", [P, 160])
        ada_cols = sb("ada_cols", [P, 48])
        gmul = sb("gmul", [P, 2, KC])
        gate_row = sb("gate_row", [P, 2, D])
        ada_acc = sb("ada_acc", [P, 2, 256])

        base = -(-nc.sbuf_base // 64) * 64
        size = (nc.sbuf_usable_end - base) // 64 * 64 - 64
        sb("arena_fence", [P, size // 4 - 16])

        def at(name, kb, shape, dt=F32):
            n = 2 if dt == U8 else 4
            for extent in shape[1:]:
                n *= extent
            assert kb * 1024 + n <= size, (name, kb + n / 1024, size / 1024)
            return nc.alloc_sbuf_tensor_at(name, shape, dt, offset=base + kb * 1024)

        x_in = at("x_in", 0, [P, TB, D])
        x_norm = at("x_norm", 16, [P, TB, D])
        h_tmp = at("h_tmp", 32, [P, 2, T])
        lev_f32 = at("lev_f32", 40, [P, 2 * LEVELS + 1, P])
        oc_hi = at("oc_hi", 0, [P, 4, T], F32R)
        oc_lo = at("oc_lo", 8, [P, 4, T], F32R)
        R = at("R", 16, [P, 4, T])
        K = at("K", 24, [P, 4, T])
        V = at("V", 32, [P, 4, T])
        A = at("A", 40, [P, 4, T])
        B = at("B", 48, [P, 4, T])
        gate_lo = at("gate_lo", 56, [P, T])
        bonus = at("bonus", 58, [8, T])
        lora_w = at("lora_w", 60, [P, 2, T])
        lora_in = at("lora_in", 64, [P, T])
        u_prev = at("u_prev", 66, [P, 2, T + 1])
        decay = at("decay", 71, [P, 4, T])
        cum = at("cum", 79, [P, 4, T])
        tmp = at("tmp", 87, [P, 4, T])
        ARz = at("ARz", 64, [P, 4, 2, 2, P])
        tok = at("tok", 72, [P, 3, T])
        SC = [at("sc0", 78, [P, 4, T]), at("sc1", 0, [P, 4, T])]
        X = at("X", 8, [P, 2, T])
        XT = at("XT", 12, [P, 2, T])
        LX = at("LX", 86, [P, 2, T])
        rhs_u = at("rhs_u", 90, [P, 2, 256])
        U = at("U", 92, [P, 2, 256])
        M = at("M", 94, [P, 4, 64])
        epi = at("epi", 64, [P, 4, T])
        epi2 = at("epi2", 72, [P, 4, T])
        ob_hi = at("ob_hi", 16, [P, 4, T], F32R)
        ob_lo = at("ob_lo", 24, [P, 4, T], F32R)
        Z = at("Z", 16, [P, 4, T])
        Hb = at("Hb", 24, [P, 4, T])
        Hq = at("Hq", 32, [P, 4, T])
        Hg = at("Hg", 40, [P, 4, T])
        Hk = at("Hk", 48, [P, 4, T])
        Hv = at("Hv", 56, [P, TB, T])
        q_lev = at("q_lev", 64, [P, 4, T])
        k_lev = at("k_lev", 72, [P, 4, T])
        ST = at("ST", 80, [P, TB, 4, P])
        Hs = at("Hs", 88, [P, 4, P])
        k_tok = at("k_tok", 90, [P, T])
        oa_hi = at("oa_hi", 32, [P, 4, T], F32R)
        oa_lo = at("oa_lo", 40, [P, 4, T], F32R)
        qk = at("qk", 48, [P, 2, 4, T])
        v_tok = at("v_tok", 64, [P, TB, T])
        cos_sin = at("cos_sin", 72, [P, 2, T])
        rot = at("rot", 76, [P, 4, T])
        prob = at("prob", 76, [P, 2, 2, T])
        probT = at("probT", 84, [P, T])
        pos_i = at("pos_i", 84, [P, T], I32)
        ang = at("ang", 86, [P, 3, T])
        att = at("att", 86, [P, T])
        att2 = at("att2", 88, [P, T])
        lam_in = at("lam_in", 92, [P, 256])
        sg = at("sg", 48, [P, 3, 2, T])
        mg_hi = at("mg_hi", 60, [P, KC, T], F32R)
        mg_lo = at("mg_lo", 76, [P, KC, T], F32R)
        mg = at("mg", 92, [P, 2, T])
        mg_tmp = at("mg_tmp", 96, [P, T])
        x1 = at("x1", 0, [P, TB, D])
        x1_norm = at("x1_norm", 16, [P, TB, D])
        h_tmp2 = at("h_tmp2", 32, [P, 2, T])
        hid = at("hid", 16, [P, FFN // P, T])
        d_hi = at("d_hi", 60, [P, 2, T], F32R)
        d_lo = at("d_lo", 64, [P, 2, T], F32R)
        f_tmp = at("f_tmp", 68, [P, 2, T])
        final_row = at("final_row", 92, [P, D])
        y = at("y", 76, [P, TB, D])

        psum = [ctx.enter_context(nc.psum_tensor(f"bank{b}", [P, T], F32)) for b in range(BANKS)]

        bank_full = [ctx.enter_context(nc.semaphore(f"bank{b}_full")) for b in range(BANKS)]
        bank_free = [ctx.enter_context(nc.semaphore(f"bank{b}_free")) for b in range(BANKS)]
        raw_loaded = [ctx.enter_context(nc.semaphore(f"raw{s}_loaded")) for s in range(RAW)]
        def sem(name):
            return ctx.enter_context(nc.semaphore(name))

        s_act_step = sem("act_step")
        s_angles = sem("angles")
        s_c_act = sem("c_act")
        s_constants_in = sem("constants_in")
        s_cos_sin = sem("cos_sin")
        s_d_hi = sem("d_hi")
        s_d_lo = sem("d_lo")
        s_da_hi = sem("da_hi")
        s_da_lo = sem("da_lo")
        s_da_out = sem("da_out")
        s_da_p = sem("da_p")
        s_da_rstd = sem("da_rstd")
        s_da_sq = sem("da_sq")
        s_down_k = sem("down_k")
        s_dve_step = sem("dve_step")
        s_ffn_sig = sem("ffn_sig")
        s_final_rstd = sem("final_rstd")
        s_final_weight_in = sem("final_weight_in")
        s_gate_bias_in = sem("gate_bias_in")
        s_h_hi = sem("h_hi")
        s_h_lo = sem("h_lo")
        s_hg_neg_abs = sem("hg_neg_abs")
        s_hg_e_b = sem("hg_e_b")
        s_hg_e_last = sem("hg_e_last")
        s_hg_e_left = sem("hg_e_left")
        s_hg_e_rel = sem("hg_e_rel")
        s_hg_hi = sem("hg_hi")
        s_hg_k_left = sem("hg_k_left")
        s_hg_key = sem("hg_key")
        s_hg_last = sem("hg_last")
        s_hg_left = sem("hg_left")
        s_hg_lev = sem("hg_lev")
        s_hg_ln = sem("hg_ln")
        s_hg_ls_less_z = sem("hg_ls_less_z")
        s_hg_out = sem("hg_out")
        s_hg_rel = sem("hg_rel")
        s_hg_rstd = sem("hg_rstd")
        s_hg_split = sem("hg_split")
        s_hg_sq = sem("hg_sq")
        s_lam_dot = sem("lam_dot")
        s_lam_exp = sem("lam_exp")
        s_lambda_in = sem("lambda_in")
        s_lora_in = sem("lora_in")
        s_masks = sem("masks")
        s_masks_in = sem("masks_in")
        s_max = sem("max")
        s_merged = sem("merged")
        s_mg_hi = sem("mg_hi")
        s_mg_sum = sem("mg_sum")
        s_normed = sem("normed")
        s_panel_hi = sem("panel_hi")
        s_panel_taken = sem("panel_taken")
        s_panel_used = sem("panel_used")
        s_pool_step = sem("pool_step")
        s_positions_in = sem("positions_in")
        s_roped = sem("roped")
        s_rw_arz = sem("rw_arz")
        s_rw_e_a = sem("rw_e_a")
        s_rw_e_bk = sem("rw_e_bk")
        s_rw_e_r = sem("rw_e_r")
        s_rw_factor = sem("rw_factor")
        s_rw_hi = sem("rw_hi")
        s_rw_k_k = sem("rw_k_k")
        s_rw_kk2 = sem("rw_kk2")
        s_rw_lora = sem("rw_lora")
        s_rw_norm = sem("rw_norm")
        s_rw_prev = sem("rw_prev")
        s_rw_rkk = sem("rw_rkk")
        s_rw_rstd = sem("rw_rstd")
        s_rw_split = sem("rw_split")
        s_rw_sq = sem("rw_sq")
        s_rw_state = sem("rw_state")
        s_rw_sums = sem("rw_sums")
        s_rw_x = sem("rw_x")
        s_stored = sem("stored")
        s_u_prev_zero = sem("u_prev_zero")
        s_vectors_in = sem("vectors_in")
        s_x_again = sem("x_again")
        s_x_in = sem("x_in")
        s_x1_ready = sem("x1_ready")
        s_x2_ready = sem("x2_ready")
        s_y_ready = sem("y_ready")

        counts = {}

        def up(semaphore):
            counts[semaphore.name] = counts.get(semaphore.name, 0) + 1
            return counts[semaphore.name]

        def bank_of(*use):
            return psum[plan.of[use][0]]

        def full(*use):
            bank, k = plan.of[use]
            return bank_full[bank], k + 1

        def free_sem(*use):
            return bank_free[plan.of[use][0]]

        def freed(*use):
            bank, k = plan.of[use]
            return bank_free[bank], k + 1

        weights = [n for n, (kind, _) in enumerate(panels) if kind == "w"]
        ends = panel_ends()
        assert len(ends) == len(weights)

        def slot_released(eng, m):
            kind, what = ends[m]
            if kind == "bank":
                eng.wait_ge(*full(*what))
            else:
                eng.wait_ge({"panel used": s_panel_used, "down k": s_down_k}[kind], what)

        def loaded(eng, n):
            eng.wait_ge(raw_loaded[n % RAW], 16 * (n // RAW + 1))
            a, cols = panels[n][1].shape[1:]
            return raw[:, n % RAW, 0:a * cols]

        def bcast(ap, *shape):
            return ap.to_broadcast(list(shape))

        def blocks(tile):
            return tile[:, :, :].rearrange("p a (b t) -> p (a b) t", t=P)

        ident = cst[:, C_ID:C_ID + P]
        ones = cst[:, C_ONES:C_ONES + P]
        pair_ones = cst[:, C_BLK:C_BLK + P]
        SS, RSTD, OM_MU, OM_KA, BREF, BLAST, FAC, HLAST, MX, NB, SUM, RS, LR, NLAM, SUBW = (
            0, 4, 8, 22, 26, 42, 58, 74, 90, 92, 94, 96, 98, 100, 101)

        def col(k, n=1):
            return small[:, k:k + n]

        def blk16(k):
            return small[:, k:k + 16]

        block = ctx.enter_context(nc.Block())

        @block.sync
        def _(sp):
            sp.dma_start(vrow[:, :], vecs).then_inc(s_vectors_in, 16)
            sp.dma_start(cst[:, :], consts).then_inc(s_constants_in, 16)
            for n, (kind, src) in enumerate(panels):
                if n >= RAW:
                    sp.wait_ge(s_panel_taken, n - RAW + 1)
                a, cols = src.shape[1:]
                dst = raw[:, n % RAW, 0:a * cols].rearrange("p (a n) -> p a n", a=a)
                sp.dma_start(dst, src).then_inc(raw_loaded[n % RAW], 16)

        @block.gpsimd
        def _(pool):
            pool.dma_start(x_in[:, :, :], x.rearrange("(b p) d -> p b d", p=P)).then_inc(s_x_in, 16)
            pool.dma_start(lev_f32[:, :, :], levels.rearrange("p (l c) -> p l c", c=P)).then_inc(s_masks_in, 16)
            for g in range(2):
                pool.dma_start(gate_row[:, g, :], gate_b[3 * D * g + 2 * D:3 * D * g + 3 * D].rearrange(
                    "(a n) -> a n", a=1).to_broadcast([P, D])).then_inc(s_gate_bias_in, 16)
            pool.dma_start(lora_w[0:64, 0, :], w2).then_inc(s_lora_in, 16)
            pool.dma_start(lora_w[64:128, 0, :], a2).then_inc(s_lora_in, 16)
            pool.dma_start(lora_w[:, 1, :], g2).then_inc(s_lora_in, 16)
            pool.wait_ge(s_masks_in, 16)
            nc.gpsimd.tensor_copy(lev_mask[:, :, :], lev_f32[:, :, :]).then_inc(s_masks, 1)
            pool.wait_ge(s_masks, up(s_masks))
            pool.wait_ge(s_rw_state, 1)
            nc.gpsimd.memset(ARz[0:64, :, 1, :, :], 0.0).then_inc(s_pool_step, 1)
            pool.wait_ge(s_pool_step, up(s_pool_step))
            nc.gpsimd.memset(ARz[64:128, :, 0, :, :], 0.0).then_inc(s_pool_step, 1)
            pool.wait_ge(s_pool_step, up(s_pool_step))
            for c in range(TB):
                if c:
                    pool.wait_ge(*full("rw m", c - 1, 1))
                ts = slice(c * P, c * P + P)
                for par in range(2):
                    rows = slice(64 * par, 64 * par + 64)
                    nc.gpsimd.tensor_copy(ARz[rows, :, par, 0, :], A[rows, :, ts]).then_inc(s_rw_arz, 1)
                    pool.wait_ge(s_rw_arz, up(s_rw_arz))
                    nc.gpsimd.tensor_copy(ARz[rows, :, par, 1, :], R[rows, :, ts]).then_inc(s_rw_arz, 1)
                    pool.wait_ge(s_rw_arz, up(s_rw_arz))
            pool.wait_ge(*full("hg ss", 3))
            pool.wait_ge(s_hg_split, 4)
            pool.dma_start(pos_i[:, :], positions.rearrange("(a n) -> a n", a=1).to_broadcast([P, T])
                           ).then_inc(s_positions_in, 16)
            pool.dma_start(lam_in[:, :], lam.rearrange("(a n) -> a n", a=1).to_broadcast([P, 256])
                           ).then_inc(s_lambda_in, 16)
            pool.wait_ge(*full("branch", 3, 2, 1))
            pool.dma_start(x1[:, :, :], x.rearrange("(b p) d -> p b d", p=P)).then_inc(s_x_again, 16)
            pool.wait_ge(s_x1_ready, 2 * TB)
            pool.dma_start(final_row[:, :], final_w.rearrange("(a n) -> a n", a=1).to_broadcast([P, D])
                           ).then_inc(s_final_weight_in, 16)
            for tb in range(TB):
                pool.wait_ge(s_y_ready, tb + 1)
                pool.dma_start(out[tb * P:tb * P + P, :], y[:, tb, :]).then_inc(s_stored, 16)
            pool.wait_ge(s_stored, 16 * TB)

        @block.scalar
        def _(act):
            do = nc.scalar.activation
            split_next = [0]

            def split_hi():
                m = split_next[0]
                split_next[0] += 1
                if m >= len(weights):
                    return
                src = loaded(act, weights[m])
                if m >= RING:
                    slot_released(act, m - RING)
                do(whi[:, m % RING, 0:src.shape[1]], src, ACT.Copy).then_inc(s_panel_hi, 1)
                act.wait_ge(s_panel_hi, up(s_panel_hi))

            def norm(k, src, dst):
                for tb in range(TB):
                    if k:
                        act.wait_ge(s_x1_ready, TB + tb + 1)
                    do(dst[:, tb, :], src[:, tb, :], ACT.Square, accum_out=col(SS + tb)).then_inc(s_act_step, 1)
                    act.wait_ge(s_act_step, up(s_act_step))
                do(col(RSTD, 4), col(SS, 4), ACT.Ln, scale=1.0 / D, bias=cst[:, C_EPS:C_EPS + 1])\
                    .then_inc(s_act_step, 1)
                act.wait_ge(s_act_step, up(s_act_step))
                do(col(RSTD, 4), col(RSTD, 4), ACT.Exp, scale=-0.5).then_inc(s_act_step, 1)
                act.wait_ge(s_act_step, up(s_act_step))
                for tb in range(TB):
                    do(dst[:, tb, :], src[:, tb, :], ACT.Copy, scale=col(RSTD + tb)).then_inc(s_normed, 1)
                    act.wait_ge(s_normed, up(s_normed))
                for kc in range(KC):
                    act.wait_ge(*freed("h", k, kc))
                    tmp_ = (h_tmp2 if k else h_tmp)[:, kc % 2, :]
                    do(hhi[:, kc, :], tmp_, ACT.Copy).then_inc(s_h_hi, 1)
                    act.wait_ge(s_h_hi, up(s_h_hi))

            act.wait_ge(*freed("vectors"))
            do(ca[:, :], vc[:, V_C:V_C + KC], ACT.Silu).then_inc(s_c_act, 1)
            act.wait_ge(s_c_act, up(s_c_act))
            act.wait_ge(s_x_in, 16)
            act.wait_ge(s_constants_in, 16)
            split_hi()
            norm(0, x_in, x_norm)
            for n in range(7):
                split_hi()
                for b in (2 * n, 2 * n + 1):
                    act.wait_ge(*full("rw", b))
                    ps = bank_of("rw", b)
                    if b >= 2:
                        act.wait_ge(*freed("rw", b - 2))
                    elif b == 0:
                        act.wait_ge(s_u_prev_zero, 1)
                    do(u_prev[:, b % 2, 1:T + 1], ps[:, :], ACT.Copy, scale=vc[:, V_MU + b:V_MU + b + 1])\
                        .then_inc(s_rw_prev, 1)
                    act.wait_ge(s_rw_prev, up(s_rw_prev))
            act.wait_ge(*freed("rw", 13))
            do(lora_in[0:64, :], lora_in[0:64, :], ACT.Tanh).then_inc(s_rw_lora, 1)
            act.wait_ge(s_rw_lora, up(s_rw_lora))
            do(gate_lo[:, :], gate_lo[:, :], ACT.Sigmoid).then_inc(s_rw_lora, 1)
            act.wait_ge(s_rw_lora, up(s_rw_lora))
            for c in range(4):
                act.wait_ge(*full("rw w", c))
                ps = bank_of("rw w", c)
                do(decay[:, c, :], ps[:, :], ACT.Sigmoid, bias=vc[:, V_W0 + c:V_W0 + c + 1]).then_inc(free_sem("rw w", c), 1)
                act.wait_ge(*freed("rw w", c))
            act.wait_ge(s_rw_k_k, 4)
            for c in range(4):
                act.wait_ge(*full("rw a", c))
                ps = bank_of("rw a", c)
                do(B[:, c, :], ps[:, :], ACT.Sigmoid, bias=vc[:, V_A0 + c:V_A0 + c + 1]).then_inc(free_sem("rw a", c), 1)
                act.wait_ge(*freed("rw a", c))
            do(tmp[:, :, :], A[:, :, :], ACT.Square).then_inc(s_rw_kk2, 1)
            act.wait_ge(s_rw_kk2, up(s_rw_kk2))
            act.wait_ge(*freed("rw kk", 3))
            do(tmp[:, :, :], tmp[:, :, :], ACT.Sqrt).then_inc(s_rw_norm, 1)
            act.wait_ge(s_rw_norm, up(s_rw_norm))
            act.wait_ge(s_rw_sums, 1)
            do(tmp[:, :, :], cum[:, :, :], ACT.Exp, scale=-DECAY).then_inc(s_rw_e_r, 1)
            act.wait_ge(s_rw_e_r, up(s_rw_e_r))
            do(decay[:, :, :], decay[:, :, :], ACT.Exp, scale=-DECAY).then_inc(s_rw_e_a, 1)
            act.wait_ge(s_rw_e_a, up(s_rw_e_a))
            do(cum[:, :, :], cum[:, :, :], ACT.Exp, scale=DECAY).then_inc(s_rw_e_bk, 1)
            act.wait_ge(s_rw_e_bk, up(s_rw_e_bk))
            do(blk16(FAC), blk16(FAC), ACT.Exp, scale=-DECAY).then_inc(s_rw_factor, 1)
            act.wait_ge(s_rw_factor, up(s_rw_factor))
            act.wait_ge(s_rw_state, 1)
            for c in range(TB):
                for x_ in range(3):
                    act.wait_ge(*full("rw tok", c, x_))
                    ps = bank_of("rw tok", c, x_)
                    do(tok[:, x_, :], ps[:, :], ACT.Copy).then_inc(free_sem("rw tok", c, x_), 1)
                    act.wait_ge(*freed("rw tok", c, x_))
                for g in range(2):
                    act.wait_ge(*full("rw n", c, g))
                    ps = bank_of("rw n", c, g)
                    do(LX[:, g, :], ps[:, :], ACT.Copy, scale=-1.0).then_inc(free_sem("rw n", c, g), 1)
                    act.wait_ge(*freed("rw n", c, g))
                for i in range(1, LEVELS):
                    for g in range(2):
                        act.wait_ge(*full("rw t", c, g, i))
                        ps = bank_of("rw t", c, g, i)
                        do(LX[:, g, :], ps[:, :], ACT.Copy).then_inc(free_sem("rw t", c, g, i), 1)
                        act.wait_ge(*freed("rw t", c, g, i))
                for what, dst in (("rw r", rhs_u), ("rw u", U)):
                    for g in range(2):
                        act.wait_ge(*full(what, c, g))
                        ps = bank_of(what, c, g)
                        do(dst[:, g, :], ps[:, 0:256], ACT.Copy, scale=-1.0 if dst is rhs_u else 1.0)\
                            .then_inc(free_sem(what, c, g), 1)
                        act.wait_ge(*freed(what, c, g))
                for g in range(2):
                    act.wait_ge(*full("rw o", c, g))
                    ps = bank_of("rw o", c, g)
                    do(R[:, 2 * g:2 * g + 2, c * P:c * P + P], ps[:, 0:256].rearrange("p (b t) -> p b t", b=2), ACT.Copy)\
                        .then_inc(free_sem("rw o", c, g), 1)
                    act.wait_ge(*freed("rw o", c, g))
            act.wait_ge(*freed("rw mean", 3))
            do(epi[:, :, :], R[:, :, :], ACT.Square).then_inc(s_rw_sq, 1)
            act.wait_ge(s_rw_sq, up(s_rw_sq))
            for c in range(4):
                act.wait_ge(*full("rw var", c))
                ps = bank_of("rw var", c)
                do(epi[:, c, :], ps[:, :], ACT.Ln, scale=1.0 / 64, bias=cst[:, C_GEPS:C_GEPS + 1])\
                    .then_inc(free_sem("rw var", c), 1)
                act.wait_ge(*freed("rw var", c))
            do(epi[:, :, :], epi[:, :, :], ACT.Exp, scale=-0.5).then_inc(s_rw_rstd, 1)
            act.wait_ge(s_rw_rstd, up(s_rw_rstd))
            act.wait_ge(*freed("rw g", 3))
            do(oc_hi[:, :, :], epi2[:, :, :], ACT.Copy).then_inc(s_rw_hi, 1)
            act.wait_ge(s_rw_hi, up(s_rw_hi))
            act.wait_ge(s_rw_split, 1)
            for n in range(6):
                split_hi()
                for b in (2 * n, 2 * n + 1):
                    act.wait_ge(*full("hg", b))
                    ps = bank_of("hg", b)
                    dst = (Z, Hq, Hg)[b // 4]
                    do(dst[:, b % 4, :], ps[:, :], ACT.Silu if dst is Hg else ACT.Copy).then_inc(free_sem("hg", b), 1)
                    act.wait_ge(*freed("hg", b))
            split_hi()
            split_hi()
            for tb in range(TB):
                act.wait_ge(*full("hg v", tb))
                ps = bank_of("hg v", tb)
                do(Hv[:, tb, :], ps[:, :], ACT.Copy).then_inc(free_sem("hg v", tb), 1)
                act.wait_ge(*freed("hg v", tb))
            act.wait_ge(s_hg_neg_abs, 1)
            do(q_lev[:, :, :], Hk[:, :, :], ACT.Exp).then_inc(s_act_step, 1)
            act.wait_ge(s_act_step, up(s_act_step))
            do(q_lev[:, :, :], q_lev[:, :, :], ACT.Ln, bias=1.0).then_inc(s_hg_ln, 1)
            act.wait_ge(s_hg_ln, up(s_hg_ln))
            act.wait_ge(s_hg_ls_less_z, 1)
            do(Hk[:, :, :], Hk[:, :, :], ACT.Exp).then_inc(s_hg_key, 1)
            act.wait_ge(s_hg_key, up(s_hg_key))
            act.wait_ge(s_hg_last, 1)
            do(blk16(HLAST), blk16(HLAST), ACT.Exp).then_inc(s_hg_e_last, 1)
            act.wait_ge(s_hg_e_last, up(s_hg_e_last))
            for i in range(LEVELS):
                act.wait_ge(s_hg_rel, i + 1)
                do(Z[:, :, :], Z[:, :, :], ACT.Abs).then_inc(s_act_step, 1)
                act.wait_ge(s_act_step, up(s_act_step))
                do(Z[:, :, :], Z[:, :, :], ACT.Exp, scale=-1.0).then_inc(s_hg_e_rel, 1)
                act.wait_ge(s_hg_e_rel, up(s_hg_e_rel))
            act.wait_ge(s_hg_lev, LEVELS)
            do(Z[:, :, :], Hb[:, :, :], ACT.Exp).then_inc(s_hg_e_b, 1)
            act.wait_ge(s_hg_e_b, up(s_hg_e_b))
            act.wait_ge(s_hg_left, 1)
            do(Z[:, :, :], Z[:, :, :], ACT.Exp, scale=-1.0).then_inc(s_hg_e_left, 1)
            act.wait_ge(s_hg_e_left, up(s_hg_e_left))
            for c in range(TB):
                act.wait_ge(*full("hg tok", c))
                ps = bank_of("hg tok", c)
                do(k_tok[:, :], ps[:, :], ACT.Copy).then_inc(free_sem("hg tok", c), 1)
                act.wait_ge(*freed("hg tok", c))
                act.wait_ge(*full("hg o", c))
                ps = bank_of("hg o", c)
                do(q_lev[:, :, c * P:c * P + P], ps[:, :].rearrange("p (h t) -> p h t", h=4), ACT.Copy)\
                    .then_inc(free_sem("hg o", c), 1)
                act.wait_ge(*freed("hg o", c))
            do(k_lev[:, :, :], q_lev[:, :, :], ACT.Square).then_inc(s_hg_sq, 1)
            act.wait_ge(s_hg_sq, up(s_hg_sq))
            for h in range(4):
                act.wait_ge(*full("hg ss", h))
                ps = bank_of("hg ss", h)
                do(Z[:, h, :], ps[:, :], ACT.Ln, scale=1.0 / P, bias=cst[:, C_EPS:C_EPS + 1])\
                    .then_inc(free_sem("hg ss", h), 1)
                act.wait_ge(*freed("hg ss", h))
            do(Z[:, :, :], Z[:, :, :], ACT.Exp, scale=-0.5).then_inc(s_hg_rstd, 1)
            act.wait_ge(s_hg_rstd, up(s_hg_rstd))
            act.wait_ge(s_hg_out, 4)
            for h in range(4):
                do(ob_hi[:, h, :], q_lev[:, h, :], ACT.Copy).then_inc(s_hg_hi, 1)
                act.wait_ge(s_hg_hi, up(s_hg_hi))
            act.wait_ge(s_hg_split, 4)
            for n in range(4):
                split_hi()
                for b in (2 * n, 2 * n + 1):
                    act.wait_ge(*full("da", b))
                    ps = bank_of("da", b)
                    do(qk[:, b // 4, b % 4, :], ps[:, :], ACT.Copy).then_inc(free_sem("da", b), 1)
                    act.wait_ge(*freed("da", b))
            split_hi()
            split_hi()
            for tb in range(TB):
                act.wait_ge(*full("da v", tb))
                ps = bank_of("da v", tb)
                do(v_tok[:, tb, :], ps[:, :], ACT.Copy).then_inc(free_sem("da v", tb), 1)
                act.wait_ge(*freed("da v", tb))
            act.wait_ge(s_angles, 2)
            do(cos_sin[:, :, :], ang[:, 0:2, :], ACT.Sin).then_inc(s_cos_sin, 1)
            act.wait_ge(s_cos_sin, up(s_cos_sin))
            act.wait_ge(s_lam_dot, 2)
            do(col(LR, 2), col(LR, 2), ACT.Exp).then_inc(s_lam_exp, 1)
            act.wait_ge(s_lam_exp, up(s_lam_exp))
            act.wait_ge(s_roped, 8)
            for h in range(4):
                for i in range(TB):
                    n = (i + 1) * P
                    for m in range(2):
                        u = 2 * (4 * h + i) + m
                        act.wait_ge(s_max, u + 1)
                        if u >= 4:
                            act.wait_ge(*full("da pt", *divmod(4 * h + i - 2, TB)))
                        ps = bank_of("da s", h, i, m)
                        do(prob[:, i % 2, m, 0:n], ps[:, 0:n], ACT.Exp, scale=0.125, bias=col(NB + m), accum_out=col(SUM + m))\
                            .then_inc(free_sem("da s", h, i, m), 1)
                        act.wait_ge(*freed("da s", h, i, m))
                    act.wait_ge(*full("da pt", h, i))
                    ps = bank_of("da pt", h, i)
                    do(probT[:, 0:n], ps[:, 0:n], ACT.Copy).then_inc(free_sem("da pt", h, i), 1)
                    act.wait_ge(*freed("da pt", h, i))
                if h:
                    act.wait_ge(s_da_lo, h)
                act.wait_ge(*full("da o", h))
                ps = bank_of("da o", h)
                do(att[:, :], ps[:, :], ACT.Copy).then_inc(free_sem("da o", h), 1)
                act.wait_ge(*freed("da o", h))
                do(att2[:, :], att[:, :], ACT.Square).then_inc(s_da_sq, 1)
                act.wait_ge(s_da_sq, up(s_da_sq))
                act.wait_ge(*full("da ss", h))
                ps = bank_of("da ss", h)
                do(att2[:, :], ps[:, :], ACT.Ln, scale=1.0 / P, bias=cst[:, C_EPS:C_EPS + 1])\
                    .then_inc(free_sem("da ss", h), 1)
                act.wait_ge(*freed("da ss", h))
                do(att2[:, :], att2[:, :], ACT.Exp, scale=-0.5).then_inc(s_da_rstd, 1)
                act.wait_ge(s_da_rstd, up(s_da_rstd))
                act.wait_ge(s_da_out, h + 1)
                do(oa_hi[:, h, :], att[:, :], ACT.Copy).then_inc(s_da_hi, 1)
                act.wait_ge(s_da_hi, up(s_da_hi))
            act.wait_ge(s_da_lo, 4)
            for j in range(4):
                for g in range(3):
                    split_hi()
                    for m in range(2):
                        act.wait_ge(*full("gate", j, g, m))
                        ps = bank_of("gate", j, g, m)
                        if j and g == 0 and m == 0:
                            act.wait_ge(*freed("branch", j - 1, 2, 1))
                        do(sg[:, g, m, :], ps[:, :], ACT.Sigmoid).then_inc(free_sem("gate", j, g, m), 1)
                        act.wait_ge(*freed("gate", j, g, m))
                for g in range(3):
                    split_hi()
                for m in range(2):
                    act.wait_ge(s_mg_sum, 4 * j + m + 3)
                    do(mg_hi[:, 2 * j + m, :], mg[:, m, :], ACT.Copy).then_inc(s_mg_hi, 1)
                    act.wait_ge(s_mg_hi, up(s_mg_hi))
            for n in range(4):
                split_hi()
            norm(1, x1, x1_norm)
            for j in range(FFN // 256):
                for which in range(2):
                    split_hi()
                    if which == 0:
                        for m in range(2):
                            act.wait_ge(*full("ffn", j, 0, m))
                            ps = bank_of("ffn", j, 0, m)
                            if j:
                                act.wait_ge(*freed("ffn", j - 1, 1, m))
                            do(f_tmp[:, m, :], ps[:, :], ACT.Sigmoid).then_inc(s_ffn_sig, 1)
                            act.wait_ge(s_ffn_sig, up(s_ffn_sig))
            for j in range(FFN // 256):
                for k in range(2):
                    kk = 2 * j + k
                    if kk >= 2:
                        act.wait_ge(s_down_k, kk - 1)
                    do(d_hi[:, k, :], hid[:, kk, :], ACT.Copy).then_inc(s_d_hi, 1)
                    act.wait_ge(s_d_hi, up(s_d_hi))
                split_hi()
            for tb in range(TB):
                act.wait_ge(s_x2_ready, 2 * tb + 2)
                do(y[:, tb, :], x1[:, tb, :], ACT.Square, accum_out=col(SS + tb)).then_inc(s_act_step, 1)
                act.wait_ge(s_act_step, up(s_act_step))
                do(col(RSTD + tb), col(SS + tb), ACT.Ln, scale=1.0 / D, bias=cst[:, C_EPS:C_EPS + 1])\
                    .then_inc(s_act_step, 1)
                act.wait_ge(s_act_step, up(s_act_step))
                do(col(RSTD + tb), col(RSTD + tb), ACT.Exp, scale=-0.5).then_inc(s_final_rstd, 1)
                act.wait_ge(s_final_rstd, up(s_final_rstd))
            assert split_next[0] >= len(weights), (split_next, len(weights))

        @block.vector
        def _(dve):
            v = nc.vector
            stream_next, split_next, taken = [0], [0], [0]

            def tt(out_, a, b, op):
                return v.tensor_tensor(out_, a, b, op)

            def stt(out_, a, s_, b, op0, op1):
                return v.scalar_tensor_tensor(out=out_, in0=a, scalar=s_, in1=b, op0=op0, op1=op1)

            def ts(out_, a, s1, op0, s2=None, op1=None):
                if op1 is None:
                    return v.tensor_scalar(out_, a, s1, None, op0)
                return v.tensor_scalar(out_, a, s1, s2, op0, op1)

            def ada_sum(n, i):
                src = loaded(dve, i).rearrange("p (k n) -> p k n", k=KC)
                acc = ada_acc[:, n % 2, :]
                if n >= 2:
                    dve.wait_ge(*full("ada", n - 2))
                ts(acc, src[:, 0, :], ca[:, 0:1], ALU.mult).then_inc(s_dve_step, 1)
                dve.wait_ge(s_dve_step, up(s_dve_step))
                for k in range(1, KC - 1):
                    stt(acc, src[:, k, :], ca[:, k:k + 1], acc, ALU.mult, ALU.add).then_inc(s_dve_step, 1)
                    dve.wait_ge(s_dve_step, up(s_dve_step))
                stt(acc, src[:, KC - 1, :], ca[:, KC - 1:KC], acc, ALU.mult, ALU.add).then_inc(s_panel_taken, 1)
                dve.wait_ge(s_panel_taken, up(s_panel_taken))

            def ada_out(n):
                dve.wait_ge(*full("ada", n))
                ps = bank_of("ada", n)
                section = n // 4
                if section in (2, 5):
                    row = gate_row[:, section // 3, (n % 4) * 256:(n % 4) * 256 + 256]
                    tt(row, ps[:, 0:256], row, ALU.add).then_inc(free_sem("ada", n), 1)
                    dve.wait_ge(*freed("ada", n))
                else:
                    tt(ada_cols[:, 2 * n:2 * n + 2], ps[:, 0:2], vc[:, V_ADAB + 2 * n:V_ADAB + 2 * n + 2], ALU.add)\
                        .then_inc(free_sem("ada", n), 1)
                    dve.wait_ge(*freed("ada", n))

            def take_panel():
                m = split_next[0]
                split_next[0] += 1
                if m >= len(weights):
                    return
                i = weights[m]
                src = loaded(dve, i)
                dve.wait_ge(s_panel_hi, m + 1)
                n = src.shape[1]
                tt(wlo[:, m % RING, 0:n], src, whi[:, m % RING, 0:n].bitcast(F32), ALU.subtract)\
                    .then_inc(s_panel_taken, 1)
                dve.wait_ge(s_panel_taken, up(s_panel_taken))
                if i + 1 < len(panels) and panels[i + 1][0] == "ada":
                    ada_sum(8 + taken[0], i + 1)
                    taken[0] += 1

            def normed_blocks(k):
                stt(gmul[:, k, :], ada_cols[:, 24 * k + 8:24 * k + 16], 1.0, vc[:, (V_NF if k else V_NM):(V_NF if k else V_NM) + KC], ALU.add, ALU.mult)\
                    .then_inc(s_dve_step, 1)
                dve.wait_ge(s_dve_step, up(s_dve_step))
                for kc in range(KC):
                    dve.wait_ge(*full("h", k, kc))
                    ps = bank_of("h", k, kc)
                    tmp_ = (h_tmp2 if k else h_tmp)[:, kc % 2, :]
                    ts(tmp_, ps[:, :], gmul[:, k, kc:kc + 1], ALU.mult, ada_cols[:, 24 * k + kc:24 * k + kc + 1], ALU.add)\
                        .then_inc(free_sem("h", k, kc), 1)
                    dve.wait_ge(*freed("h", k, kc))
                    dve.wait_ge(s_h_hi, 8 * k + kc + 1)
                    tt(hlo[:, kc, :], tmp_, hhi[:, kc, :].bitcast(F32), ALU.subtract).then_inc(s_h_lo, 1)
                    dve.wait_ge(s_h_lo, up(s_h_lo))

            dve.wait_ge(*full("vectors"))
            ps = bank_of("vectors")
            v.tensor_copy(vc[:, :], ps[:, 0:NVEC]).then_inc(free_sem("vectors"), 1)
            dve.wait_ge(*freed("vectors"))
            ts(col(OM_MU, 14), vc[:, V_MU:V_MU + 14], -1.0, ALU.mult, 1.0, ALU.add).then_inc(s_dve_step, 1)
            dve.wait_ge(s_dve_step, up(s_dve_step))
            ts(col(OM_KA, 4), vc[:, V_KA:V_KA + 4], -1.0, ALU.mult, 1.0, ALU.add).then_inc(s_dve_step, 1)
            dve.wait_ge(s_dve_step, up(s_dve_step))
            ts(col(SUBW), vc[:, V_SUB:V_SUB + 1], 1.0 - LAM_INIT, ALU.mult).then_inc(s_dve_step, 1)
            dve.wait_ge(s_dve_step, up(s_dve_step))
            v.memset(u_prev[:, :, 0:1], 0.0).then_inc(s_u_prev_zero, 1)
            dve.wait_ge(s_u_prev_zero, up(s_u_prev_zero))
            dve.wait_ge(s_c_act, 1)
            dve.wait_ge(s_gate_bias_in, 32)
            for n in range(8):
                ada_sum(n, n)
                if n:
                    ada_out(n - 1)
            ada_out(7)
            take_panel()
            normed_blocks(0)
            dve.wait_ge(s_masks, 1)
            for n in range(7):
                take_panel()
                for b in (2 * n, 2 * n + 1):
                    dve.wait_ge(s_rw_prev, b + 1)
                    ps = bank_of("rw", b)
                    dst = (R[:, b, :] if b < 4 else K[:, b - 4, :] if b < 8 else V[:, b - 8, :] if b < 12
                           else lora_in[:, :] if b == 12 else gate_lo[:, :])
                    stt(dst, ps[:, :], col(OM_MU + b), u_prev[:, b % 2, 0:T], ALU.mult, ALU.add)\
                        .then_inc(free_sem("rw", b), 1)
                    dve.wait_ge(*freed("rw", b))
                ada_out(8 + n)
            for c in range(4):
                ts(A[:, c, :], K[:, c, :], vc[:, V_KK + c:V_KK + c + 1], ALU.mult).then_inc(s_rw_k_k, 1)
                dve.wait_ge(s_rw_k_k, up(s_rw_k_k))
            for c in range(4):
                dve.wait_ge(*full("rw kk", c))
                ts(tmp[:, c, :], bank_of("rw kk", c)[:, :], 1e-24, ALU.max).then_inc(free_sem("rw kk", c), 1)
                dve.wait_ge(*freed("rw kk", c))
            dve.wait_ge(s_rw_norm, 1)
            v.reciprocal(tmp[:, :, :], tmp[:, :, :]).then_inc(s_dve_step, 1)
            dve.wait_ge(s_dve_step, up(s_dve_step))
            tt(A[:, :, :], A[:, :, :], tmp[:, :, :], ALU.mult).then_inc(s_dve_step, 1)
            dve.wait_ge(s_dve_step, up(s_dve_step))
            for c in range(4):
                ts(cum[:, c, :], B[:, c, :], vc[:, V_KA + c:V_KA + c + 1], ALU.mult, col(OM_KA + c), ALU.add)\
                    .then_inc(s_dve_step, 1)
                dve.wait_ge(s_dve_step, up(s_dve_step))
            tt(K[:, :, :], K[:, :, :], cum[:, :, :], ALU.mult).then_inc(s_dve_step, 1)
            dve.wait_ge(s_dve_step, up(s_dve_step))
            for c in range(4):
                stt(cum[:, c, :], R[:, c, :], vc[:, V_RK + c:V_RK + c + 1], K[:, c, :], ALU.mult, ALU.mult)\
                    .then_inc(s_rw_rkk, 1)
                dve.wait_ge(s_rw_rkk, up(s_rw_rkk))
            dve.wait_ge(*full("rw bonus"))
            v.tensor_copy(bonus[:, :], bank_of("rw bonus")[0:8, :]).then_inc(free_sem("rw bonus"), 1)
            dve.wait_ge(*freed("rw bonus"))
            tt(B[:, :, :], A[:, :, :], B[:, :, :], ALU.mult).then_inc(s_dve_step, 1)
            dve.wait_ge(s_dve_step, up(s_dve_step))
            for n in range(16):
                v.tensor_tensor_scan(blocks(cum)[:, n, :], ones, blocks(decay)[:, n, :], 0.0, ALU.mult, ALU.add)\
                    .then_inc(s_dve_step, 1)
                dve.wait_ge(s_dve_step, up(s_dve_step))
            v.tensor_copy(blk16(BREF), blocks(cum)[:, :, 63]).then_inc(s_dve_step, 1)
            dve.wait_ge(s_dve_step, up(s_dve_step))
            v.tensor_copy(blk16(BLAST), blocks(cum)[:, :, P - 1]).then_inc(s_dve_step, 1)
            dve.wait_ge(s_dve_step, up(s_dve_step))
            tt(decay[:, :, :], cum[:, :, :], decay[:, :, :], ALU.subtract).then_inc(s_dve_step, 1)
            dve.wait_ge(s_dve_step, up(s_dve_step))
            middle = bcast(blk16(BREF).unsqueeze(2), P, 16, P)
            tt(blocks(decay), blocks(decay), middle, ALU.subtract).then_inc(s_dve_step, 1)
            dve.wait_ge(s_dve_step, up(s_dve_step))
            tt(blocks(cum), blocks(cum), middle, ALU.subtract).then_inc(s_dve_step, 1)
            dve.wait_ge(s_dve_step, up(s_dve_step))
            tt(blk16(FAC), blk16(BLAST), blk16(BREF), ALU.subtract).then_inc(s_dve_step, 1)
            dve.wait_ge(s_dve_step, up(s_dve_step))
            fac = blk16(FAC).rearrange("p (a c) -> p a c", c=TB)
            ref = blk16(BREF).rearrange("p (a c) -> p a c", c=TB)
            tt(fac[:, :, 0:TB - 1], fac[:, :, 0:TB - 1], ref[:, :, 1:TB], ALU.add).then_inc(s_rw_sums, 1)
            dve.wait_ge(s_rw_sums, up(s_rw_sums))
            dve.wait_ge(s_rw_e_r, 1)
            tt(R[:, :, :], R[:, :, :], tmp[:, :, :], ALU.mult).then_inc(s_dve_step, 1)
            dve.wait_ge(s_dve_step, up(s_dve_step))
            dve.wait_ge(s_rw_e_a, 1)
            tt(A[:, :, :], A[:, :, :], decay[:, :, :], ALU.mult).then_inc(s_dve_step, 1)
            dve.wait_ge(s_dve_step, up(s_dve_step))
            dve.wait_ge(s_rw_e_bk, 1)
            tt(B[:, :, :], B[:, :, :], cum[:, :, :], ALU.mult).then_inc(s_dve_step, 1)
            dve.wait_ge(s_dve_step, up(s_dve_step))
            tt(K[:, :, :], K[:, :, :], cum[:, :, :], ALU.mult).then_inc(s_dve_step, 1)
            dve.wait_ge(s_dve_step, up(s_dve_step))
            dve.wait_ge(s_rw_factor, 1)
            dve.wait_ge(s_masks, 1)
            v.memset(M[:, :, :], 0.0).then_inc(s_rw_state, 1)
            dve.wait_ge(s_rw_state, up(s_rw_state))

            def four(ap):
                return ap.rearrange("p (h t) -> p h t", h=4)

            def lmask(i, upper):
                return bcast(lev_mask[:, 2 * i + upper, :].unsqueeze(1), P, 4, P)

            id4 = bcast(ident.unsqueeze(1), P, 4, P)
            for c in range(TB):
                for g in range(2):
                    for hl in range(4):
                        dve.wait_ge(*full("rw sc", c, g, hl))
                        ps = bank_of("rw sc", c, g, hl)
                        tt(SC[g][:, hl, :], ps[:, :], cst[:, C_MASK:C_MASK + T], ALU.mult).then_inc(free_sem("rw sc", c, g, hl), 1)
                        dve.wait_ge(*freed("rw sc", c, g, hl))
                for g in range(2):
                    dve.wait_ge(*freed("rw n", c, g))
                    v.tensor_copy(four(X[:, g, :]), id4).then_inc(s_dve_step, 1)
                    dve.wait_ge(s_dve_step, up(s_dve_step))
                    v.tensor_copy(four(XT[:, g, :]), id4).then_inc(s_dve_step, 1)
                    dve.wait_ge(s_dve_step, up(s_dve_step))
                    v.copy_predicated(four(XT[:, g, :]), lmask(0, 1), SC[g][:, :, 0:P]).then_inc(s_dve_step, 1)
                    dve.wait_ge(s_dve_step, up(s_dve_step))
                    v.copy_predicated(four(X[:, g, :]), lmask(0, 0), four(LX[:, g, :])).then_inc(s_rw_x, 1)
                    dve.wait_ge(s_rw_x, up(s_rw_x))
                for i in range(1, LEVELS):
                    for g in range(2):
                        if i < LEVELS - 1:
                            dve.wait_ge(*full("rw p", c, g, i))
                            ps = bank_of("rw p", c, g, i)
                            v.copy_predicated(four(X[:, g, :]), lmask(i, 0), four(ps[:, :])).then_inc(free_sem("rw p", c, g, i), 1)
                            dve.wait_ge(*freed("rw p", c, g, i))
                        dve.wait_ge(*full("rw pt", c, g, i))
                        ps = bank_of("rw pt", c, g, i)
                        v.copy_predicated(four(XT[:, g, :]), lmask(i, 1), four(ps[:, :])).then_inc(free_sem("rw pt", c, g, i), 1)
                        dve.wait_ge(*freed("rw pt", c, g, i))
                if c < TB - 1:
                    for g in range(2):
                        dve.wait_ge(*full("rw m", c, g))
                        ps = bank_of("rw m", c, g)
                        state = M[:, 2 * g:2 * g + 2, :]
                        tt(state, state, ps[:, 0:P].rearrange("p (b v) -> p b v", b=2), ALU.add)\
                            .then_inc(free_sem("rw m", c, g), 1)
                        dve.wait_ge(*freed("rw m", c, g))
                        tt(state, state, bcast(fac[:, 2 * g:2 * g + 2, c:c + 1], P, 2, 64), ALU.mult)\
                            .then_inc(s_rw_state, 1)
                        dve.wait_ge(s_rw_state, up(s_rw_state))
            dve.wait_ge(*freed("rw o", TB - 1, 1))
            for c in range(4):
                dve.wait_ge(*full("rw mean", c))
                ps = bank_of("rw mean", c)
                stt(R[:, c, :], ps[:, :], -1.0 / 64, R[:, c, :], ALU.mult, ALU.add).then_inc(free_sem("rw mean", c), 1)
                dve.wait_ge(*freed("rw mean", c))
            dve.wait_ge(s_rw_rstd, 1)
            tt(R[:, :, :], R[:, :, :], epi[:, :, :], ALU.mult).then_inc(s_dve_step, 1)
            dve.wait_ge(s_dve_step, up(s_dve_step))
            for c in range(4):
                ts(R[:, c, :], R[:, c, :], vc[:, V_GNW + c:V_GNW + c + 1], ALU.mult, vc[:, V_GNB + c:V_GNB + c + 1], ALU.add)\
                    .then_inc(s_dve_step, 1)
                dve.wait_ge(s_dve_step, up(s_dve_step))
            for c in range(4):
                dve.wait_ge(*full("rw bv", c))
                ps = bank_of("rw bv", c)
                tt(epi2[:, c, :], V[:, c, :], ps[:, :], ALU.mult).then_inc(free_sem("rw bv", c), 1)
                dve.wait_ge(*freed("rw bv", c))
            tt(R[:, :, :], R[:, :, :], epi2[:, :, :], ALU.add).then_inc(s_dve_step, 1)
            dve.wait_ge(s_dve_step, up(s_dve_step))
            for c in range(4):
                dve.wait_ge(*full("rw g", c))
                ps = bank_of("rw g", c)
                tt(epi2[:, c, :], R[:, c, :], ps[:, :], ALU.mult).then_inc(free_sem("rw g", c), 1)
                dve.wait_ge(*freed("rw g", c))
            dve.wait_ge(s_rw_hi, 1)
            tt(oc_lo[:, :, :], epi2[:, :, :], oc_hi[:, :, :].bitcast(F32), ALU.subtract).then_inc(s_rw_split, 1)
            dve.wait_ge(s_rw_split, up(s_rw_split))
            for n in range(6):
                take_panel()
                dve.wait_ge(*freed("hg", 2 * n + 1))
                ada_out(15 + n)
            take_panel()
            take_panel()
            ada_out(21)
            ada_out(22)
            stt(Hk[:, :, :], Z[:, :, :], -1.0, Z[:, :, :], ALU.mult, ALU.min).then_inc(s_hg_neg_abs, 1)
            dve.wait_ge(s_hg_neg_abs, up(s_hg_neg_abs))
            dve.wait_ge(s_hg_ln, 1)
            stt(k_lev[:, :, :], Z[:, :, :], 0.0, q_lev[:, :, :], ALU.min, ALU.subtract).then_inc(s_dve_step, 1)
            dve.wait_ge(s_dve_step, up(s_dve_step))
            tt(Hk[:, :, :], k_lev[:, :, :], Z[:, :, :], ALU.subtract).then_inc(s_hg_ls_less_z, 1)
            dve.wait_ge(s_hg_ls_less_z, up(s_hg_ls_less_z))
            for n in range(16):
                v.tensor_tensor_scan(blocks(Hb)[:, n, :], ones, blocks(k_lev)[:, n, :], 0.0, ALU.mult, ALU.add)\
                    .then_inc(s_dve_step, 1)
                dve.wait_ge(s_dve_step, up(s_dve_step))
            v.tensor_copy(blk16(HLAST), blocks(Hb)[:, :, P - 1]).then_inc(s_dve_step, 1)
            dve.wait_ge(s_dve_step, up(s_dve_step))
            v.tensor_copy(blk16(BLAST), blk16(HLAST)).then_inc(s_hg_last, 1)
            dve.wait_ge(s_hg_last, up(s_hg_last))
            v.memset(ST[:, :, :, :], 0.0).then_inc(s_dve_step, 1)
            dve.wait_ge(s_dve_step, up(s_dve_step))
            v.memset(q_lev[:, :, :], 0.0).then_inc(s_dve_step, 1)
            dve.wait_ge(s_dve_step, up(s_dve_step))
            v.memset(k_lev[:, :, :], 0.0).then_inc(s_dve_step, 1)
            dve.wait_ge(s_dve_step, up(s_dve_step))

            def halves(tile, s):
                return tile[:, :, :].rearrange("p a (n s) -> p (a n) s", s=2 * s)

            def rel(i):
                s = 1 << i
                hb = halves(Hb, s)
                tt(halves(Z, s), hb, bcast(hb[:, :, s - 1:s], P, 1024 // s, 2 * s), ALU.subtract)\
                    .then_inc(s_hg_rel, 1)
                dve.wait_ge(s_hg_rel, up(s_hg_rel))

            def gather(lev, mask):
                for c in range(TB):
                    dve.wait_ge(*full("hg sc", lev, c))
                    ps = bank_of("hg sc", lev, c)
                    v.copy_predicated(ST[:, c, :, :], bcast(mask.unsqueeze(1), P, 4, P), four(ps[:, :]))\
                        .then_inc(free_sem("hg sc", lev, c), 1)
                    dve.wait_ge(*freed("hg sc", lev, c))

            for i in range(LEVELS):
                s = 1 << i
                rel(i)
                if i == 0:
                    dve.wait_ge(s_hg_key, 1)
                    gather(0, lev_mask[:, 2 * LEVELS, :])
                else:
                    gather(i, lev_mask[:, 2 * (i - 1) + 1, :])
                dve.wait_ge(s_hg_e_rel, i + 1)
                z, q, k = halves(Z, s), halves(Hq, s), halves(Hk, s)
                tt(halves(q_lev, s)[:, :, s:], q[:, :, s:], z[:, :, s:], ALU.mult).then_inc(s_dve_step, 1)
                dve.wait_ge(s_dve_step, up(s_dve_step))
                tt(halves(k_lev, s)[:, :, :s], k[:, :, :s], z[:, :, :s], ALU.mult).then_inc(s_hg_lev, 1)
                dve.wait_ge(s_hg_lev, up(s_hg_lev))
            gather(LEVELS, lev_mask[:, 2 * LEVELS - 1, :])
            dve.wait_ge(s_hg_e_b, 1)
            tt(Hq[:, :, :], Hq[:, :, :], Z[:, :, :], ALU.mult).then_inc(s_dve_step, 1)
            dve.wait_ge(s_dve_step, up(s_dve_step))
            tt(blocks(Z), blocks(Hb), bcast(blk16(BLAST).unsqueeze(2), P, 16, P), ALU.subtract)\
                .then_inc(s_hg_left, 1)
            dve.wait_ge(s_hg_left, up(s_hg_left))
            dve.wait_ge(s_hg_e_left, 1)
            tt(Hk[:, :, :], Hk[:, :, :], Z[:, :, :], ALU.mult).then_inc(s_hg_k_left, 1)
            dve.wait_ge(s_hg_k_left, up(s_hg_k_left))
            dve.wait_ge(s_hg_e_last, 1)
            for c in range(TB - 1):
                dve.wait_ge(*full("hg s", c))
                ps = bank_of("hg s", c)
                if c == 0:
                    v.tensor_copy(Hs[:, :, :], four(ps[:, :])).then_inc(free_sem("hg s", c), 1)
                    dve.wait_ge(*freed("hg s", c))
                else:
                    for h in range(4):
                        k = HLAST + 4 * h + c
                        stt(Hs[:, h, :], Hs[:, h, :], col(k), ps[:, h * P:h * P + P], ALU.mult, ALU.add)\
                            .then_inc(s_dve_step, 1)
                        dve.wait_ge(s_dve_step, up(s_dve_step))
                    v.tensor_copy(Hs[:, 0, 0:2], Hs[:, 0, 0:2]).then_inc(free_sem("hg s", c), 1)
                    dve.wait_ge(*freed("hg s", c))
            dve.wait_ge(s_hg_rstd, 1)
            for h in range(4):
                tt(q_lev[:, h, :], q_lev[:, h, :], Z[:, h, :], ALU.mult).then_inc(s_dve_step, 1)
                dve.wait_ge(s_dve_step, up(s_dve_step))
                stt(q_lev[:, h, :], q_lev[:, h, :], vc[:, V_HGN:V_HGN + 1], Hg[:, h, :], ALU.mult, ALU.mult)\
                    .then_inc(s_hg_out, 1)
                dve.wait_ge(s_hg_out, up(s_hg_out))
            for h in range(4):
                dve.wait_ge(s_hg_hi, h + 1)
                tt(ob_lo[:, h, :], q_lev[:, h, :], ob_hi[:, h, :].bitcast(F32), ALU.subtract)\
                    .then_inc(s_hg_split, 1)
                dve.wait_ge(s_hg_split, up(s_hg_split))
            for n in range(4):
                take_panel()
                if n == 0:
                    ada_out(23)
            take_panel()
            take_panel()
            dve.wait_ge(s_positions_in, 16)
            dve.wait_ge(s_lambda_in, 16)
            turn, n_ = ang[:, 0, :], ang[:, 1, :]
            v.tensor_copy(ang[:, 2, :], pos_i[:, :]).then_inc(s_dve_step, 1)
            dve.wait_ge(s_dve_step, up(s_dve_step))
            ts(ang[:, 2, :], ang[:, 2, :], cst[:, C_FREQ:C_FREQ + 1], ALU.mult).then_inc(s_dve_step, 1)
            dve.wait_ge(s_dve_step, up(s_dve_step))
            for x_ in (1, 0):
                dst = ang[:, x_, :]
                ts(probT[:, :], ang[:, 2, :], 1.0 / TWO_PI, ALU.mult, 0.0 if x_ else 0.25, ALU.add)\
                    .then_inc(s_dve_step, 1)
                dve.wait_ge(s_dve_step, up(s_dve_step))
                ts(probT[:, :], probT[:, :], ROUND, ALU.add).then_inc(s_dve_step, 1)
                dve.wait_ge(s_dve_step, up(s_dve_step))
                ts(probT[:, :], probT[:, :], ROUND, ALU.subtract).then_inc(s_dve_step, 1)
                dve.wait_ge(s_dve_step, up(s_dve_step))
                stt(dst, probT[:, :], -TURN[0], ang[:, 2, :], ALU.mult, ALU.add).then_inc(s_dve_step, 1)
                dve.wait_ge(s_dve_step, up(s_dve_step))
                stt(dst, probT[:, :], -TURN[1], dst, ALU.mult, ALU.add).then_inc(s_dve_step, 1)
                dve.wait_ge(s_dve_step, up(s_dve_step))
                stt(dst, probT[:, :], -TURN[2], dst, ALU.mult, ALU.add).then_inc(s_dve_step, 1)
                dve.wait_ge(s_dve_step, up(s_dve_step))
                ts(dst, dst, 0.0 if x_ else TWO_PI / 4, ALU.add).then_inc(s_dve_step, 1)
                dve.wait_ge(s_dve_step, up(s_dve_step))
                ts(dst, dst, 3.1415925, ALU.min, -3.1415925, ALU.max).then_inc(s_angles, 1)
                dve.wait_ge(s_angles, up(s_angles))
            for x_ in range(2):
                pair = lam_in[:, 128 * x_:128 * x_ + 128].rearrange("p (a e) -> p a e", a=2)
                tt(pair[:, 0, :], pair[:, 0, :], pair[:, 1, :], ALU.mult).then_inc(s_dve_step, 1)
                dve.wait_ge(s_dve_step, up(s_dve_step))
                v.reduce_sum(col(LR + x_), pair[:, 0, :], AX_X).then_inc(s_lam_dot, 1)
                dve.wait_ge(s_lam_dot, up(s_lam_dot))
            dve.wait_ge(s_lam_exp, 1)
            stt(col(NLAM), col(LR + 1), -LAM_INIT, col(LR), ALU.add, ALU.subtract).then_inc(s_dve_step, 1)
            dve.wait_ge(s_dve_step, up(s_dve_step))
            dve.wait_ge(s_cos_sin, 1)
            for n in range(8):
                dve.wait_ge(*full("da rot", n))
                ps = bank_of("da rot", n)
                x_ = qk[:, n // 4, n % 4, :]
                tt(rot[:, n % 4, :], ps[:, :], cos_sin[:, 1, :], ALU.mult).then_inc(free_sem("da rot", n), 1)
                dve.wait_ge(*freed("da rot", n))
                tt(x_, x_, cos_sin[:, 0, :], ALU.mult).then_inc(s_dve_step, 1)
                dve.wait_ge(s_dve_step, up(s_dve_step))
                tt(x_, x_, rot[:, n % 4, :], ALU.add).then_inc(s_roped, 1)
                dve.wait_ge(s_roped, up(s_roped))
            for h in range(4):
                for i in range(TB):
                    n = (i + 1) * P
                    for m in range(2):
                        dve.wait_ge(*full("da s", h, i, m))
                        ps = bank_of("da s", h, i, m)
                        v.reduce_max(col(MX + m), ps[:, 0:n], AX_X).then_inc(s_dve_step, 1)
                        dve.wait_ge(s_dve_step, up(s_dve_step))
                        ts(col(NB + m), col(MX + m), -0.125, ALU.mult).then_inc(s_max, 1)
                        dve.wait_ge(s_max, up(s_max))
                    dve.wait_ge(*freed("da s", h, i, 1))
                    v.reciprocal(col(RS, 2), col(SUM, 2)).then_inc(s_dve_step, 1)
                    dve.wait_ge(s_dve_step, up(s_dve_step))
                    tt(col(LR), col(RS + 1), col(NLAM), ALU.mult).then_inc(s_dve_step, 1)
                    dve.wait_ge(s_dve_step, up(s_dve_step))
                    p0, p1 = prob[:, i % 2, 0, 0:n], prob[:, i % 2, 1, 0:n]
                    ts(p0, p0, col(RS), ALU.mult).then_inc(s_dve_step, 1)
                    dve.wait_ge(s_dve_step, up(s_dve_step))
                    stt(p0, p1, col(LR), p0, ALU.mult, ALU.add).then_inc(s_da_p, 1)
                    dve.wait_ge(s_da_p, up(s_da_p))
                dve.wait_ge(s_da_rstd, h + 1)
                stt(att[:, :], att[:, :], col(SUBW), att2[:, :], ALU.mult, ALU.mult).then_inc(s_da_out, 1)
                dve.wait_ge(s_da_out, up(s_da_out))
                dve.wait_ge(s_da_hi, h + 1)
                tt(oa_lo[:, h, :], att[:, :], oa_hi[:, h, :].bitcast(F32), ALU.subtract).then_inc(s_da_lo, 1)
                dve.wait_ge(s_da_lo, up(s_da_lo))
            for j in range(4):
                for g in range(6):
                    take_panel()
                for g in range(3):
                    for m in range(2):
                        dve.wait_ge(*full("branch", j, g, m))
                        ps = bank_of("branch", j, g, m)
                        dve.wait_ge(*freed("gate", j, g, m))
                        if g == 0:
                            tt(mg[:, m, :], sg[:, g, m, :], ps[:, :], ALU.mult).then_inc(free_sem("branch", j, g, m), 1)
                            dve.wait_ge(*freed("branch", j, g, m))
                        else:
                            tt(mg_tmp[:, :], sg[:, g, m, :], ps[:, :], ALU.mult).then_inc(free_sem("branch", j, g, m), 1)
                            dve.wait_ge(*freed("branch", j, g, m))
                            tt(mg[:, m, :], mg[:, m, :], mg_tmp[:, :], ALU.add).then_inc(s_mg_sum, 1)
                            dve.wait_ge(s_mg_sum, up(s_mg_sum))
                for m in range(2):
                    dve.wait_ge(s_mg_hi, 2 * j + m + 1)
                    tt(mg_lo[:, 2 * j + m, :], mg[:, m, :], mg_hi[:, 2 * j + m, :].bitcast(F32), ALU.subtract)\
                        .then_inc(s_merged, 1)
                    dve.wait_ge(s_merged, up(s_merged))
            for n in range(4):
                take_panel()
            dve.wait_ge(s_x_again, 16)
            for n in range(2):
                for tb in range(TB):
                    dve.wait_ge(*full("out", n, tb))
                    ps = bank_of("out", n, tb)
                    cols_ = slice(n * T, n * T + T)
                    tt(mg[:, 0, :], gate_row[:, 0, cols_], ps[:, :], ALU.mult).then_inc(free_sem("out", n, tb), 1)
                    dve.wait_ge(*freed("out", n, tb))
                    tt(x1[:, tb, cols_], x1[:, tb, cols_], mg[:, 0, :], ALU.add).then_inc(s_x1_ready, 1)
                    dve.wait_ge(s_x1_ready, up(s_x1_ready))
            normed_blocks(1)
            for j in range(FFN // 256):
                take_panel()
                take_panel()
                for m in range(2):
                    dve.wait_ge(s_ffn_sig, 2 * j + m + 1)
                    tt(f_tmp[:, m, :], f_tmp[:, m, :], bank_of("ffn", j, 0, m)[:, :], ALU.mult)\
                        .then_inc(free_sem("ffn", j, 0, m), 1)
                    dve.wait_ge(*freed("ffn", j, 0, m))
                    dve.wait_ge(*full("ffn", j, 1, m))
                    ps = bank_of("ffn", j, 1, m)
                    tt(hid[:, 2 * j + m, :], f_tmp[:, m, :], ps[:, :], ALU.mult).then_inc(free_sem("ffn", j, 1, m), 1)
                    dve.wait_ge(*freed("ffn", j, 1, m))
            for j in range(FFN // 256):
                for k in range(2):
                    kk = 2 * j + k
                    dve.wait_ge(s_d_hi, kk + 1)
                    tt(d_lo[:, k, :], hid[:, kk, :], d_hi[:, k, :].bitcast(F32), ALU.subtract)\
                        .then_inc(s_d_lo, 1)
                    dve.wait_ge(s_d_lo, up(s_d_lo))
                take_panel()
            dve.wait_ge(s_final_weight_in, 16)
            for tb in range(TB):
                for n in range(2):
                    dve.wait_ge(*full("down", tb, n))
                    ps = bank_of("down", tb, n)
                    cols_ = slice(n * T, n * T + T)
                    tt(f_tmp[:, n, :], gate_row[:, 1, cols_], ps[:, :], ALU.mult).then_inc(free_sem("down", tb, n), 1)
                    dve.wait_ge(*freed("down", tb, n))
                    tt(x1[:, tb, cols_], x1[:, tb, cols_], f_tmp[:, n, :], ALU.add).then_inc(s_x2_ready, 1)
                    dve.wait_ge(s_x2_ready, up(s_x2_ready))
                dve.wait_ge(s_final_rstd, tb + 1)
                stt(y[:, tb, :], x1[:, tb, :], col(RSTD + tb), final_row[:, :], ALU.mult, ALU.mult)\
                    .then_inc(s_y_ready, 1)
                dve.wait_ge(s_y_ready, up(s_y_ready))

        @block.tensor
        def _(pe):
            t = nc.tensor
            started = [0] * BANKS
            m_next = [0]
            ada_next = [8]
            ada_at = [i for i, (kind, _) in enumerate(panels) if kind == "ada"]

            def begin(*use):
                bank, k = plan.of[use]
                assert k == started[bank], use
                started[bank] += 1
                if k:
                    pe.wait_ge(bank_free[bank], k)
                return psum[bank]

            def end(instruction, *use):
                instruction.then_inc(bank_full[plan.of[use][0]], 1)

            def mm(out_, lhsT, rhs, start=True, stop=True):
                return t.matmul(out_, lhsT, rhs, start=start, stop=stop, skip_group_check=True)

            def next_panel():
                m = m_next[0]
                m_next[0] += 1
                pe.wait_ge(s_panel_taken, weights[m] + 1)
                return m % RING

            def split3(ps, w, x_, first, last):
                mm(ps, w[0], x_[0], first, False)
                mm(ps, w[0], x_[1], False, False)
                return mm(ps, w[1], x_[0], False, last)

            def stationary_unit(slot, m, xs, kcs, *use):
                ps = begin(*use)
                for k in range(kcs):
                    at_ = slice(256 * k + P * m, 256 * k + P * m + P)
                    last = split3(ps[:, :], (whi[:, slot, at_], wlo[:, slot, at_]),
                                  (xs[0][:, k, :], xs[1][:, k, :]), k == 0, k == kcs - 1)
                end(last, *use)

            def moving_units(xs, uses):
                tiles = [begin(*u) for u in uses]
                for half in range(2):
                    slot = next_panel()
                    for tb, ps in enumerate(tiles):
                        for k in range(4):
                            kk, cols_ = 4 * half + k, slice(T * k, T * k + T)
                            toks = slice(tb * P, tb * P + P)
                            last = split3(ps[:, :], (xs[0][:, kk, toks], xs[1][:, kk, toks]),
                                          (whi[:, slot, cols_], wlo[:, slot, cols_]), kk == 0, kk == KC - 1)
                        if half:
                            end(last, *uses[tb])
                    if not half:
                        last.then_inc(s_panel_used, 1)

            def ada(n):
                pe.wait_ge(s_panel_taken, ada_at[n] + 1)
                ps = begin("ada", n)
                acc = ada_acc[:, n % 2, :]
                if n // 4 in (2, 5):
                    last = mm(ps[:, 0:256], ones, acc)
                else:
                    for m in range(2):
                        last = mm(ps[:, m:m + 1], acc[:, P * m:P * m + P], ones[:, 0:1])
                end(last, "ada", n)

            def late_ada():
                ada(ada_next[0])
                ada_next[0] += 1

            def transposes(k, src):
                pe.wait_ge(s_normed, TB * (k + 1))
                for kc in range(KC):
                    ps = begin("h", k, kc)
                    for tb in range(TB):
                        last = t.transpose(ps[:, tb * P:tb * P + P], src[:, tb, kc * P:kc * P + P], ident)
                    end(last, "h", k, kc)

            h_in = (hhi, hlo)
            pe.wait_ge(s_vectors_in, 16)
            pe.wait_ge(s_constants_in, 16)
            ps = begin("vectors")
            end(t.transpose(ps[:, 0:NVEC], vrow[:, :], cst[0:NVEC, C_ID:C_ID + NVEC]), "vectors")
            for n in range(8):
                ada(n)
            transposes(0, x_norm)
            pe.wait_ge(s_h_lo, KC)
            for n in range(7):
                slot = next_panel()
                for m in range(2):
                    stationary_unit(slot, m, h_in, KC, "rw", 2 * n + m)
                late_ada()
            pe.wait_ge(s_lora_in, 48)
            pe.wait_ge(s_rw_lora, 1)
            for c in range(4):
                ps = begin("rw w", c)
                end(mm(ps[:, :], lora_w[0:64, 0, c * P:c * P + P], lora_in[0:64, :]), "rw w", c)
            for c in range(4):
                ps = begin("rw a", c)
                end(mm(ps[:, :], lora_w[64:128, 0, c * P:c * P + P], lora_in[64:128, :]), "rw a", c)
            pe.wait_ge(s_rw_kk2, 1)
            for c in range(4):
                ps = begin("rw kk", c)
                end(mm(ps[:, :], pair_ones, tmp[:, c, :]), "rw kk", c)
            pe.wait_ge(s_rw_rkk, 4)
            ps = begin("rw bonus")
            for c in range(4):
                last = mm(ps[0:8, :], cst[:, C_SEL + 8 * c:C_SEL + 8 * c + 8], cum[:, c, :], c == 0, c == 3)
            end(last, "rw bonus")
            pe.wait_ge(s_rw_state, 1)
            for c in range(TB):
                toks = slice(c * P, c * P + P)
                for x_, src in enumerate((V, K, B)):
                    ps = begin("rw tok", c, x_)
                    for b in range(4):
                        last = t.transpose(ps[:, b * P:b * P + P], src[:, b, toks], ident)
                    end(last, "rw tok", c, x_)
                pe.wait_ge(s_rw_arz, 4 * (c + 1))
                for g in range(2):
                    for hl in range(4):
                        b, par = 2 * g + hl // 2, hl % 2
                        ps = begin("rw sc", c, g, hl)
                        ar = ARz[:, b, par, :, :].rearrange("p x t -> p (x t)")
                        mm(ps[:, 0:256], B[:, b, toks], ar)
                        end(mm(ps[:, 256:512], K[:, b, toks], ar), "rw sc", c, g, hl)
                    ps = begin("rw n", c, g)
                    for hl in range(4):
                        b, par = 2 * g + hl // 2, hl % 2
                        last = mm(ps[:, hl * P:hl * P + P], ARz[:, b, par, 0, :], B[:, b, toks])
                    end(last, "rw n", c, g)

                def heads(g):
                    return [(hl, slice(hl * P, hl * P + P)) for hl in range(4)]

                for i in range(1, LEVELS):
                    for g in range(2):
                        if i == 1:
                            pe.wait_ge(s_rw_x, 2 * c + g + 1)
                        else:
                            pe.wait_ge(*freed("rw pt", c, g, i - 1))
                        ps = begin("rw t", c, g, i)
                        for hl, at_ in heads(g):
                            last = mm(ps[:, at_], SC[g][:, hl, 0:P], X[:, g, at_])
                        end(last, "rw t", c, g, i)
                    for g in range(2):
                        pe.wait_ge(*freed("rw t", c, g, i))
                        if i < LEVELS - 1:
                            ps = begin("rw p", c, g, i)
                            for hl, at_ in heads(g):
                                last = mm(ps[:, at_], XT[:, g, at_], LX[:, g, at_])
                            end(last, "rw p", c, g, i)
                        ps = begin("rw pt", c, g, i)
                        for hl, at_ in heads(g):
                            last = mm(ps[:, at_], LX[:, g, at_], XT[:, g, at_])
                        end(last, "rw pt", c, g, i)
                for g in range(2):
                    pe.wait_ge(s_rw_state, 2 * c + g if c else 1)
                    for x_ in range(3) if g == 0 else ():
                        pe.wait_ge(*freed("rw tok", c, x_))
                    ps = begin("rw r", c, g)
                    for hl in range(4):
                        b, par = 2 * g + hl // 2, hl % 2
                        cols_ = slice(64 * hl, 64 * hl + 64)
                        mm(ps[:, cols_], ARz[:, b, par, 0, :], M[:, b, :], True, False)
                        last = mm(ps[:, cols_], SC[g][:, hl, 256:384],
                                  tok[:, 0, 64 * (4 * g + hl):64 * (4 * g + hl) + 64], False, True)
                    end(last, "rw r", c, g)
                for g in range(2):
                    pe.wait_ge(*freed("rw pt", c, g, LEVELS - 1))
                    pe.wait_ge(*freed("rw r", c, g))
                    ps = begin("rw u", c, g)
                    for hl, at_ in heads(g):
                        last = mm(ps[:, 64 * hl:64 * hl + 64], XT[:, g, at_], rhs_u[:, g, 64 * hl:64 * hl + 64])
                    end(last, "rw u", c, g)
                for g in range(2):
                    pe.wait_ge(*freed("rw u", c, g))
                    ps = begin("rw o", c, g)
                    for hl in range(4):
                        b, par, head = 2 * g + hl // 2, hl % 2, 4 * g + hl
                        rows = slice(64 * par, 64 * par + 64)
                        o = ps[rows, P * (hl // 2):P * (hl // 2) + P]
                        mm(o, tok[:, 0, 64 * head:64 * head + 64], SC[g][:, hl, 384:512], True, False)
                        mm(o, U[:, g, 64 * hl:64 * hl + 64], SC[g][:, hl, 128:256], False, False)
                        last = mm(o, M[:, b, :], ARz[:, b, par, 1, :], False, True)
                    end(last, "rw o", c, g)
                for g in range(2) if c < TB - 1 else ():
                    ps = begin("rw m", c, g)
                    for hl in range(4):
                        par, head = hl % 2, 4 * g + hl
                        o = ps[64 * par:64 * par + 64, 64 * (hl // 2):64 * (hl // 2) + 64]
                        at_ = slice(64 * head, 64 * head + 64)
                        mm(o, tok[:, 1, at_], tok[:, 0, at_], True, False)
                        last = mm(o, tok[:, 2, at_], U[:, g, 64 * hl:64 * hl + 64], False, True)
                    end(last, "rw m", c, g)
            pe.wait_ge(*freed("rw o", TB - 1, 1))
            for c in range(4):
                ps = begin("rw mean", c)
                end(mm(ps[:, :], pair_ones, R[:, c, :]), "rw mean", c)
            pe.wait_ge(s_rw_sq, 1)
            for c in range(4):
                ps = begin("rw var", c)
                end(mm(ps[:, :], pair_ones, epi[:, c, :]), "rw var", c)
            for c in range(4):
                ps = begin("rw bv", c)
                end(mm(ps[:, :], cst[0:8, C_SELT + P * c:C_SELT + P * c + P], bonus[:, :]), "rw bv", c)
            pe.wait_ge(s_rw_lora, 2)
            for c in range(4):
                ps = begin("rw g", c)
                end(mm(ps[:, :], lora_w[:, 1, c * P:c * P + P], gate_lo[:, :]), "rw g", c)
            for n in range(6):
                slot = next_panel()
                for m in range(2):
                    stationary_unit(slot, m, h_in, KC, "hg", 2 * n + m)
                late_ada()
            moving_units(h_in, [("hg v", tb) for tb in range(TB)])
            late_ada()
            late_ada()
            pe.wait_ge(s_hg_key, 1)
            for lev in range(LEVELS + 1):
                if lev:
                    pe.wait_ge(s_hg_lev, lev)
                q, k_ = (q_lev, k_lev) if lev else (Hq, Hk)
                for c in range(TB):
                    ps = begin("hg sc", lev, c)
                    for h in range(4):
                        last = mm(ps[:, h * P:h * P + P], k_[:, h, c * P:c * P + P], q[:, h, c * P:c * P + P])
                    end(last, "hg sc", lev, c)
            pe.wait_ge(s_hg_k_left, 1)
            for c in range(TB):
                ps = begin("hg tok", c)
                for h in range(4):
                    last = t.transpose(ps[:, h * P:h * P + P], Hk[:, h, c * P:c * P + P], ident)
                end(last, "hg tok", c)
                if c:
                    pe.wait_ge(*freed("hg s", c - 1))
                ps = begin("hg o", c)
                for h in range(4):
                    o, v_ = ps[:, h * P:h * P + P], Hv[:, c, h * P:h * P + P]
                    last = mm(o, v_, ST[:, c, h, :], True, c == 0)
                    if c:
                        last = mm(o, Hs[:, h, :], Hq[:, h, c * P:c * P + P], False, True)
                end(last, "hg o", c)
                if c < TB - 1:
                    pe.wait_ge(*freed("hg tok", c))
                    ps = begin("hg s", c)
                    for h in range(4):
                        last = mm(ps[:, h * P:h * P + P], k_tok[:, h * P:h * P + P], Hv[:, c, h * P:h * P + P])
                    end(last, "hg s", c)
            pe.wait_ge(s_hg_sq, 1)
            for h in range(4):
                ps = begin("hg ss", h)
                end(mm(ps[:, :], ones, k_lev[:, h, :]), "hg ss", h)
            for n in range(4):
                slot = next_panel()
                for m in range(2):
                    stationary_unit(slot, m, h_in, KC, "da", 2 * n + m)
                if n == 0:
                    late_ada()
            moving_units(h_in, [("da v", tb) for tb in range(TB)])
            for n in range(8):
                pe.wait_ge(*freed("da", n))
                ps = begin("da rot", n)
                end(mm(ps[:, :], cst[:, C_PERM:C_PERM + P], qk[:, n // 4, n % 4, :]), "da rot", n)
            pe.wait_ge(s_roped, 8)
            for tb in range(TB):
                pe.wait_ge(*freed("da v", tb))
            for h in range(4):
                po = begin("da o", h)
                for i in range(TB):
                    n = (i + 1) * P
                    for m in range(2):
                        rows = slice(64 * m, 64 * m + 64)
                        ps = begin("da s", h, i, m)
                        mm(ps[:, 0:n], qk[rows, 0, h, i * P:i * P + P], qk[rows, 1, h, 0:n], True, False)
                        end(mm(ps[:, n - P:n], cst[rows, C_MA:C_MA + P], cst[rows, C_MB:C_MB + P], False, True),
                            "da s", h, i, m)
                    pe.wait_ge(s_da_p, 4 * h + i + 1)
                    ps = begin("da pt", h, i)
                    for j in range(i + 1):
                        last = t.transpose(ps[:, j * P:j * P + P], prob[:, i % 2, 0, j * P:j * P + P], ident)
                    end(last, "da pt", h, i)
                    pe.wait_ge(*freed("da pt", h, i))
                    for j in range(i + 1):
                        last = mm(po[:, i * P:i * P + P], v_tok[:, j, h * P:h * P + P], probT[:, j * P:j * P + P],
                                  j == 0, j == i)
                end(last, "da o", h)
                pe.wait_ge(s_da_sq, h + 1)
                ps = begin("da ss", h)
                end(mm(ps[:, :], ones, att2[:, :]), "da ss", h)
            branches = ((oa_hi, oa_lo), (ob_hi, ob_lo), (oc_hi, oc_lo))
            pe.wait_ge(s_da_lo, 4)
            for j in range(4):
                for g in range(3):
                    slot = next_panel()
                    for m in range(2):
                        stationary_unit(slot, m, h_in, KC, "gate", j, g, m)
                for g in range(3):
                    slot = next_panel()
                    for m in range(2):
                        stationary_unit(slot, m, branches[g], 4, "branch", j, g, m)
            pe.wait_ge(s_merged, KC)
            for n in range(2):
                moving_units((mg_hi, mg_lo), [("out", n, tb) for tb in range(TB)])
            transposes(1, x1_norm)
            pe.wait_ge(s_h_lo, 2 * KC)
            for j in range(FFN // 256):
                for which in range(2):
                    slot = next_panel()
                    for m in range(2):
                        stationary_unit(slot, m, h_in, KC, "ffn", j, which, m)
            tiles = [[begin("down", tb, n) for n in range(2)] for tb in range(TB)]
            for j in range(FFN // 256):
                slot = next_panel()
                for k in range(2):
                    kk = 2 * j + k
                    pe.wait_ge(s_d_lo, kk + 1)
                    for tb in range(TB):
                        toks = slice(tb * P, tb * P + P)
                        for n in range(2):
                            at_ = slice(D * k + T * n, D * k + T * n + T)
                            last = split3(tiles[tb][n][:, :], (d_hi[:, k, toks], d_lo[:, k, toks]),
                                          (whi[:, slot, at_], wlo[:, slot, at_]), kk == 0, kk == FFN // P - 1)
                            if kk == FFN // P - 1:
                                end(last, "down", tb, n)
                    if kk < FFN // P - 1:
                        last.then_inc(s_down_k, 1)


def constants():
    import numpy as np
    c = np.zeros((P, NCONST), np.float32)
    i = np.arange(P)
    c[:, C_ID:C_ID + P] = np.eye(P)
    for p in range(P):
        if p % 64 < 32:
            c[p + 32, C_PERM + p] = -1.0
        else:
            c[p - 32, C_PERM + p] = 1.0
    c[:, C_ONES:C_ONES + P] = 1.0
    c[:, C_BLK:C_BLK + P] = i[:, None] // 64 == i[None, :] // 64
    strict, incl = i[:, None] < i[None, :], i[:, None] <= i[None, :]
    for n, part in enumerate((-1.0 * strict, incl, strict, incl)):
        c[:, C_MASK + n * P:C_MASK + n * P + P] = part
    for row in (0, 64):
        c[row, C_MA:C_MA + 64] = 1.0
        c[row, C_MB + 64:C_MB + P] = -2.0 ** 100
    c[:, C_FREQ] = np.float32(10000.0) ** (-(2 * (i % 32)).astype(np.float32) / np.float32(64))
    c[:, C_EPS], c[:, C_GEPS], c[:, C_HPI] = EPS, GN_EPS, TWO_PI / 4
    for b in range(4):
        c[:, C_SEL + 8 * b + 2 * b] = i < 64
        c[:, C_SEL + 8 * b + 2 * b + 1] = i >= 64
        c[2 * b, C_SELT + P * b:C_SELT + P * b + 64] = 1.0
        c[2 * b + 1, C_SELT + P * b + 64:C_SELT + P * b + P] = 1.0
    lev = np.zeros((P, 2 * LEVELS + 1, P), np.float32)
    for n in range(LEVELS):
        s = 1 << n
        same = i[:, None] // (2 * s) == i[None, :] // (2 * s)
        upper = same & (i[:, None] % (2 * s) < s) & (i[None, :] % (2 * s) >= s)
        lev[:, 2 * n, :], lev[:, 2 * n + 1, :] = upper.T, upper
    lev[:, 2 * LEVELS, :] = np.eye(P)
    return c, lev.reshape(P, -1)


def kernel(**inputs):
    import numpy as np
    import concourse.bacc as bacc
    from concourse.bass_utils import run_bass_kernel_spmd

    a = {k: np.ascontiguousarray(v) for k, v in inputs.items()}
    names = ("rw_mu", "rw_w0", "rw_a0", "rw_k_k", "rw_k_a", "rw_r_k", "rw_gn_w", "rw_gn_b",
             "hg_norm_w", "da_subln_w", "norm_mix_w", "norm_ffn_w", "c", "ada_b")
    vecs = np.concatenate([a[n].reshape(-1, P) for n in names])
    consts, levels = constants()
    arrays = {
        "x": a["x"][0], "ada_w": a["ada_w"][0], "w_in": a["w_in"][0],
        "w_a": a["w_branch_a"][0], "w_b": a["w_branch_b"][0], "w_c": a["w_branch_c"][0],
        "w_out": a["w_out"][0], "f_in": a["ffn_w_in"][0], "f_out": a["ffn_w_out"][0],
        "w2": a["rw_w2"][0], "a2": a["rw_a2"][0], "g2": a["rw_g2"][0],
        "vecs": vecs, "consts": consts, "levels": levels,
        "gate_b": a["ada_b"][0], "final_w": a["final_norm_w"], "lam": a["da_lambda"].reshape(-1),
        "positions": a["positions"][0],
    }
    nc = bacc.Bacc("TRN2", target_bir_lowering=False, num_devices=1)
    aps = [nc.dram_tensor(f"in_{k}", v.shape, mybir.dt.from_np(v.dtype), kind="ExternalInput").ap()
           for k, v in arrays.items()]
    aps.append(nc.dram_tensor("out_x", (T, D), F32, kind="ExternalOutput").ap())
    build(nc, *aps)
    r = run_bass_kernel_spmd(nc, [{f"in_{k}": v for k, v in arrays.items()}], core_ids=[0])
    return r.results[0]["out_x"].reshape(1, T, D)
```

```python
from contextlib import ExitStack

import concourse.bass as bass
from concourse import mybir

F32 = mybir.dt.float32
F32R = mybir.dt.float32r
U8 = mybir.dt.uint8
I32 = mybir.dt.int32
ALU = mybir.AluOpType
ACT = mybir.ActivationFunctionType
AX_X = mybir.AxisListType.X

P = 128
D = 1024
T = 512
KC = D // P
TB = T // P
FFN = 2816
EPS = 1e-6
GN_EPS = 64e-5
DECAY = 0.6065306597126334
LAM_INIT = 0.2
TWO_PI = 6.283185307179586
TURN = (6.28125, 0.0019350051879882812, 3.0198680e-07)
ROUND = 12582912.0
LEVELS = 7

DA_Q, DA_K, DA_V, HG_F, HG_I, HG_Q, HG_G, RW_U, GATES = 0, 512, 1024, 1536, 2048, 2560, 3072, 3584, 5376

V_MU, V_W0, V_A0, V_KK, V_KA, V_RK, V_GNW, V_GNB, V_HGN, V_SUB, V_NM, V_NF, V_C, V_ADAB = (
    0, 14, 18, 22, 26, 30, 34, 38, 42, 43, 44, 52, 60, 68)
NVEC = 116

C_ID, C_PERM, C_ONES, C_BLK, C_MASK, C_MA, C_MB, C_LOW = 0, 128, 256, 384, 512, 1024, 1152, 1280
C_FREQ, C_EPS, C_GEPS, C_HPI, C_SEL, C_SELT = 1408, 1409, 1410, 1411, 1412, 1444
NCONST = C_SELT + 512

EARLY = [("rw lora", 4), ("rw kk", 4), ("rw bonus", 4)] + [(("rw sums", n), 4) for n in range(4)]
EARLY += [((what, c), n) for c in range(TB) for what, n in (("rw tok", 1), ("rw x", 2), ("rw r", 1), ("rw u", 2))]
EARLY += [("rw mean", 4), ("rw var", 4), ("rw g", 4), ("hg", 0)]
EARLY += [("hg z", 4)] + [(("hg sc", lev), 2) for lev in range(1, LEVELS + 1)] + [("hg left", 4), ("hg ss", 2), ("end", 0)]
ADA_AT_BRANCH = ((0, 0), (0, 2), (1, 2), (2, 2), (3, 2))
U_Z, U_HQ, U_HG, U_QK, U_GATES, N_EARLY = 0, 4, 8, 12, 20, 44


def filled(place):
    total = 0
    for name, n in EARLY:
        if name == place:
            return total
        total += n
    raise KeyError(place)


RAW = 3
RING = 2
BANKS = 8


def panel_stream(w_in, ada_w, wbr, w_out, f_in, f_out):
    def stationary(w, col, kc=KC):
        return w.rearrange("(k p) n -> p k n", p=P)[:, 0:kc, col:col + 256]

    def moving(w, half, col):
        return w.rearrange("(k p) n -> p k n", p=P)[:, 4 * half:4 * half + 4, col:col + 512]

    out = [("ada", stationary(ada_w, 256 * n)) for n in range(8)]
    late = [("ada", stationary(ada_w, 256 * n)) for n in range(8, 24)]
    for n in range(7):
        out += [("w", stationary(w_in, RW_U + 256 * n)), late.pop(0)]
    early = [("w", stationary(w_in, base + 256 * n)) for base in (HG_F, HG_Q, HG_G) for n in range(2)]
    early += [("w", stationary(w_in, DA_Q + 256 * n)) for n in range(4)]
    early += [("w", stationary(w_in, GATES + D * g + 256 * j)) for j in range(4) for g in range(3)]
    split = filled("hg") // 4
    out += early[:split]
    out += [("w", moving(w_in, half, HG_I)) for half in range(2)]
    out += early[split:]
    out += [("w", moving(w_in, half, DA_V)) for half in range(2)]
    for j in range(4):
        for g, w in enumerate(wbr):
            out.append(("w", stationary(w, 256 * j, 4)))
            if (j, g) in ADA_AT_BRANCH:
                out.append(late.pop(0))
    out += [("w", moving(w_out, half, 512 * n)) for n in range(2) for half in range(2)]
    for j in range(FFN // 256):
        out.append(("w", stationary(f_in, 256 * j)))
        if late:
            out.append(late.pop(0))
        out.append(("w", stationary(f_in, FFN + 256 * j)))
    fo = f_out.rearrange("(k p) n -> p k n", p=P)
    out += [("w", fo[:, 2 * j:2 * j + 2, :]) for j in range(FFN // 256)]
    assert not late
    return out


class Banks:

    def __init__(self):
        self.of, self.count, self.next, self.used = {}, [0] * BANKS, 0, BANKS

    def rotate(self, n):
        self.used, self.next = n, 0

    def add(self, *name, bank=None):
        if bank is None:
            bank = self.next
            self.next = (bank + 1) % self.used
        self.of[name] = (bank, self.count[bank])
        self.count[bank] += 1


def bank_plan():
    b = Banks()
    b.add("vectors")
    for n in range(8):
        b.add("ada", n)
    for kc in range(KC):
        b.add("h", 0, kc)
    late = list(range(8, 24))

    def late_ada():
        if late:
            b.add("ada", late.pop(0))

    for n in range(7):
        b.add("rw", 2 * n)
        b.add("rw", 2 * n + 1)
        late_ada()
    for u in range(filled("hg") // 2):
        b.add("early", u, bank=6 + u % 2)
    b.rotate(6)
    for what in ("rw w", "rw a", "rw kk"):
        for c in range(4):
            b.add(what, c)
    b.add("rw bonus")
    for c in range(TB):
        for x in range(3):
            b.add("rw tok", c, x)
        for g in range(2):
            for hl in range(4):
                b.add("rw sc", c, g, hl)
            b.add("rw n", c, g)
        for i in range(1, LEVELS):
            for g in range(2):
                b.add("rw t", c, g, i)
            for g in range(2):
                if i < LEVELS - 1:
                    b.add("rw p", c, g, i)
                b.add("rw pt", c, g, i)
        for what in ("rw r", "rw u", "rw o") + (("rw m",) if c < TB - 1 else ()):
            for g in range(2):
                b.add(what, c, g)
    b.rotate(6)
    for what in ("rw mean", "rw bv", "rw var", "rw g"):
        for c in range(4):
            b.add(what, c)
    for tb in range(TB):
        b.add("hg v", tb, bank=4 + tb)
    for u in range(filled("hg") // 2, N_EARLY):
        b.add("early", u, bank=6 + u % 2)
    b.rotate(6)
    for lev in range(LEVELS + 1):
        for c in range(TB):
            b.add("hg sc", lev, c)
    for c in range(TB):
        b.add("hg tok", c)
        b.add("hg o", c)
        if c < TB - 1:
            b.add("hg s", c)
    for h in range(4):
        b.add("hg ss", h)
    b.rotate(8)
    for tb in range(TB):
        b.add("da v", tb)
    for n in range(8):
        b.add("da rot", n)
    b.rotate(6)
    for t in range(-2, 4 * TB + 3):
        if t >= 6 and t % 4 == 2:
            b.add("da ss", (t - 6) // 4)
        if t + 2 < 4 * TB:
            for m in range(2):
                b.add("da s", t + 2, m)
        if 0 <= t < 4 * TB:
            b.add("da pt", t)
    for h in range(4):
        b.add("da o", h, bank=6 + h % 2)
    b.rotate(8)
    for j in range(4):
        for g in range(3):
            for m in range(2):
                b.add("branch", j, g, m)
            if (j, g) in ADA_AT_BRANCH:
                late_ada()
    for n in range(2):
        for tb in range(TB):
            b.add("out", n, tb)
    for kc in range(KC):
        b.add("h", 1, kc)
    for j in range(FFN // 256):
        for which in range(2):
            for m in range(2):
                b.add("ffn", j, which, m)
            if which == 0:
                late_ada()
    for tb in range(TB):
        for n in range(2):
            b.add("down", tb, n)
    assert not late
    return b


def panel_ends():
    ends = [("bank", ("rw", 2 * n + 1)) for n in range(7)]
    early = [("bank", ("early", 2 * q + 1)) for q in range(N_EARLY // 2)]
    split = filled("hg") // 4
    ends += early[:split] + [("panel used", 1), ("bank", ("hg v", TB - 1))]
    ends += early[split:] + [("panel used", 2), ("bank", ("da v", TB - 1))]
    for j in range(4):
        ends += [("bank", ("branch", j, g, 1)) for g in range(3)]
    for n in range(2):
        ends += [("panel used", 3 + n), ("bank", ("out", n, TB - 1))]
    for j in range(FFN // 256):
        ends += [("bank", ("ffn", j, which, 1)) for which in range(2)]
    ends += [("down k", 2 * j + 2) for j in range(FFN // 256)]
    return ends


def build(nc, x, ada_w, w_in, wba, wbb, wbc, w_out, f_in, f_out, w2, a2, g2,
          vecs, consts, levels, gate_b, final_w, lam, positions, out):
    panels = panel_stream(w_in, ada_w, (wba, wbb, wbc), w_out, f_in, f_out)
    plan = bank_plan()
    with ExitStack() as ctx:
        def sb(name, shape, dt=F32):
            return ctx.enter_context(nc.sbuf_tensor(name, shape, dt))

        raw = sb("raw", [P, RAW, 2048])
        whi = sb("whi", [P, RING, 2048], F32R)
        wlo = sb("wlo", [P, RING, 2048], F32R)
        hhi = sb("hhi", [P, KC, T], F32R)
        hlo = sb("hlo", [P, KC, T], F32R)
        cst = sb("cst", [P, NCONST])
        lev_mask = sb("lev_mask", [P, 2 * LEVELS + 1, P], U8)
        vrow = sb("vrow", [NVEC, P])
        vc = sb("vc", [P, NVEC])
        ca = sb("ca", [P, KC])
        small = sb("small", [P, 160])
        ada_cols = sb("ada_cols", [P, 48])
        gmul = sb("gmul", [P, 2, KC])
        gate_row = sb("gate_row", [P, 2, D])
        ada_acc = sb("ada_acc", [P, 2, 256])
        stage = gate_row[:, 1, :].rearrange("p (s t) -> p s t", s=2)
        early_out = nc.dram_tensor("early_out", (N_EARLY, P, T), F32, kind="Internal").ap()

        base = -(-nc.sbuf_base // 64) * 64
        size = (nc.sbuf_usable_end - base) // 64 * 64 - 64
        sb("arena_fence", [P, size // 4 - 16])

        def at(name, kb, shape, dt=F32):
            n = 2 if dt == U8 else 4
            for extent in shape[1:]:
                n *= extent
            assert kb * 1024 + n <= size, (name, kb + n / 1024, size / 1024)
            return nc.alloc_sbuf_tensor_at(name, shape, dt, offset=base + kb * 1024)

        x_in = at("x_in", 0, [P, TB, D])
        x_norm = at("x_norm", 16, [P, TB, D])
        h_tmp = at("h_tmp", 32, [P, 2, T])
        lev_f32 = at("lev_f32", 40, [P, 2 * LEVELS + 1, P])
        oc_hi = at("oc_hi", 0, [P, 4, T], F32R)
        oc_lo = at("oc_lo", 8, [P, 4, T], F32R)
        R = at("R", 16, [P, 4, T])
        K = at("K", 24, [P, 4, T])
        V = at("V", 32, [P, 4, T])
        A = at("A", 40, [P, 4, T])
        B = at("B", 48, [P, 4, T])
        gate_lo = at("gate_lo", 56, [P, T])
        bonus = at("bonus", 58, [8, T])
        lora_w = at("lora_w", 60, [P, 2, T])
        lora_in = at("lora_in", 64, [P, T])
        u_prev = at("u_prev", 66, [P, 2, T + 1])
        decay = at("decay", 71, [P, 4, T])
        cum = at("cum", 79, [P, 4, T])
        tmp = at("tmp", 87, [P, 4, T])
        tok = at("tok", 72, [P, 3, T])
        SC = [at("sc0", 78, [P, 4, T]), at("sc1", 0, [P, 4, T])]
        X = at("X", 8, [P, 2, T])
        XT = at("XT", 12, [P, 2, T])
        LX = at("LX", 86, [P, 2, T])
        rhs_u = at("rhs_u", 90, [P, 2, 256])
        U = at("U", 92, [P, 2, 256])
        M = at("M", 94, [P, 4, 64])
        epi = at("epi", 64, [P, 4, T])
        epi2 = at("epi2", 72, [P, 4, T])
        ob_hi = at("ob_hi", 16, [P, 4, T], F32R)
        ob_lo = at("ob_lo", 24, [P, 4, T], F32R)
        Z = at("Z", 40, [P, 4, T])
        Hb = at("Hb", 24, [P, 4, T])
        Hq = at("Hq", 32, [P, 4, T])
        Hg = at("Hg", 16, [P, 4, T])
        Hk = at("Hk", 48, [P, 4, T])
        Hv = at("Hv", 56, [P, TB, T])
        q_lev = at("q_lev", 64, [P, 4, T])
        k_lev = at("k_lev", 72, [P, 4, T])
        ST = at("ST", 80, [P, TB, 4, P])
        Hs = at("Hs", 88, [P, 4, P])
        k_tok = at("k_tok", 90, [P, T])
        oa_hi = at("oa_hi", 32, [P, 4, T], F32R)
        oa_lo = at("oa_lo", 40, [P, 4, T], F32R)
        qk = at("qk", 48, [P, 2, 4, T])
        v_tok = at("v_tok", 64, [P, TB, T])
        cos_sin = at("cos_sin", 72, [P, 2, T])
        rot = at("rot", 76, [P, 4, T])
        prob = at("prob", 72, [P, 3, 2, T])
        probT = [at("probT0", 84, [P, T]), at("probT1", 90, [P, T])]
        turns = at("turns", 84, [P, T])
        pos_i = at("pos_i", 84, [P, T], I32)
        ang = at("ang", 86, [P, 3, T])
        att = at("att", 86, [P, T])
        att2 = at("att2", 88, [P, T])
        lam_in = at("lam_in", 92, [P, 256])
        sg = at("sg", 48, [P, 3, 2, T])
        mg_hi = at("mg_hi", 60, [P, KC, T], F32R)
        mg_lo = at("mg_lo", 76, [P, KC, T], F32R)
        mg = at("mg", 92, [P, 2, T])
        mg_tmp = at("mg_tmp", 96, [P, T])
        x1 = at("x1", 0, [P, TB, D])
        x1_norm = at("x1_norm", 16, [P, TB, D])
        h_tmp2 = at("h_tmp2", 32, [P, 2, T])
        hid = at("hid", 16, [P, FFN // P, T])
        d_hi = at("d_hi", 60, [P, 2, T], F32R)
        d_lo = at("d_lo", 64, [P, 2, T], F32R)
        f_tmp = at("f_tmp", 68, [P, 2, T])
        final_row = at("final_row", 92, [P, D])
        y = at("y", 76, [P, TB, D])

        psum = [ctx.enter_context(nc.psum_tensor(f"bank{b}", [P, T], F32)) for b in range(BANKS)]

        bank_full = [ctx.enter_context(nc.semaphore(f"bank{b}_full")) for b in range(BANKS)]
        bank_free = [ctx.enter_context(nc.semaphore(f"bank{b}_free")) for b in range(BANKS)]
        raw_loaded = [ctx.enter_context(nc.semaphore(f"raw{s}_loaded")) for s in range(RAW)]
        def sem(name):
            return ctx.enter_context(nc.semaphore(name))

        s_act_step = sem("act_step")
        s_angles = sem("angles")
        s_c_act = sem("c_act")
        s_constants_in = sem("constants_in")
        s_cos_sin = sem("cos_sin")
        s_d_hi = sem("d_hi")
        s_d_lo = sem("d_lo")
        s_da_hi = sem("da_hi")
        s_da_lo = sem("da_lo")
        s_da_out = sem("da_out")
        s_da_p = sem("da_p")
        s_da_rstd = sem("da_rstd")
        s_da_sq = sem("da_sq")
        s_down_k = sem("down_k")
        s_dve_step = sem("dve_step")
        s_ffn_sig = sem("ffn_sig")
        s_final_rstd = sem("final_rstd")
        s_final_weight_in = sem("final_weight_in")
        s_gate_bias_in = sem("gate_bias_in")
        s_h_hi = sem("h_hi")
        s_h_lo = sem("h_lo")
        s_hg_neg_abs = sem("hg_neg_abs")
        s_hg_e_b = sem("hg_e_b")
        s_hg_e_last = sem("hg_e_last")
        s_hg_e_left = sem("hg_e_left")
        s_hg_e_rel = sem("hg_e_rel")
        s_hg_hi = sem("hg_hi")
        s_hg_k_left = sem("hg_k_left")
        s_hg_key = sem("hg_key")
        s_hg_last = sem("hg_last")
        s_hg_left = sem("hg_left")
        s_hg_lev = sem("hg_lev")
        s_hg_ln = sem("hg_ln")
        s_hg_ls_less_z = sem("hg_ls_less_z")
        s_hg_out = sem("hg_out")
        s_hg_rel = sem("hg_rel")
        s_hg_rstd = sem("hg_rstd")
        s_hg_split = sem("hg_split")
        s_hg_sq = sem("hg_sq")
        s_lam_dot = sem("lam_dot")
        s_lam_exp = sem("lam_exp")
        s_lambda_in = sem("lambda_in")
        s_lora_in = sem("lora_in")
        s_masks = sem("masks")
        s_masks_in = sem("masks_in")
        s_max = sem("max")
        s_merged = sem("merged")
        s_mg_hi = sem("mg_hi")
        s_mg_sum = sem("mg_sum")
        s_normed = sem("normed")
        s_panel_hi = sem("panel_hi")
        s_panel_taken = sem("panel_taken")
        s_panel_used = sem("panel_used")
        s_pool_step = sem("pool_step")
        s_positions_in = sem("positions_in")
        s_roped = sem("roped")
        s_rw_e_a = sem("rw_e_a")
        s_rw_e_bk = sem("rw_e_bk")
        s_rw_e_r = sem("rw_e_r")
        s_rw_factor = sem("rw_factor")
        s_rw_hi = sem("rw_hi")
        s_rw_k_k = sem("rw_k_k")
        s_rw_kk2 = sem("rw_kk2")
        s_rw_lora = sem("rw_lora")
        s_rw_norm = sem("rw_norm")
        s_rw_prev = sem("rw_prev")
        s_rw_rkk = sem("rw_rkk")
        s_rw_rstd = sem("rw_rstd")
        s_rw_split = sem("rw_split")
        s_rw_sq = sem("rw_sq")
        s_rw_state = sem("rw_state")
        s_rw_sums = sem("rw_sums")
        s_rw_x = sem("rw_x")
        s_stored = sem("stored")
        s_spilled = [sem("spilled0"), sem("spilled1")]
        s_z_in, s_hq_in, s_hg_in, s_qk_in = sem("z_in"), sem("hq_in"), sem("hg_in"), sem("qk_in")
        s_hg_silu = sem("hg_silu")
        s_gate_in = [sem("gate0_in"), sem("gate1_in"), sem("gate2_in")]
        s_gated = sem("gated")
        s_u_prev_zero = sem("u_prev_zero")
        s_vectors_in = sem("vectors_in")
        s_x_again = sem("x_again")
        s_x_in = sem("x_in")
        s_x1_ready = sem("x1_ready")
        s_x2_ready = sem("x2_ready")
        s_y_ready = sem("y_ready")

        counts = {}

        def up(semaphore):
            counts[semaphore.name] = counts.get(semaphore.name, 0) + 1
            return counts[semaphore.name]

        def bank_of(*use):
            return psum[plan.of[use][0]]

        def full(*use):
            bank, k = plan.of[use]
            return bank_full[bank], k + 1

        def free_sem(*use):
            return bank_free[plan.of[use][0]]

        def freed(*use):
            bank, k = plan.of[use]
            return bank_free[bank], k + 1

        weights = [n for n, (kind, _) in enumerate(panels) if kind == "w"]
        ends = panel_ends()
        assert len(ends) == len(weights)

        def slot_released(eng, m):
            kind, what = ends[m]
            if kind == "bank":
                eng.wait_ge(*full(*what))
            else:
                eng.wait_ge({"panel used": s_panel_used, "down k": s_down_k}[kind], what)

        def loaded(eng, n):
            eng.wait_ge(raw_loaded[n % RAW], 16 * (n // RAW + 1))
            a, cols = panels[n][1].shape[1:]
            return raw[:, n % RAW, 0:a * cols]

        def spilled(u):
            return s_spilled[u % 2], 16 * (u // 2 + 1)

        def region(place):
            at_hg = filled("hg")
            return (0, at_hg) if filled(place) < at_hg or place == "hg" else (at_hg, 2 * N_EARLY)

        def bcast(ap, *shape):
            return ap.to_broadcast(list(shape))

        def blocks(tile):
            return tile[:, :, :].rearrange("p a (b t) -> p (a b) t", t=P)

        ident = cst[:, C_ID:C_ID + P]
        ones = cst[:, C_ONES:C_ONES + P]
        pair_ones = cst[:, C_BLK:C_BLK + P]
        SS, RSTD, OM_MU, OM_KA, BREF, BLAST, FAC, HLAST, MX, RS, LR, NLAM, SUBW, NB, SUM = (
            0, 4, 8, 22, 26, 42, 58, 74, 90, 96, 98, 100, 101, 104, 110)

        def col(k, n=1):
            return small[:, k:k + n]

        def blk16(k):
            return small[:, k:k + 16]

        block = ctx.enter_context(nc.Block())

        @block.sync
        def _(sp):
            sp.dma_start(vrow[:, :], vecs).then_inc(s_vectors_in, 16)
            sp.dma_start(cst[:, :], consts).then_inc(s_constants_in, 16)
            for n, (kind, src) in enumerate(panels):
                if n >= RAW:
                    sp.wait_ge(s_panel_taken, n - RAW + 1)
                a, cols = src.shape[1:]
                dst = raw[:, n % RAW, 0:a * cols].rearrange("p (a n) -> p a n", a=a)
                sp.dma_start(dst, src).then_inc(raw_loaded[n % RAW], 16)

        @block.gpsimd
        def _(pool):
            pool.dma_start(x_in[:, :, :], x.rearrange("(b p) d -> p b d", p=P)).then_inc(s_x_in, 16)
            pool.dma_start(lev_f32[:, :, :], levels.rearrange("p (l c) -> p l c", c=P)).then_inc(s_masks_in, 16)

            def gate_bias(g):
                pool.dma_start(gate_row[:, g, :], gate_b[3 * D * g + 2 * D:3 * D * g + 3 * D].rearrange(
                    "(a n) -> a n", a=1).to_broadcast([P, D])).then_inc(s_gate_bias_in, 16)

            gate_bias(0)
            pool.dma_start(lora_w[0:64, 0, :], w2).then_inc(s_lora_in, 16)
            pool.dma_start(lora_w[64:128, 0, :], a2).then_inc(s_lora_in, 16)
            pool.dma_start(lora_w[:, 1, :], g2).then_inc(s_lora_in, 16)
            pool.wait_ge(s_masks_in, 16)
            nc.gpsimd.tensor_copy(lev_mask[:, :, :], lev_f32[:, :, :]).then_inc(s_masks, 1)
            pool.wait_ge(s_masks, up(s_masks))
            def reload(dst, u, n, arrived):
                pool.wait_ge(*spilled(u + n - 2))
                pool.wait_ge(*spilled(u + n - 1))
                pool.dma_start(dst, early_out[u:u + n].rearrange("u p t -> p u t")).then_inc(arrived, 16)

            pool.wait_ge(*full("rw o", TB - 1, 1))
            reload(Z[:, :, :], U_Z, 4, s_z_in)
            pool.wait_ge(*freed("rw bv", 3))
            reload(Hq[:, :, :], U_HQ, 4, s_hq_in)
            pool.wait_ge(*freed("rw g", 3))
            reload(Hg[:, :, :], U_HG, 4, s_hg_in)
            pool.wait_ge(s_hg_k_left, 1)
            pool.wait_ge(*full("hg o", TB - 1))
            reload(qk[:, :, :, :].rearrange("p a h t -> p (a h) t"), U_QK, 8, s_qk_in)
            pool.wait_ge(*full("hg ss", 3))
            pool.wait_ge(s_hg_split, 4)
            pool.dma_start(pos_i[:, :], positions.rearrange("(a n) -> a n", a=1).to_broadcast([P, T])
                           ).then_inc(s_positions_in, 16)
            pool.dma_start(lam_in[:, :], lam.rearrange("(a n) -> a n", a=1).to_broadcast([P, 256])
                           ).then_inc(s_lambda_in, 16)
            pool.wait_ge(*full("da pt", 4 * TB - 1))
            for j in range(4):
                for g in range(3):
                    if j:
                        pool.wait_ge(*freed("branch", j - 1, g, 1))
                    reload(sg[:, g, :, :], U_GATES + 6 * j + 2 * g, 2, s_gate_in[g])
            gate_bias(1)
            pool.wait_ge(*full("branch", 3, 2, 1))
            pool.dma_start(x1[:, :, :], x.rearrange("(b p) d -> p b d", p=P)).then_inc(s_x_again, 16)
            pool.wait_ge(s_x1_ready, 2 * TB)
            pool.dma_start(final_row[:, :], final_w.rearrange("(a n) -> a n", a=1).to_broadcast([P, D])
                           ).then_inc(s_final_weight_in, 16)
            for tb in range(TB):
                pool.wait_ge(s_y_ready, tb + 1)
                pool.dma_start(out[tb * P:tb * P + P, :], y[:, tb, :]).then_inc(s_stored, 16)
            pool.wait_ge(s_stored, 16 * TB)

        @block.scalar
        def _(act):
            do = nc.scalar.activation
            split_next = [0]

            def split_hi():
                m = split_next[0]
                split_next[0] += 1
                if m >= len(weights):
                    return
                src = loaded(act, weights[m])
                if m >= RING:
                    slot_released(act, m - RING)
                do(whi[:, m % RING, 0:src.shape[1]], src, ACT.Copy).then_inc(s_panel_hi, 1)
                act.wait_ge(s_panel_hi, up(s_panel_hi))

            evicted = [0]

            def early(place):
                k = filled(place)
                first, end_ = region(place)
                while split_next[0] < 7 + 1 + (2 if first else 0) + min(k // 4 + 1, end_ // 4):
                    split_hi()
                while evicted[0] < k // 2:
                    u = evicted[0]
                    evicted[0] += 1
                    act.wait_ge(*full("early", u))
                    if u >= 2:
                        act.wait_ge(*spilled(u - 2))
                    do(stage[:, u % 2, :], bank_of("early", u)[:, :], ACT.Copy).then_inc(free_sem("early", u), 1)
                    act.wait_ge(*freed("early", u))
                    act.dma_start(early_out[u], stage[:, u % 2, :]).then_inc(s_spilled[u % 2], 16)

            def norm(k, src, dst):
                for tb in range(TB):
                    if k:
                        act.wait_ge(s_x1_ready, TB + tb + 1)
                    do(dst[:, tb, :], src[:, tb, :], ACT.Square, accum_out=col(SS + tb)).then_inc(s_act_step, 1)
                    act.wait_ge(s_act_step, up(s_act_step))
                do(col(RSTD, 4), col(SS, 4), ACT.Ln, scale=1.0 / D, bias=cst[:, C_EPS:C_EPS + 1])\
                    .then_inc(s_act_step, 1)
                act.wait_ge(s_act_step, up(s_act_step))
                do(col(RSTD, 4), col(RSTD, 4), ACT.Exp, scale=-0.5).then_inc(s_act_step, 1)
                act.wait_ge(s_act_step, up(s_act_step))
                for tb in range(TB):
                    do(dst[:, tb, :], src[:, tb, :], ACT.Copy, scale=col(RSTD + tb)).then_inc(s_normed, 1)
                    act.wait_ge(s_normed, up(s_normed))
                for kc in range(KC):
                    act.wait_ge(*freed("h", k, kc))
                    tmp_ = (h_tmp2 if k else h_tmp)[:, kc % 2, :]
                    do(hhi[:, kc, :], tmp_, ACT.Copy).then_inc(s_h_hi, 1)
                    act.wait_ge(s_h_hi, up(s_h_hi))

            act.wait_ge(*freed("vectors"))
            do(ca[:, :], vc[:, V_C:V_C + KC], ACT.Silu).then_inc(s_c_act, 1)
            act.wait_ge(s_c_act, up(s_c_act))
            act.wait_ge(s_x_in, 16)
            act.wait_ge(s_constants_in, 16)
            split_hi()
            norm(0, x_in, x_norm)
            for n in range(7):
                split_hi()
                for b in (2 * n, 2 * n + 1):
                    act.wait_ge(*full("rw", b))
                    ps = bank_of("rw", b)
                    if b >= 2:
                        act.wait_ge(*freed("rw", b - 2))
                    elif b == 0:
                        act.wait_ge(s_u_prev_zero, 1)
                    do(u_prev[:, b % 2, 1:T + 1], ps[:, :], ACT.Copy, scale=vc[:, V_MU + b:V_MU + b + 1])\
                        .then_inc(s_rw_prev, 1)
                    act.wait_ge(s_rw_prev, up(s_rw_prev))
            act.wait_ge(*freed("rw", 13))
            do(lora_in[0:64, :], lora_in[0:64, :], ACT.Tanh).then_inc(s_rw_lora, 1)
            act.wait_ge(s_rw_lora, up(s_rw_lora))
            do(gate_lo[:, :], gate_lo[:, :], ACT.Sigmoid).then_inc(s_rw_lora, 1)
            act.wait_ge(s_rw_lora, up(s_rw_lora))
            early("rw lora")
            for c in range(4):
                act.wait_ge(*full("rw w", c))
                ps = bank_of("rw w", c)
                do(decay[:, c, :], ps[:, :], ACT.Sigmoid, bias=vc[:, V_W0 + c:V_W0 + c + 1]).then_inc(free_sem("rw w", c), 1)
                act.wait_ge(*freed("rw w", c))
            act.wait_ge(s_rw_k_k, 4)
            for c in range(4):
                act.wait_ge(*full("rw a", c))
                ps = bank_of("rw a", c)
                do(B[:, c, :], ps[:, :], ACT.Sigmoid, bias=vc[:, V_A0 + c:V_A0 + c + 1]).then_inc(free_sem("rw a", c), 1)
                act.wait_ge(*freed("rw a", c))
            early("rw kk")
            do(tmp[:, :, :], A[:, :, :], ACT.Square).then_inc(s_rw_kk2, 1)
            act.wait_ge(s_rw_kk2, up(s_rw_kk2))
            early("rw bonus")
            act.wait_ge(*freed("rw kk", 3))
            do(tmp[:, :, :], tmp[:, :, :], ACT.Sqrt).then_inc(s_rw_norm, 1)
            act.wait_ge(s_rw_norm, up(s_rw_norm))
            early(("rw sums", 0))
            early(("rw sums", 1))
            act.wait_ge(s_rw_sums, 1)
            do(tmp[:, :, :], cum[:, :, :], ACT.Exp, scale=-DECAY).then_inc(s_rw_e_r, 1)
            act.wait_ge(s_rw_e_r, up(s_rw_e_r))
            do(decay[:, :, :], decay[:, :, :], ACT.Exp, scale=-DECAY).then_inc(s_rw_e_a, 1)
            act.wait_ge(s_rw_e_a, up(s_rw_e_a))
            early(("rw sums", 2))
            do(cum[:, :, :], cum[:, :, :], ACT.Exp, scale=DECAY).then_inc(s_rw_e_bk, 1)
            act.wait_ge(s_rw_e_bk, up(s_rw_e_bk))
            do(blk16(FAC), blk16(FAC), ACT.Exp, scale=-DECAY).then_inc(s_rw_factor, 1)
            act.wait_ge(s_rw_factor, up(s_rw_factor))
            early(("rw sums", 3))
            act.wait_ge(s_rw_state, 1)
            for c in range(TB):
                for x_ in range(3):
                    act.wait_ge(*full("rw tok", c, x_))
                    ps = bank_of("rw tok", c, x_)
                    do(tok[:, x_, :], ps[:, :], ACT.Copy).then_inc(free_sem("rw tok", c, x_), 1)
                    act.wait_ge(*freed("rw tok", c, x_))
                early(("rw tok", c))
                for g in range(2):
                    act.wait_ge(*full("rw n", c, g))
                    ps = bank_of("rw n", c, g)
                    do(LX[:, g, :], ps[:, :], ACT.Copy, scale=-1.0).then_inc(free_sem("rw n", c, g), 1)
                    act.wait_ge(*freed("rw n", c, g))
                early(("rw x", c))
                for i in range(1, LEVELS):
                    for g in range(2):
                        act.wait_ge(*full("rw t", c, g, i))
                        ps = bank_of("rw t", c, g, i)
                        do(LX[:, g, :], ps[:, :], ACT.Copy).then_inc(free_sem("rw t", c, g, i), 1)
                        act.wait_ge(*freed("rw t", c, g, i))
                for what, dst in (("rw r", rhs_u), ("rw u", U)):
                    for g in range(2):
                        act.wait_ge(*full(what, c, g))
                        ps = bank_of(what, c, g)
                        do(dst[:, g, :], ps[:, 0:256], ACT.Copy, scale=-1.0 if dst is rhs_u else 1.0)\
                            .then_inc(free_sem(what, c, g), 1)
                        act.wait_ge(*freed(what, c, g))
                    early((what, c))
                for g in range(2):
                    act.wait_ge(*full("rw o", c, g))
                    ps = bank_of("rw o", c, g)
                    rows = slice(64 * g, 64 * g + 64)
                    do(R[rows, :, c * P:c * P + P], ps[rows, :].rearrange("p (b t) -> p b t", b=4), ACT.Copy)\
                        .then_inc(free_sem("rw o", c, g), 1)
                    act.wait_ge(*freed("rw o", c, g))
            early("rw mean")
            early("rw var")
            act.wait_ge(*freed("rw mean", 3))
            do(epi[:, :, :], R[:, :, :], ACT.Square).then_inc(s_rw_sq, 1)
            act.wait_ge(s_rw_sq, up(s_rw_sq))
            for c in range(4):
                act.wait_ge(*full("rw var", c))
                ps = bank_of("rw var", c)
                do(epi[:, c, :], ps[:, :], ACT.Ln, scale=1.0 / 64, bias=cst[:, C_GEPS:C_GEPS + 1])\
                    .then_inc(free_sem("rw var", c), 1)
                act.wait_ge(*freed("rw var", c))
            do(epi[:, :, :], epi[:, :, :], ACT.Exp, scale=-0.5).then_inc(s_rw_rstd, 1)
            act.wait_ge(s_rw_rstd, up(s_rw_rstd))
            early("rw g")
            act.wait_ge(*freed("rw g", 3))
            do(oc_hi[:, :, :], epi2[:, :, :], ACT.Copy).then_inc(s_rw_hi, 1)
            act.wait_ge(s_rw_hi, up(s_rw_hi))
            early("hg")
            act.wait_ge(s_rw_split, 1)
            split_hi()
            split_hi()
            for tb in range(TB):
                act.wait_ge(*full("hg v", tb))
                ps = bank_of("hg v", tb)
                do(Hv[:, tb, :], ps[:, :], ACT.Copy).then_inc(free_sem("hg v", tb), 1)
                act.wait_ge(*freed("hg v", tb))
            act.wait_ge(s_hg_neg_abs, 1)
            do(q_lev[:, :, :], Hk[:, :, :], ACT.Exp).then_inc(s_act_step, 1)
            act.wait_ge(s_act_step, up(s_act_step))
            do(q_lev[:, :, :], q_lev[:, :, :], ACT.Ln, bias=1.0).then_inc(s_hg_ln, 1)
            act.wait_ge(s_hg_ln, up(s_hg_ln))
            early("hg z")
            act.wait_ge(s_hg_ls_less_z, 1)
            do(Hk[:, :, :], Hk[:, :, :], ACT.Exp).then_inc(s_hg_key, 1)
            act.wait_ge(s_hg_key, up(s_hg_key))
            act.wait_ge(s_hg_in, 16)
            do(Hg[:, :, :], Hg[:, :, :], ACT.Silu).then_inc(s_hg_silu, 1)
            act.wait_ge(s_hg_silu, up(s_hg_silu))
            act.wait_ge(s_hg_last, 1)
            do(blk16(HLAST), blk16(HLAST), ACT.Exp).then_inc(s_hg_e_last, 1)
            act.wait_ge(s_hg_e_last, up(s_hg_e_last))
            for i in range(LEVELS):
                act.wait_ge(s_hg_rel, i + 1)
                do(Z[:, :, :], Z[:, :, :], ACT.Abs).then_inc(s_act_step, 1)
                act.wait_ge(s_act_step, up(s_act_step))
                do(Z[:, :, :], Z[:, :, :], ACT.Exp, scale=-1.0).then_inc(s_hg_e_rel, 1)
                act.wait_ge(s_hg_e_rel, up(s_hg_e_rel))
                early(("hg sc", i + 1))
            act.wait_ge(s_hg_lev, LEVELS)
            do(Z[:, :, :], Hb[:, :, :], ACT.Exp).then_inc(s_hg_e_b, 1)
            act.wait_ge(s_hg_e_b, up(s_hg_e_b))
            early("hg left")
            act.wait_ge(s_hg_left, 1)
            do(Z[:, :, :], Z[:, :, :], ACT.Exp, scale=-1.0).then_inc(s_hg_e_left, 1)
            act.wait_ge(s_hg_e_left, up(s_hg_e_left))
            for c in range(TB):
                act.wait_ge(*full("hg tok", c))
                ps = bank_of("hg tok", c)
                do(k_tok[:, :], ps[:, :], ACT.Copy).then_inc(free_sem("hg tok", c), 1)
                act.wait_ge(*freed("hg tok", c))
                act.wait_ge(*full("hg o", c))
                ps = bank_of("hg o", c)
                do(q_lev[:, :, c * P:c * P + P], ps[:, :].rearrange("p (h t) -> p h t", h=4), ACT.Copy)\
                    .then_inc(free_sem("hg o", c), 1)
                act.wait_ge(*freed("hg o", c))
            do(k_lev[:, :, :], q_lev[:, :, :], ACT.Square).then_inc(s_hg_sq, 1)
            act.wait_ge(s_hg_sq, up(s_hg_sq))
            early("hg ss")
            for h in range(4):
                act.wait_ge(*full("hg ss", h))
                ps = bank_of("hg ss", h)
                do(Z[:, h, :], ps[:, :], ACT.Ln, scale=1.0 / P, bias=cst[:, C_EPS:C_EPS + 1])\
                    .then_inc(free_sem("hg ss", h), 1)
                act.wait_ge(*freed("hg ss", h))
            do(Z[:, :, :], Z[:, :, :], ACT.Exp, scale=-0.5).then_inc(s_hg_rstd, 1)
            act.wait_ge(s_hg_rstd, up(s_hg_rstd))
            act.wait_ge(s_hg_out, 4)
            for h in range(4):
                do(ob_hi[:, h, :], q_lev[:, h, :], ACT.Copy).then_inc(s_hg_hi, 1)
                act.wait_ge(s_hg_hi, up(s_hg_hi))
            early("end")
            act.wait_ge(s_hg_split, 4)
            split_hi()
            act.wait_ge(s_angles, 2)
            do(cos_sin[:, :, :], ang[:, 0:2, :], ACT.Sin).then_inc(s_cos_sin, 1)
            act.wait_ge(s_cos_sin, up(s_cos_sin))
            act.wait_ge(s_lam_dot, 2)
            do(col(LR, 2), col(LR, 2), ACT.Exp).then_inc(s_lam_exp, 1)
            act.wait_ge(s_lam_exp, up(s_lam_exp))
            split_hi()
            for tb in range(TB):
                act.wait_ge(*full("da v", tb))
                ps = bank_of("da v", tb)
                do(v_tok[:, tb, :], ps[:, :], ACT.Copy).then_inc(free_sem("da v", tb), 1)
                act.wait_ge(*freed("da v", tb))
            for t_ in range(4 * TB + 4):
                n = (t_ % TB + 1) * P
                if t_ < 4 * TB:
                    for m in range(2):
                        act.wait_ge(s_max, 2 * t_ + m + 1)
                        if t_ >= 3:
                            act.wait_ge(*full("da pt", t_ - 3))
                        ps = bank_of("da s", t_, m)
                        do(prob[:, t_ % 3, m, 0:n], ps[:, 0:n], ACT.Exp, scale=0.125, bias=col(NB + 2 * (t_ % 3) + m),
                           accum_out=col(SUM + 2 * (t_ % 3) + m)).then_inc(free_sem("da s", t_, m), 1)
                        act.wait_ge(*freed("da s", t_, m))
                if 1 <= t_ <= 4 * TB:
                    n = ((t_ - 1) % TB + 1) * P
                    act.wait_ge(*full("da pt", t_ - 1))
                    ps = bank_of("da pt", t_ - 1)
                    do(probT[(t_ - 1) % 2][:, 0:n], ps[:, 0:n], ACT.Copy).then_inc(free_sem("da pt", t_ - 1), 1)
                    act.wait_ge(*freed("da pt", t_ - 1))
                h = t_ // 4 - 1
                if h >= 0 and t_ % 4 == 1:
                    if h:
                        act.wait_ge(s_da_lo, h)
                    act.wait_ge(*full("da o", h))
                    ps = bank_of("da o", h)
                    do(att[:, :], ps[:, :], ACT.Copy).then_inc(free_sem("da o", h), 1)
                    act.wait_ge(*freed("da o", h))
                    do(att2[:, :], att[:, :], ACT.Square).then_inc(s_da_sq, 1)
                    act.wait_ge(s_da_sq, up(s_da_sq))
                elif h >= 0 and t_ % 4 == 2:
                    act.wait_ge(*full("da ss", h))
                    ps = bank_of("da ss", h)
                    do(att2[:, :], ps[:, :], ACT.Ln, scale=1.0 / P, bias=cst[:, C_EPS:C_EPS + 1])\
                        .then_inc(free_sem("da ss", h), 1)
                    act.wait_ge(*freed("da ss", h))
                    do(att2[:, :], att2[:, :], ACT.Exp, scale=-0.5).then_inc(s_da_rstd, 1)
                    act.wait_ge(s_da_rstd, up(s_da_rstd))
                elif h >= 0 and t_ % 4 == 3:
                    act.wait_ge(s_da_out, h + 1)
                    do(oa_hi[:, h, :], att[:, :], ACT.Copy).then_inc(s_da_hi, 1)
                    act.wait_ge(s_da_hi, up(s_da_hi))
            act.wait_ge(s_da_lo, 4)
            for j in range(4):
                for g in range(3):
                    split_hi()
                    act.wait_ge(s_gate_in[g], 16 * (j + 1))
                    do(sg[:, g, :, :], sg[:, g, :, :], ACT.Sigmoid).then_inc(s_gated, 1)
                    act.wait_ge(s_gated, up(s_gated))
                for m in range(2):
                    act.wait_ge(s_mg_sum, 4 * j + m + 3)
                    do(mg_hi[:, 2 * j + m, :], mg[:, m, :], ACT.Copy).then_inc(s_mg_hi, 1)
                    act.wait_ge(s_mg_hi, up(s_mg_hi))
            for n in range(4):
                split_hi()
            norm(1, x1, x1_norm)
            for j in range(FFN // 256):
                for which in range(2):
                    split_hi()
                    if which == 0:
                        for m in range(2):
                            act.wait_ge(*full("ffn", j, 0, m))
                            ps = bank_of("ffn", j, 0, m)
                            if j:
                                act.wait_ge(*freed("ffn", j - 1, 1, m))
                            do(f_tmp[:, m, :], ps[:, :], ACT.Sigmoid).then_inc(s_ffn_sig, 1)
                            act.wait_ge(s_ffn_sig, up(s_ffn_sig))
            for j in range(FFN // 256):
                for k in range(2):
                    kk = 2 * j + k
                    if kk >= 2:
                        act.wait_ge(s_down_k, kk - 1)
                    do(d_hi[:, k, :], hid[:, kk, :], ACT.Copy).then_inc(s_d_hi, 1)
                    act.wait_ge(s_d_hi, up(s_d_hi))
                split_hi()
            for tb in range(TB):
                act.wait_ge(s_x2_ready, 2 * tb + 2)
                do(y[:, tb, :], x1[:, tb, :], ACT.Square, accum_out=col(SS + tb)).then_inc(s_act_step, 1)
                act.wait_ge(s_act_step, up(s_act_step))
                do(col(RSTD + tb), col(SS + tb), ACT.Ln, scale=1.0 / D, bias=cst[:, C_EPS:C_EPS + 1])\
                    .then_inc(s_act_step, 1)
                act.wait_ge(s_act_step, up(s_act_step))
                do(col(RSTD + tb), col(RSTD + tb), ACT.Exp, scale=-0.5).then_inc(s_final_rstd, 1)
                act.wait_ge(s_final_rstd, up(s_final_rstd))
            assert split_next[0] >= len(weights), (split_next, len(weights))

        @block.vector
        def _(dve):
            v = nc.vector
            stream_next, split_next, taken = [0], [0], [0]

            def tt(out_, a, b, op):
                return v.tensor_tensor(out_, a, b, op)

            def stt(out_, a, s_, b, op0, op1):
                return v.scalar_tensor_tensor(out=out_, in0=a, scalar=s_, in1=b, op0=op0, op1=op1)

            def ts(out_, a, s1, op0, s2=None, op1=None):
                if op1 is None:
                    return v.tensor_scalar(out_, a, s1, None, op0)
                return v.tensor_scalar(out_, a, s1, s2, op0, op1)

            def ada_sum(n, i):
                src = loaded(dve, i).rearrange("p (k n) -> p k n", k=KC)
                acc = ada_acc[:, n % 2, :]
                if n >= 2:
                    dve.wait_ge(*full("ada", n - 2))
                ts(acc, src[:, 0, :], ca[:, 0:1], ALU.mult).then_inc(s_dve_step, 1)
                dve.wait_ge(s_dve_step, up(s_dve_step))
                for k in range(1, KC - 1):
                    stt(acc, src[:, k, :], ca[:, k:k + 1], acc, ALU.mult, ALU.add).then_inc(s_dve_step, 1)
                    dve.wait_ge(s_dve_step, up(s_dve_step))
                stt(acc, src[:, KC - 1, :], ca[:, KC - 1:KC], acc, ALU.mult, ALU.add).then_inc(s_panel_taken, 1)
                dve.wait_ge(s_panel_taken, up(s_panel_taken))

            def ada_out(n):
                dve.wait_ge(*full("ada", n))
                ps = bank_of("ada", n)
                section = n // 4
                if section in (2, 5):
                    dve.wait_ge(s_gate_bias_in, 16 * (1 + section // 3))
                    row = gate_row[:, section // 3, (n % 4) * 256:(n % 4) * 256 + 256]
                    tt(row, ps[:, 0:256], row, ALU.add).then_inc(free_sem("ada", n), 1)
                    dve.wait_ge(*freed("ada", n))
                else:
                    tt(ada_cols[:, 2 * n:2 * n + 2], ps[:, 0:2], vc[:, V_ADAB + 2 * n:V_ADAB + 2 * n + 2], ALU.add)\
                        .then_inc(free_sem("ada", n), 1)
                    dve.wait_ge(*freed("ada", n))

            def take_panel():
                m = split_next[0]
                split_next[0] += 1
                if m >= len(weights):
                    return
                i = weights[m]
                src = loaded(dve, i)
                dve.wait_ge(s_panel_hi, m + 1)
                n = src.shape[1]
                tt(wlo[:, m % RING, 0:n], src, whi[:, m % RING, 0:n].bitcast(F32), ALU.subtract)\
                    .then_inc(s_panel_taken, 1)
                dve.wait_ge(s_panel_taken, up(s_panel_taken))
                if i + 1 < len(panels) and panels[i + 1][0] == "ada":
                    ada_sum(8 + taken[0], i + 1)
                    taken[0] += 1

            def early(place):
                k = filled(place)
                first, end_ = region(place)
                while split_next[0] < 7 + 1 + (2 if first else 0) + min(k // 4 + 1, end_ // 4):
                    take_panel()

            def normed_blocks(k):
                stt(gmul[:, k, :], ada_cols[:, 24 * k + 8:24 * k + 16], 1.0, vc[:, (V_NF if k else V_NM):(V_NF if k else V_NM) + KC], ALU.add, ALU.mult)\
                    .then_inc(s_dve_step, 1)
                dve.wait_ge(s_dve_step, up(s_dve_step))
                for kc in range(KC):
                    dve.wait_ge(*full("h", k, kc))
                    ps = bank_of("h", k, kc)
                    tmp_ = (h_tmp2 if k else h_tmp)[:, kc % 2, :]
                    ts(tmp_, ps[:, :], gmul[:, k, kc:kc + 1], ALU.mult, ada_cols[:, 24 * k + kc:24 * k + kc + 1], ALU.add)\
                        .then_inc(free_sem("h", k, kc), 1)
                    dve.wait_ge(*freed("h", k, kc))
                    dve.wait_ge(s_h_hi, 8 * k + kc + 1)
                    tt(hlo[:, kc, :], tmp_, hhi[:, kc, :].bitcast(F32), ALU.subtract).then_inc(s_h_lo, 1)
                    dve.wait_ge(s_h_lo, up(s_h_lo))

            dve.wait_ge(*full("vectors"))
            ps = bank_of("vectors")
            v.tensor_copy(vc[:, :], ps[:, 0:NVEC]).then_inc(free_sem("vectors"), 1)
            dve.wait_ge(*freed("vectors"))
            ts(col(OM_MU, 14), vc[:, V_MU:V_MU + 14], -1.0, ALU.mult, 1.0, ALU.add).then_inc(s_dve_step, 1)
            dve.wait_ge(s_dve_step, up(s_dve_step))
            ts(col(OM_KA, 4), vc[:, V_KA:V_KA + 4], -1.0, ALU.mult, 1.0, ALU.add).then_inc(s_dve_step, 1)
            dve.wait_ge(s_dve_step, up(s_dve_step))
            ts(col(SUBW), vc[:, V_SUB:V_SUB + 1], 1.0 - LAM_INIT, ALU.mult).then_inc(s_dve_step, 1)
            dve.wait_ge(s_dve_step, up(s_dve_step))
            v.memset(u_prev[:, :, 0:1], 0.0).then_inc(s_u_prev_zero, 1)
            dve.wait_ge(s_u_prev_zero, up(s_u_prev_zero))
            dve.wait_ge(s_c_act, 1)
            for n in range(8):
                ada_sum(n, n)
                if n:
                    ada_out(n - 1)
            ada_out(7)
            take_panel()
            normed_blocks(0)
            dve.wait_ge(s_masks, 1)
            for n in range(7):
                take_panel()
                for b in (2 * n, 2 * n + 1):
                    dve.wait_ge(s_rw_prev, b + 1)
                    ps = bank_of("rw", b)
                    dst = (R[:, b, :] if b < 4 else K[:, b - 4, :] if b < 8 else V[:, b - 8, :] if b < 12
                           else lora_in[:, :] if b == 12 else gate_lo[:, :])
                    stt(dst, ps[:, :], col(OM_MU + b), u_prev[:, b % 2, 0:T], ALU.mult, ALU.add)\
                        .then_inc(free_sem("rw", b), 1)
                    dve.wait_ge(*freed("rw", b))
                ada_out(8 + n)
            for c in range(4):
                ts(A[:, c, :], K[:, c, :], vc[:, V_KK + c:V_KK + c + 1], ALU.mult).then_inc(s_rw_k_k, 1)
                dve.wait_ge(s_rw_k_k, up(s_rw_k_k))
            early("rw lora")
            early("rw kk")
            for c in range(4):
                dve.wait_ge(*full("rw kk", c))
                ts(tmp[:, c, :], bank_of("rw kk", c)[:, :], 1e-24, ALU.max).then_inc(free_sem("rw kk", c), 1)
                dve.wait_ge(*freed("rw kk", c))
            early("rw bonus")
            dve.wait_ge(s_rw_norm, 1)
            v.reciprocal(tmp[:, :, :], tmp[:, :, :]).then_inc(s_dve_step, 1)
            dve.wait_ge(s_dve_step, up(s_dve_step))
            tt(A[:, :, :], A[:, :, :], tmp[:, :, :], ALU.mult).then_inc(s_dve_step, 1)
            dve.wait_ge(s_dve_step, up(s_dve_step))
            for c in range(4):
                ts(cum[:, c, :], B[:, c, :], vc[:, V_KA + c:V_KA + c + 1], ALU.mult, col(OM_KA + c), ALU.add)\
                    .then_inc(s_dve_step, 1)
                dve.wait_ge(s_dve_step, up(s_dve_step))
            tt(K[:, :, :], K[:, :, :], cum[:, :, :], ALU.mult).then_inc(s_dve_step, 1)
            dve.wait_ge(s_dve_step, up(s_dve_step))
            for c in range(4):
                stt(cum[:, c, :], R[:, c, :], vc[:, V_RK + c:V_RK + c + 1], K[:, c, :], ALU.mult, ALU.mult)\
                    .then_inc(s_rw_rkk, 1)
                dve.wait_ge(s_rw_rkk, up(s_rw_rkk))
            dve.wait_ge(*full("rw bonus"))
            v.tensor_copy(bonus[:, :], bank_of("rw bonus")[0:8, :]).then_inc(free_sem("rw bonus"), 1)
            dve.wait_ge(*freed("rw bonus"))
            early(("rw sums", 0))
            tt(B[:, :, :], A[:, :, :], B[:, :, :], ALU.mult).then_inc(s_dve_step, 1)
            dve.wait_ge(s_dve_step, up(s_dve_step))
            for n in range(16):
                v.tensor_tensor_scan(blocks(cum)[:, n, :], ones, blocks(decay)[:, n, :], 0.0, ALU.mult, ALU.add)\
                    .then_inc(s_dve_step, 1)
                dve.wait_ge(s_dve_step, up(s_dve_step))
            early(("rw sums", 1))
            v.tensor_copy(blk16(BREF), blocks(cum)[:, :, 63]).then_inc(s_dve_step, 1)
            dve.wait_ge(s_dve_step, up(s_dve_step))
            v.tensor_copy(blk16(BLAST), blocks(cum)[:, :, P - 1]).then_inc(s_dve_step, 1)
            dve.wait_ge(s_dve_step, up(s_dve_step))
            tt(decay[:, :, :], cum[:, :, :], decay[:, :, :], ALU.subtract).then_inc(s_dve_step, 1)
            dve.wait_ge(s_dve_step, up(s_dve_step))
            middle = bcast(blk16(BREF).unsqueeze(2), P, 16, P)
            tt(blocks(decay), blocks(decay), middle, ALU.subtract).then_inc(s_dve_step, 1)
            dve.wait_ge(s_dve_step, up(s_dve_step))
            tt(blocks(cum), blocks(cum), middle, ALU.subtract).then_inc(s_dve_step, 1)
            dve.wait_ge(s_dve_step, up(s_dve_step))
            tt(blk16(FAC), blk16(BLAST), blk16(BREF), ALU.subtract).then_inc(s_dve_step, 1)
            dve.wait_ge(s_dve_step, up(s_dve_step))
            fac = blk16(FAC).rearrange("p (a c) -> p a c", c=TB)
            ref = blk16(BREF).rearrange("p (a c) -> p a c", c=TB)
            tt(fac[:, :, 0:TB - 1], fac[:, :, 0:TB - 1], ref[:, :, 1:TB], ALU.add).then_inc(s_rw_sums, 1)
            dve.wait_ge(s_rw_sums, up(s_rw_sums))
            early(("rw sums", 2))
            dve.wait_ge(s_rw_e_r, 1)
            tt(R[:, :, :], R[:, :, :], tmp[:, :, :], ALU.mult).then_inc(s_dve_step, 1)
            dve.wait_ge(s_dve_step, up(s_dve_step))
            dve.wait_ge(s_rw_e_a, 1)
            tt(A[:, :, :], A[:, :, :], decay[:, :, :], ALU.mult).then_inc(s_dve_step, 1)
            dve.wait_ge(s_dve_step, up(s_dve_step))
            early(("rw sums", 3))
            dve.wait_ge(s_rw_e_bk, 1)
            tt(B[:, :, :], B[:, :, :], cum[:, :, :], ALU.mult).then_inc(s_dve_step, 1)
            dve.wait_ge(s_dve_step, up(s_dve_step))
            tt(K[:, :, :], K[:, :, :], cum[:, :, :], ALU.mult).then_inc(s_dve_step, 1)
            dve.wait_ge(s_dve_step, up(s_dve_step))
            dve.wait_ge(s_rw_factor, 1)
            dve.wait_ge(s_masks, 1)
            v.memset(M[:, :, :], 0.0).then_inc(s_rw_state, 1)
            dve.wait_ge(s_rw_state, up(s_rw_state))

            def four(ap):
                return ap.rearrange("p (h t) -> p h t", h=4)

            def lmask(i, upper):
                return bcast(lev_mask[:, 2 * i + upper, :].unsqueeze(1), P, 4, P)

            id4 = bcast(ident.unsqueeze(1), P, 4, P)
            for c in range(TB):
                early(("rw tok", c))
                for g in range(2):
                    for hl in range(4):
                        dve.wait_ge(*full("rw sc", c, g, hl))
                        ps = bank_of("rw sc", c, g, hl)
                        tt(SC[g][:, hl, :], ps[:, :], cst[:, C_MASK:C_MASK + T], ALU.mult).then_inc(free_sem("rw sc", c, g, hl), 1)
                        dve.wait_ge(*freed("rw sc", c, g, hl))
                for g in range(2):
                    dve.wait_ge(*freed("rw n", c, g))
                    v.tensor_copy(four(X[:, g, :]), id4).then_inc(s_dve_step, 1)
                    dve.wait_ge(s_dve_step, up(s_dve_step))
                    v.tensor_copy(four(XT[:, g, :]), id4).then_inc(s_dve_step, 1)
                    dve.wait_ge(s_dve_step, up(s_dve_step))
                    v.copy_predicated(four(XT[:, g, :]), lmask(0, 1), SC[g][:, :, 0:P]).then_inc(s_dve_step, 1)
                    dve.wait_ge(s_dve_step, up(s_dve_step))
                    v.copy_predicated(four(X[:, g, :]), lmask(0, 0), four(LX[:, g, :])).then_inc(s_rw_x, 1)
                    dve.wait_ge(s_rw_x, up(s_rw_x))
                early(("rw x", c))
                for i in range(1, LEVELS):
                    for g in range(2):
                        if i < LEVELS - 1:
                            dve.wait_ge(*full("rw p", c, g, i))
                            ps = bank_of("rw p", c, g, i)
                            v.copy_predicated(four(X[:, g, :]), lmask(i, 0), four(ps[:, :])).then_inc(free_sem("rw p", c, g, i), 1)
                            dve.wait_ge(*freed("rw p", c, g, i))
                        dve.wait_ge(*full("rw pt", c, g, i))
                        ps = bank_of("rw pt", c, g, i)
                        v.copy_predicated(four(XT[:, g, :]), lmask(i, 1), four(ps[:, :])).then_inc(free_sem("rw pt", c, g, i), 1)
                        dve.wait_ge(*freed("rw pt", c, g, i))
                early(("rw r", c))
                early(("rw u", c))
                if c < TB - 1:
                    for g in range(2):
                        dve.wait_ge(*full("rw m", c, g))
                        ps = bank_of("rw m", c, g)
                        rows = slice(64 * g, 64 * g + 64)
                        state = M[rows, :, :]
                        tt(state, state, ps[rows, 0:256].rearrange("p (b v) -> p b v", b=4), ALU.add)\
                            .then_inc(free_sem("rw m", c, g), 1)
                        dve.wait_ge(*freed("rw m", c, g))
                        tt(state, state, bcast(fac[rows, :, c:c + 1], 64, 4, 64), ALU.mult)\
                            .then_inc(s_rw_state, 1)
                        dve.wait_ge(s_rw_state, up(s_rw_state))
            early("rw mean")
            dve.wait_ge(*freed("rw o", TB - 1, 1))
            for c in range(4):
                dve.wait_ge(*full("rw mean", c))
                ps = bank_of("rw mean", c)
                stt(R[:, c, :], ps[:, :], -1.0 / 64, R[:, c, :], ALU.mult, ALU.add).then_inc(free_sem("rw mean", c), 1)
                dve.wait_ge(*freed("rw mean", c))
            for c in range(4):
                dve.wait_ge(*full("rw bv", c))
                ps = bank_of("rw bv", c)
                tt(epi2[:, c, :], V[:, c, :], ps[:, :], ALU.mult).then_inc(free_sem("rw bv", c), 1)
                dve.wait_ge(*freed("rw bv", c))
            early("rw var")
            dve.wait_ge(s_rw_rstd, 1)
            tt(R[:, :, :], R[:, :, :], epi[:, :, :], ALU.mult).then_inc(s_dve_step, 1)
            dve.wait_ge(s_dve_step, up(s_dve_step))
            for c in range(4):
                ts(R[:, c, :], R[:, c, :], vc[:, V_GNW + c:V_GNW + c + 1], ALU.mult, vc[:, V_GNB + c:V_GNB + c + 1], ALU.add)\
                    .then_inc(s_dve_step, 1)
                dve.wait_ge(s_dve_step, up(s_dve_step))
            early("rw g")
            tt(R[:, :, :], R[:, :, :], epi2[:, :, :], ALU.add).then_inc(s_dve_step, 1)
            dve.wait_ge(s_dve_step, up(s_dve_step))
            for c in range(4):
                dve.wait_ge(*full("rw g", c))
                ps = bank_of("rw g", c)
                tt(epi2[:, c, :], R[:, c, :], ps[:, :], ALU.mult).then_inc(free_sem("rw g", c), 1)
                dve.wait_ge(*freed("rw g", c))
            dve.wait_ge(s_rw_hi, 1)
            tt(oc_lo[:, :, :], epi2[:, :, :], oc_hi[:, :, :].bitcast(F32), ALU.subtract).then_inc(s_rw_split, 1)
            dve.wait_ge(s_rw_split, up(s_rw_split))
            early("hg")
            take_panel()
            take_panel()
            dve.wait_ge(s_z_in, 16)
            stt(Hk[:, :, :], Z[:, :, :], -1.0, Z[:, :, :], ALU.mult, ALU.min).then_inc(s_hg_neg_abs, 1)
            dve.wait_ge(s_hg_neg_abs, up(s_hg_neg_abs))
            early("hg z")
            dve.wait_ge(s_hg_ln, 1)
            stt(k_lev[:, :, :], Z[:, :, :], 0.0, q_lev[:, :, :], ALU.min, ALU.subtract).then_inc(s_dve_step, 1)
            dve.wait_ge(s_dve_step, up(s_dve_step))
            tt(Hk[:, :, :], k_lev[:, :, :], Z[:, :, :], ALU.subtract).then_inc(s_hg_ls_less_z, 1)
            dve.wait_ge(s_hg_ls_less_z, up(s_hg_ls_less_z))
            for n in range(16):
                v.tensor_tensor_scan(blocks(Hb)[:, n, :], ones, blocks(k_lev)[:, n, :], 0.0, ALU.mult, ALU.add)\
                    .then_inc(s_dve_step, 1)
                dve.wait_ge(s_dve_step, up(s_dve_step))
            v.tensor_copy(blk16(HLAST), blocks(Hb)[:, :, P - 1]).then_inc(s_dve_step, 1)
            dve.wait_ge(s_dve_step, up(s_dve_step))
            v.tensor_copy(blk16(BLAST), blk16(HLAST)).then_inc(s_hg_last, 1)
            dve.wait_ge(s_hg_last, up(s_hg_last))
            v.memset(ST[:, :, :, :], 0.0).then_inc(s_dve_step, 1)
            dve.wait_ge(s_dve_step, up(s_dve_step))
            v.memset(q_lev[:, :, :], 0.0).then_inc(s_dve_step, 1)
            dve.wait_ge(s_dve_step, up(s_dve_step))
            v.memset(k_lev[:, :, :], 0.0).then_inc(s_dve_step, 1)
            dve.wait_ge(s_dve_step, up(s_dve_step))

            def halves(tile, s):
                return tile[:, :, :].rearrange("p a (n s) -> p (a n) s", s=2 * s)

            def rel(i):
                s = 1 << i
                hb = halves(Hb, s)
                tt(halves(Z, s), hb, bcast(hb[:, :, s - 1:s], P, 1024 // s, 2 * s), ALU.subtract)\
                    .then_inc(s_hg_rel, 1)
                dve.wait_ge(s_hg_rel, up(s_hg_rel))

            def gather(lev, mask):
                for c in range(TB):
                    dve.wait_ge(*full("hg sc", lev, c))
                    ps = bank_of("hg sc", lev, c)
                    v.copy_predicated(ST[:, c, :, :], bcast(mask.unsqueeze(1), P, 4, P), four(ps[:, :]))\
                        .then_inc(free_sem("hg sc", lev, c), 1)
                    dve.wait_ge(*freed("hg sc", lev, c))

            for i in range(LEVELS):
                s = 1 << i
                rel(i)
                if i == 0:
                    dve.wait_ge(s_hg_key, 1)
                    gather(0, lev_mask[:, 2 * LEVELS, :])
                else:
                    gather(i, lev_mask[:, 2 * (i - 1) + 1, :])
                dve.wait_ge(s_hg_e_rel, i + 1)
                dve.wait_ge(s_hq_in, 16)
                z, q, k = halves(Z, s), halves(Hq, s), halves(Hk, s)
                tt(halves(q_lev, s)[:, :, s:], q[:, :, s:], z[:, :, s:], ALU.mult).then_inc(s_dve_step, 1)
                dve.wait_ge(s_dve_step, up(s_dve_step))
                tt(halves(k_lev, s)[:, :, :s], k[:, :, :s], z[:, :, :s], ALU.mult).then_inc(s_hg_lev, 1)
                dve.wait_ge(s_hg_lev, up(s_hg_lev))
                early(("hg sc", i + 1))
            gather(LEVELS, lev_mask[:, 2 * LEVELS - 1, :])
            dve.wait_ge(s_hg_e_b, 1)
            tt(Hq[:, :, :], Hq[:, :, :], Z[:, :, :], ALU.mult).then_inc(s_dve_step, 1)
            dve.wait_ge(s_dve_step, up(s_dve_step))
            tt(blocks(Z), blocks(Hb), bcast(blk16(BLAST).unsqueeze(2), P, 16, P), ALU.subtract)\
                .then_inc(s_hg_left, 1)
            dve.wait_ge(s_hg_left, up(s_hg_left))
            early("hg left")
            dve.wait_ge(s_hg_e_left, 1)
            tt(Hk[:, :, :], Hk[:, :, :], Z[:, :, :], ALU.mult).then_inc(s_hg_k_left, 1)
            dve.wait_ge(s_hg_k_left, up(s_hg_k_left))
            dve.wait_ge(s_hg_e_last, 1)
            for c in range(TB - 1):
                dve.wait_ge(*full("hg s", c))
                ps = bank_of("hg s", c)
                if c == 0:
                    v.tensor_copy(Hs[:, :, :], four(ps[:, :])).then_inc(free_sem("hg s", c), 1)
                    dve.wait_ge(*freed("hg s", c))
                else:
                    for h in range(4):
                        k = HLAST + 4 * h + c
                        stt(Hs[:, h, :], Hs[:, h, :], col(k), ps[:, h * P:h * P + P], ALU.mult, ALU.add)\
                            .then_inc(s_dve_step, 1)
                        dve.wait_ge(s_dve_step, up(s_dve_step))
                    v.tensor_copy(Hs[:, 0, 0:2], Hs[:, 0, 0:2]).then_inc(free_sem("hg s", c), 1)
                    dve.wait_ge(*freed("hg s", c))
            early("hg ss")
            early("end")
            dve.wait_ge(s_hg_rstd, 1)
            dve.wait_ge(s_hg_silu, 1)
            for h in range(4):
                tt(q_lev[:, h, :], q_lev[:, h, :], Z[:, h, :], ALU.mult).then_inc(s_dve_step, 1)
                dve.wait_ge(s_dve_step, up(s_dve_step))
                stt(q_lev[:, h, :], q_lev[:, h, :], vc[:, V_HGN:V_HGN + 1], Hg[:, h, :], ALU.mult, ALU.mult)\
                    .then_inc(s_hg_out, 1)
                dve.wait_ge(s_hg_out, up(s_hg_out))
            for h in range(4):
                dve.wait_ge(s_hg_hi, h + 1)
                tt(ob_lo[:, h, :], q_lev[:, h, :], ob_hi[:, h, :].bitcast(F32), ALU.subtract)\
                    .then_inc(s_hg_split, 1)
                dve.wait_ge(s_hg_split, up(s_hg_split))
            dve.wait_ge(s_positions_in, 16)
            dve.wait_ge(s_lambda_in, 16)
            turn, n_ = ang[:, 0, :], ang[:, 1, :]
            v.tensor_copy(ang[:, 2, :], pos_i[:, :]).then_inc(s_dve_step, 1)
            dve.wait_ge(s_dve_step, up(s_dve_step))
            ts(ang[:, 2, :], ang[:, 2, :], cst[:, C_FREQ:C_FREQ + 1], ALU.mult).then_inc(s_dve_step, 1)
            dve.wait_ge(s_dve_step, up(s_dve_step))
            for x_ in (1, 0):
                dst = ang[:, x_, :]
                ts(turns[:, :], ang[:, 2, :], 1.0 / TWO_PI, ALU.mult, 0.0 if x_ else 0.25, ALU.add)\
                    .then_inc(s_dve_step, 1)
                dve.wait_ge(s_dve_step, up(s_dve_step))
                ts(turns[:, :], turns[:, :], ROUND, ALU.add).then_inc(s_dve_step, 1)
                dve.wait_ge(s_dve_step, up(s_dve_step))
                ts(turns[:, :], turns[:, :], ROUND, ALU.subtract).then_inc(s_dve_step, 1)
                dve.wait_ge(s_dve_step, up(s_dve_step))
                stt(dst, turns[:, :], -TURN[0], ang[:, 2, :], ALU.mult, ALU.add).then_inc(s_dve_step, 1)
                dve.wait_ge(s_dve_step, up(s_dve_step))
                stt(dst, turns[:, :], -TURN[1], dst, ALU.mult, ALU.add).then_inc(s_dve_step, 1)
                dve.wait_ge(s_dve_step, up(s_dve_step))
                stt(dst, turns[:, :], -TURN[2], dst, ALU.mult, ALU.add).then_inc(s_dve_step, 1)
                dve.wait_ge(s_dve_step, up(s_dve_step))
                ts(dst, dst, 0.0 if x_ else TWO_PI / 4, ALU.add).then_inc(s_dve_step, 1)
                dve.wait_ge(s_dve_step, up(s_dve_step))
                ts(dst, dst, 3.1415925, ALU.min, -3.1415925, ALU.max).then_inc(s_angles, 1)
                dve.wait_ge(s_angles, up(s_angles))
            take_panel()
            for x_ in range(2):
                pair = lam_in[:, 128 * x_:128 * x_ + 128].rearrange("p (a e) -> p a e", a=2)
                tt(pair[:, 0, :], pair[:, 0, :], pair[:, 1, :], ALU.mult).then_inc(s_dve_step, 1)
                dve.wait_ge(s_dve_step, up(s_dve_step))
                v.reduce_sum(col(LR + x_), pair[:, 0, :], AX_X).then_inc(s_lam_dot, 1)
                dve.wait_ge(s_lam_dot, up(s_lam_dot))
            dve.wait_ge(s_lam_exp, 1)
            stt(col(NLAM), col(LR + 1), -LAM_INIT, col(LR), ALU.add, ALU.subtract).then_inc(s_dve_step, 1)
            dve.wait_ge(s_dve_step, up(s_dve_step))
            dve.wait_ge(s_cos_sin, 1)
            for n in range(8):
                if n == 2:
                    take_panel()
                dve.wait_ge(*full("da rot", n))
                ps = bank_of("da rot", n)
                x_ = qk[:, n // 4, n % 4, :]
                tt(rot[:, n % 4, :], ps[:, :], cos_sin[:, 1, :], ALU.mult).then_inc(free_sem("da rot", n), 1)
                dve.wait_ge(*freed("da rot", n))
                tt(x_, x_, cos_sin[:, 0, :], ALU.mult).then_inc(s_dve_step, 1)
                dve.wait_ge(s_dve_step, up(s_dve_step))
                tt(x_, x_, rot[:, n % 4, :], ALU.add).then_inc(s_roped, 1)
                dve.wait_ge(s_roped, up(s_roped))
            for t_ in range(4 * TB + 4):
                if t_ < 4 * TB:
                    n, nb = (t_ % TB + 1) * P, NB + 2 * (t_ % 3)
                    for m in range(2):
                        dve.wait_ge(*full("da s", t_, m))
                        v.reduce_max(col(MX + m), bank_of("da s", t_, m)[:, 0:n], AX_X).then_inc(s_dve_step, 1)
                        dve.wait_ge(s_dve_step, up(s_dve_step))
                        ts(col(nb + m), col(MX + m), -0.125, ALU.mult).then_inc(s_max, 1)
                        dve.wait_ge(s_max, up(s_max))
                if 1 <= t_ <= 4 * TB:
                    n, r = ((t_ - 1) % TB + 1) * P, (t_ - 1) % 3
                    dve.wait_ge(*freed("da s", t_ - 1, 0))
                    dve.wait_ge(*freed("da s", t_ - 1, 1))
                    v.reciprocal(col(RS, 2), col(SUM + 2 * r, 2)).then_inc(s_dve_step, 1)
                    dve.wait_ge(s_dve_step, up(s_dve_step))
                    tt(col(LR), col(RS + 1), col(NLAM), ALU.mult).then_inc(s_dve_step, 1)
                    dve.wait_ge(s_dve_step, up(s_dve_step))
                    p0, p1 = prob[:, r, 0, 0:n], prob[:, r, 1, 0:n]
                    ts(p0, p0, col(RS), ALU.mult).then_inc(s_dve_step, 1)
                    dve.wait_ge(s_dve_step, up(s_dve_step))
                    stt(p0, p1, col(LR), p0, ALU.mult, ALU.add).then_inc(s_da_p, 1)
                    dve.wait_ge(s_da_p, up(s_da_p))
                h = t_ // 4 - 1
                if h >= 0 and t_ % 4 == 2:
                    dve.wait_ge(s_da_rstd, h + 1)
                    stt(att[:, :], att[:, :], col(SUBW), att2[:, :], ALU.mult, ALU.mult).then_inc(s_da_out, 1)
                    dve.wait_ge(s_da_out, up(s_da_out))
                elif h >= 0 and t_ % 4 == 3:
                    dve.wait_ge(s_da_hi, h + 1)
                    tt(oa_lo[:, h, :], att[:, :], oa_hi[:, h, :].bitcast(F32), ALU.subtract).then_inc(s_da_lo, 1)
                    dve.wait_ge(s_da_lo, up(s_da_lo))
            for j in range(4):
                for g in range(3):
                    take_panel()
                    dve.wait_ge(s_gated, 3 * j + g + 1)
                    for m in range(2):
                        dve.wait_ge(*full("branch", j, g, m))
                        ps = bank_of("branch", j, g, m)
                        if g == 0:
                            tt(mg[:, m, :], sg[:, g, m, :], ps[:, :], ALU.mult).then_inc(free_sem("branch", j, g, m), 1)
                            dve.wait_ge(*freed("branch", j, g, m))
                        else:
                            tt(mg_tmp[:, :], sg[:, g, m, :], ps[:, :], ALU.mult).then_inc(free_sem("branch", j, g, m), 1)
                            dve.wait_ge(*freed("branch", j, g, m))
                            tt(mg[:, m, :], mg[:, m, :], mg_tmp[:, :], ALU.add).then_inc(s_mg_sum, 1)
                            dve.wait_ge(s_mg_sum, up(s_mg_sum))
                    if (j, g) in ADA_AT_BRANCH:
                        ada_out(15 + ADA_AT_BRANCH.index((j, g)))
                for m in range(2):
                    dve.wait_ge(s_mg_hi, 2 * j + m + 1)
                    tt(mg_lo[:, 2 * j + m, :], mg[:, m, :], mg_hi[:, 2 * j + m, :].bitcast(F32), ALU.subtract)\
                        .then_inc(s_merged, 1)
                    dve.wait_ge(s_merged, up(s_merged))
            for n in range(4):
                take_panel()
            dve.wait_ge(s_x_again, 16)
            for n in range(2):
                for tb in range(TB):
                    dve.wait_ge(*full("out", n, tb))
                    ps = bank_of("out", n, tb)
                    cols_ = slice(n * T, n * T + T)
                    tt(mg[:, 0, :], gate_row[:, 0, cols_], ps[:, :], ALU.mult).then_inc(free_sem("out", n, tb), 1)
                    dve.wait_ge(*freed("out", n, tb))
                    tt(x1[:, tb, cols_], x1[:, tb, cols_], mg[:, 0, :], ALU.add).then_inc(s_x1_ready, 1)
                    dve.wait_ge(s_x1_ready, up(s_x1_ready))
            normed_blocks(1)
            for j in range(FFN // 256):
                take_panel()
                take_panel()
                for m in range(2):
                    dve.wait_ge(s_ffn_sig, 2 * j + m + 1)
                    tt(f_tmp[:, m, :], f_tmp[:, m, :], bank_of("ffn", j, 0, m)[:, :], ALU.mult)\
                        .then_inc(free_sem("ffn", j, 0, m), 1)
                    dve.wait_ge(*freed("ffn", j, 0, m))
                    dve.wait_ge(*full("ffn", j, 1, m))
                    ps = bank_of("ffn", j, 1, m)
                    tt(hid[:, 2 * j + m, :], f_tmp[:, m, :], ps[:, :], ALU.mult).then_inc(free_sem("ffn", j, 1, m), 1)
                    dve.wait_ge(*freed("ffn", j, 1, m))
                if j < 4:
                    ada_out(20 + j)
            for j in range(FFN // 256):
                for k in range(2):
                    kk = 2 * j + k
                    dve.wait_ge(s_d_hi, kk + 1)
                    tt(d_lo[:, k, :], hid[:, kk, :], d_hi[:, k, :].bitcast(F32), ALU.subtract)\
                        .then_inc(s_d_lo, 1)
                    dve.wait_ge(s_d_lo, up(s_d_lo))
                take_panel()
            dve.wait_ge(s_final_weight_in, 16)
            for tb in range(TB):
                for n in range(2):
                    dve.wait_ge(*full("down", tb, n))
                    ps = bank_of("down", tb, n)
                    cols_ = slice(n * T, n * T + T)
                    tt(f_tmp[:, n, :], gate_row[:, 1, cols_], ps[:, :], ALU.mult).then_inc(free_sem("down", tb, n), 1)
                    dve.wait_ge(*freed("down", tb, n))
                    tt(x1[:, tb, cols_], x1[:, tb, cols_], f_tmp[:, n, :], ALU.add).then_inc(s_x2_ready, 1)
                    dve.wait_ge(s_x2_ready, up(s_x2_ready))
                dve.wait_ge(s_final_rstd, tb + 1)
                stt(y[:, tb, :], x1[:, tb, :], col(RSTD + tb), final_row[:, :], ALU.mult, ALU.mult)\
                    .then_inc(s_y_ready, 1)
                dve.wait_ge(s_y_ready, up(s_y_ready))

        @block.tensor
        def _(pe):
            t = nc.tensor
            started = [0] * BANKS
            m_next = [0]
            ada_next = [8]
            ada_at = [i for i, (kind, _) in enumerate(panels) if kind == "ada"]

            def begin(*use):
                bank, k = plan.of[use]
                assert k == started[bank], use
                started[bank] += 1
                if k:
                    pe.wait_ge(bank_free[bank], k)
                return psum[bank]

            def end(instruction, *use):
                instruction.then_inc(bank_full[plan.of[use][0]], 1)

            def mm(out_, lhsT, rhs, start=True, stop=True):
                return t.matmul(out_, lhsT, rhs, start=start, stop=stop, skip_group_check=True)

            def next_panel():
                m = m_next[0]
                m_next[0] += 1
                pe.wait_ge(s_panel_taken, weights[m] + 1)
                return m % RING

            def split3(ps, w, x_, first, last):
                mm(ps, w[0], x_[0], first, False)
                mm(ps, w[0], x_[1], False, False)
                return mm(ps, w[1], x_[0], False, last)

            def stationary_unit(slot, m, xs, kcs, *use):
                ps = begin(*use)
                for k in range(kcs):
                    at_ = slice(256 * k + P * m, 256 * k + P * m + P)
                    last = split3(ps[:, :], (whi[:, slot, at_], wlo[:, slot, at_]),
                                  (xs[0][:, k, :], xs[1][:, k, :]), k == 0, k == kcs - 1)
                end(last, *use)

            def moving_units(xs, uses, between=None):
                tiles = [begin(*u) for u in uses]
                for half in range(2):
                    slot = next_panel()
                    for tb, ps in enumerate(tiles):
                        for k in range(4):
                            kk, cols_ = 4 * half + k, slice(T * k, T * k + T)
                            toks = slice(tb * P, tb * P + P)
                            last = split3(ps[:, :], (xs[0][:, kk, toks], xs[1][:, kk, toks]),
                                          (whi[:, slot, cols_], wlo[:, slot, cols_]), kk == 0, kk == KC - 1)
                        if half:
                            end(last, *uses[tb])
                    if not half:
                        last.then_inc(s_panel_used, 1)
                        if between:
                            between()

            def ada(n):
                pe.wait_ge(s_panel_taken, ada_at[n] + 1)
                ps = begin("ada", n)
                acc = ada_acc[:, n % 2, :]
                if n // 4 in (2, 5):
                    last = mm(ps[:, 0:256], ones, acc)
                else:
                    for m in range(2):
                        last = mm(ps[:, m:m + 1], acc[:, P * m:P * m + P], ones[:, 0:1])
                end(last, "ada", n)

            def late_ada():
                ada(ada_next[0])
                ada_next[0] += 1

            def transposes(k, src):
                pe.wait_ge(s_normed, TB * (k + 1))
                for kc in range(KC):
                    ps = begin("h", k, kc)
                    for tb in range(TB):
                        last = t.transpose(ps[:, tb * P:tb * P + P], src[:, tb, kc * P:kc * P + P], ident)
                    end(last, "h", k, kc)

            early_slot = [0]

            def early(place):
                k0 = filled(place)
                for k_ in range(k0, k0 + dict(EARLY)[place]):
                    u, half = k_ // 2, k_ % 2
                    if k_ % 4 == 0:
                        early_slot[0] = next_panel()
                    if half == 0:
                        begin("early", u)
                    ps, slot = bank_of("early", u), early_slot[0]
                    for k in range(4 * half, 4 * half + 4):
                        at_ = slice(256 * k + P * (u % 2), 256 * k + P * (u % 2) + P)
                        last = split3(ps[:, :], (whi[:, slot, at_], wlo[:, slot, at_]),
                                      (hhi[:, k, :], hlo[:, k, :]), k == 0, k == KC - 1)
                    if half:
                        end(last, "early", u)

            h_in = (hhi, hlo)
            pe.wait_ge(s_vectors_in, 16)
            pe.wait_ge(s_constants_in, 16)
            ps = begin("vectors")
            end(t.transpose(ps[:, 0:NVEC], vrow[:, :], cst[0:NVEC, C_ID:C_ID + NVEC]), "vectors")
            for n in range(8):
                ada(n)
            transposes(0, x_norm)
            pe.wait_ge(s_h_lo, KC)
            for n in range(7):
                slot = next_panel()
                for m in range(2):
                    stationary_unit(slot, m, h_in, KC, "rw", 2 * n + m)
                late_ada()
            early("rw lora")
            pe.wait_ge(s_lora_in, 48)
            pe.wait_ge(s_rw_lora, 1)
            for c in range(4):
                ps = begin("rw w", c)
                end(mm(ps[:, :], lora_w[0:64, 0, c * P:c * P + P], lora_in[0:64, :]), "rw w", c)
            for c in range(4):
                ps = begin("rw a", c)
                end(mm(ps[:, :], lora_w[64:128, 0, c * P:c * P + P], lora_in[64:128, :]), "rw a", c)
            early("rw kk")
            pe.wait_ge(s_rw_kk2, 1)
            for c in range(4):
                ps = begin("rw kk", c)
                end(mm(ps[:, :], pair_ones, tmp[:, c, :]), "rw kk", c)
            early("rw bonus")
            pe.wait_ge(s_rw_rkk, 4)
            ps = begin("rw bonus")
            for c in range(4):
                last = mm(ps[0:8, :], cst[:, C_SEL + 8 * c:C_SEL + 8 * c + 8], cum[:, c, :], c == 0, c == 3)
            end(last, "rw bonus")
            for n in range(4):
                early(("rw sums", n))
            pe.wait_ge(s_rw_state, 1)
            for c in range(TB):
                toks = slice(c * P, c * P + P)
                for x_, src in enumerate((V, K, B)):
                    ps = begin("rw tok", c, x_)
                    for b in range(4):
                        last = t.transpose(ps[:, b * P:b * P + P], src[:, b, toks], ident)
                    end(last, "rw tok", c, x_)
                early(("rw tok", c))
                for g in range(2):
                    rows = slice(64 * g, 64 * g + 64)
                    for hl in range(4):
                        ps = begin("rw sc", c, g, hl)
                        for n, (key, query) in enumerate(((B, A), (B, R), (K, A), (K, R))):
                            last = mm(ps[:, P * n:P * n + P], key[rows, hl, toks], query[rows, hl, toks])
                        end(last, "rw sc", c, g, hl)
                    ps = begin("rw n", c, g)
                    for hl in range(4):
                        last = mm(ps[:, hl * P:hl * P + P], A[rows, hl, toks], B[rows, hl, toks])
                    end(last, "rw n", c, g)
                early(("rw x", c))

                def heads(g):
                    return [(hl, slice(hl * P, hl * P + P)) for hl in range(4)]

                for i in range(1, LEVELS):
                    for g in range(2):
                        if i == 1:
                            pe.wait_ge(s_rw_x, 2 * c + g + 1)
                        else:
                            pe.wait_ge(*freed("rw pt", c, g, i - 1))
                        ps = begin("rw t", c, g, i)
                        for hl, at_ in heads(g):
                            last = mm(ps[:, at_], SC[g][:, hl, 0:P], X[:, g, at_])
                        end(last, "rw t", c, g, i)
                    for g in range(2):
                        pe.wait_ge(*freed("rw t", c, g, i))
                        if i < LEVELS - 1:
                            ps = begin("rw p", c, g, i)
                            for hl, at_ in heads(g):
                                last = mm(ps[:, at_], XT[:, g, at_], LX[:, g, at_])
                            end(last, "rw p", c, g, i)
                        ps = begin("rw pt", c, g, i)
                        for hl, at_ in heads(g):
                            last = mm(ps[:, at_], LX[:, g, at_], XT[:, g, at_])
                        end(last, "rw pt", c, g, i)
                for g in range(2):
                    pe.wait_ge(s_rw_state, 2 * c + g if c else 1)
                    for x_ in range(3) if g == 0 else ():
                        pe.wait_ge(*freed("rw tok", c, x_))
                    ps = begin("rw r", c, g)
                    rows = slice(64 * g, 64 * g + 64)
                    for hl in range(4):
                        cols_, head = slice(64 * hl, 64 * hl + 64), 2 * hl + g
                        mm(ps[:, cols_], A[rows, hl, toks], M[rows, hl, :], True, False)
                        last = mm(ps[:, cols_], SC[g][:, hl, 256:384], tok[:, 0, 64 * head:64 * head + 64], False, True)
                    end(last, "rw r", c, g)
                early(("rw r", c))
                for g in range(2):
                    pe.wait_ge(*freed("rw pt", c, g, LEVELS - 1))
                    pe.wait_ge(*freed("rw r", c, g))
                    ps = begin("rw u", c, g)
                    for hl, at_ in heads(g):
                        last = mm(ps[:, 64 * hl:64 * hl + 64], XT[:, g, at_], rhs_u[:, g, 64 * hl:64 * hl + 64])
                    end(last, "rw u", c, g)
                early(("rw u", c))
                for g in range(2):
                    pe.wait_ge(*freed("rw u", c, g))
                    ps = begin("rw o", c, g)
                    for hl in range(4):
                        head, rows = 2 * hl + g, slice(64 * g, 64 * g + 64)
                        o = ps[rows, P * hl:P * hl + P]
                        mm(o, tok[:, 0, 64 * head:64 * head + 64], SC[g][:, hl, 384:512], True, False)
                        mm(o, U[:, g, 64 * hl:64 * hl + 64], SC[g][:, hl, 128:256], False, False)
                        last = mm(o, M[rows, hl, :], R[rows, hl, toks], False, True)
                    end(last, "rw o", c, g)
                for g in range(2) if c < TB - 1 else ():
                    ps = begin("rw m", c, g)
                    for hl in range(4):
                        head = 2 * hl + g
                        o = ps[64 * g:64 * g + 64, 64 * hl:64 * hl + 64]
                        at_ = slice(64 * head, 64 * head + 64)
                        mm(o, tok[:, 1, at_], tok[:, 0, at_], True, False)
                        last = mm(o, tok[:, 2, at_], U[:, g, 64 * hl:64 * hl + 64], False, True)
                    end(last, "rw m", c, g)
            early("rw mean")
            pe.wait_ge(*freed("rw o", TB - 1, 1))
            for c in range(4):
                ps = begin("rw mean", c)
                end(mm(ps[:, :], pair_ones, R[:, c, :]), "rw mean", c)
            for c in range(4):
                ps = begin("rw bv", c)
                end(mm(ps[:, :], cst[0:8, C_SELT + P * c:C_SELT + P * c + P], bonus[:, :]), "rw bv", c)
            early("rw var")
            pe.wait_ge(s_rw_sq, 1)
            for c in range(4):
                ps = begin("rw var", c)
                end(mm(ps[:, :], pair_ones, epi[:, c, :]), "rw var", c)
            pe.wait_ge(s_rw_lora, 2)
            for c in range(4):
                ps = begin("rw g", c)
                end(mm(ps[:, :], lora_w[:, 1, c * P:c * P + P], gate_lo[:, :]), "rw g", c)
            early("rw g")
            moving_units(h_in, [("hg v", tb) for tb in range(TB)])
            early("hg z")
            pe.wait_ge(s_hg_key, 1)
            for lev in range(LEVELS + 1):
                if lev:
                    early(("hg sc", lev))
                    pe.wait_ge(s_hg_lev, lev)
                else:
                    pe.wait_ge(s_hq_in, 16)
                q, k_ = (q_lev, k_lev) if lev else (Hq, Hk)
                for c in range(TB):
                    ps = begin("hg sc", lev, c)
                    for h in range(4):
                        last = mm(ps[:, h * P:h * P + P], k_[:, h, c * P:c * P + P], q[:, h, c * P:c * P + P])
                    end(last, "hg sc", lev, c)
            early("hg left")
            pe.wait_ge(s_hg_k_left, 1)
            for c in range(TB):
                ps = begin("hg tok", c)
                for h in range(4):
                    last = t.transpose(ps[:, h * P:h * P + P], Hk[:, h, c * P:c * P + P], ident)
                end(last, "hg tok", c)
                if c:
                    pe.wait_ge(*freed("hg s", c - 1))
                ps = begin("hg o", c)
                for h in range(4):
                    o, v_ = ps[:, h * P:h * P + P], Hv[:, c, h * P:h * P + P]
                    last = mm(o, v_, ST[:, c, h, :], True, c == 0)
                    if c:
                        last = mm(o, Hs[:, h, :], Hq[:, h, c * P:c * P + P], False, True)
                end(last, "hg o", c)
                if c < TB - 1:
                    pe.wait_ge(*freed("hg tok", c))
                    ps = begin("hg s", c)
                    for h in range(4):
                        last = mm(ps[:, h * P:h * P + P], k_tok[:, h * P:h * P + P], Hv[:, c, h * P:h * P + P])
                    end(last, "hg s", c)
            early("hg ss")
            pe.wait_ge(s_hg_sq, 1)
            for h in range(4):
                ps = begin("hg ss", h)
                end(mm(ps[:, :], ones, k_lev[:, h, :]), "hg ss", h)
            def rotated(ns):
                for n in ns:
                    pe.wait_ge(s_qk_in, 16)
                    ps = begin("da rot", n)
                    end(mm(ps[:, :], cst[:, C_PERM:C_PERM + P], qk[:, n // 4, n % 4, :]), "da rot", n)

            moving_units(h_in, [("da v", tb) for tb in range(TB)], between=lambda: rotated(range(4)))
            rotated(range(4, 8))
            pe.wait_ge(s_roped, 8)
            for tb in range(TB):
                pe.wait_ge(*freed("da v", tb))

            def scores(t_):
                h, i = divmod(t_, TB)
                n = (i + 1) * P
                for m in range(2):
                    rows = slice(64 * m, 64 * m + 64)
                    ps = begin("da s", t_, m)
                    mm(ps[:, 0:n], qk[rows, 0, h, i * P:i * P + P], qk[rows, 1, h, 0:n], True, False)
                    end(mm(ps[:, n - P:n], cst[rows, C_MA:C_MA + P], cst[rows, C_MB:C_MB + P], False, True),
                        "da s", t_, m)

            scores(0)
            scores(1)
            for t_ in range(4 * TB + 3):
                if t_ >= 6 and t_ % 4 == 2:
                    pe.wait_ge(s_da_sq, (t_ - 6) // 4 + 1)
                    ps = begin("da ss", (t_ - 6) // 4)
                    end(mm(ps[:, :], ones, att2[:, :]), "da ss", (t_ - 6) // 4)
                if t_ + 2 < 4 * TB:
                    scores(t_ + 2)
                if t_ < 4 * TB:
                    pe.wait_ge(s_da_p, t_ + 1)
                    ps = begin("da pt", t_)
                    for j in range(t_ % TB + 1):
                        last = t.transpose(ps[:, j * P:j * P + P], prob[:, t_ % 3, 0, j * P:j * P + P], ident)
                    end(last, "da pt", t_)
                if 1 <= t_ <= 4 * TB:
                    h, i = divmod(t_ - 1, TB)
                    pe.wait_ge(*freed("da pt", t_ - 1))
                    if i == 0:
                        po = begin("da o", h)
                    for j in range(i + 1):
                        last = mm(po[:, i * P:i * P + P], v_tok[:, j, h * P:h * P + P],
                                  probT[(t_ - 1) % 2][:, j * P:j * P + P], j == 0, j == i)
                    if i == TB - 1:
                        end(last, "da o", h)
            branches = ((oa_hi, oa_lo), (ob_hi, ob_lo), (oc_hi, oc_lo))
            pe.wait_ge(s_da_lo, 4)
            for j in range(4):
                for g in range(3):
                    slot = next_panel()
                    for m in range(2):
                        stationary_unit(slot, m, branches[g], 4, "branch", j, g, m)
                    if (j, g) in ADA_AT_BRANCH:
                        late_ada()
            pe.wait_ge(s_merged, KC)
            for n in range(2):
                moving_units((mg_hi, mg_lo), [("out", n, tb) for tb in range(TB)])
            transposes(1, x1_norm)
            pe.wait_ge(s_h_lo, 2 * KC)
            for j in range(FFN // 256):
                for which in range(2):
                    slot = next_panel()
                    for m in range(2):
                        stationary_unit(slot, m, h_in, KC, "ffn", j, which, m)
                    if which == 0 and j < 4:
                        late_ada()
            tiles = [[begin("down", tb, n) for n in range(2)] for tb in range(TB)]
            for j in range(FFN // 256):
                slot = next_panel()
                for k in range(2):
                    kk = 2 * j + k
                    pe.wait_ge(s_d_lo, kk + 1)
                    for tb in range(TB):
                        toks = slice(tb * P, tb * P + P)
                        for n in range(2):
                            at_ = slice(D * k + T * n, D * k + T * n + T)
                            last = split3(tiles[tb][n][:, :], (d_hi[:, k, toks], d_lo[:, k, toks]),
                                          (whi[:, slot, at_], wlo[:, slot, at_]), kk == 0, kk == FFN // P - 1)
                            if kk == FFN // P - 1:
                                end(last, "down", tb, n)
                    if kk < FFN // P - 1:
                        last.then_inc(s_down_k, 1)


def constants():
    import numpy as np
    c = np.zeros((P, NCONST), np.float32)
    i = np.arange(P)
    c[:, C_ID:C_ID + P] = np.eye(P)
    for p in range(P):
        if p % 64 < 32:
            c[p + 32, C_PERM + p] = -1.0
        else:
            c[p - 32, C_PERM + p] = 1.0
    c[:, C_ONES:C_ONES + P] = 1.0
    c[:, C_BLK:C_BLK + P] = i[:, None] // 64 == i[None, :] // 64
    strict, incl = i[:, None] < i[None, :], i[:, None] <= i[None, :]
    for n, part in enumerate((-1.0 * strict, incl, strict, incl)):
        c[:, C_MASK + n * P:C_MASK + n * P + P] = part
    for row in (0, 64):
        c[row, C_MA:C_MA + 64] = 1.0
        c[row, C_MB + 64:C_MB + P] = -2.0 ** 100
    c[:, C_FREQ] = np.float32(10000.0) ** (-(2 * (i % 32)).astype(np.float32) / np.float32(64))
    c[:, C_EPS], c[:, C_GEPS], c[:, C_HPI] = EPS, GN_EPS, TWO_PI / 4
    for b in range(4):
        c[:, C_SEL + 8 * b + 2 * b] = i < 64
        c[:, C_SEL + 8 * b + 2 * b + 1] = i >= 64
        c[2 * b, C_SELT + P * b:C_SELT + P * b + 64] = 1.0
        c[2 * b + 1, C_SELT + P * b + 64:C_SELT + P * b + P] = 1.0
    lev = np.zeros((P, 2 * LEVELS + 1, P), np.float32)
    for n in range(LEVELS):
        s = 1 << n
        same = i[:, None] // (2 * s) == i[None, :] // (2 * s)
        upper = same & (i[:, None] % (2 * s) < s) & (i[None, :] % (2 * s) >= s)
        lev[:, 2 * n, :], lev[:, 2 * n + 1, :] = upper.T, upper
    lev[:, 2 * LEVELS, :] = np.eye(P)
    return c, lev.reshape(P, -1)


def kernel(**inputs):
    import numpy as np
    import concourse.bacc as bacc
    from concourse.bass_utils import run_bass_kernel_spmd

    a = {k: np.ascontiguousarray(v) for k, v in inputs.items()}
    names = ("rw_mu", "rw_w0", "rw_a0", "rw_k_k", "rw_k_a", "rw_r_k", "rw_gn_w", "rw_gn_b",
             "hg_norm_w", "da_subln_w", "norm_mix_w", "norm_ffn_w", "c", "ada_b")
    vecs = np.concatenate([a[n].reshape(-1, P) for n in names])
    consts, levels = constants()
    arrays = {
        "x": a["x"][0], "ada_w": a["ada_w"][0], "w_in": a["w_in"][0],
        "w_a": a["w_branch_a"][0], "w_b": a["w_branch_b"][0], "w_c": a["w_branch_c"][0],
        "w_out": a["w_out"][0], "f_in": a["ffn_w_in"][0], "f_out": a["ffn_w_out"][0],
        "w2": a["rw_w2"][0], "a2": a["rw_a2"][0], "g2": a["rw_g2"][0],
        "vecs": vecs, "consts": consts, "levels": levels,
        "gate_b": a["ada_b"][0], "final_w": a["final_norm_w"], "lam": a["da_lambda"].reshape(-1),
        "positions": a["positions"][0],
    }
    nc = bacc.Bacc("TRN2", target_bir_lowering=False, num_devices=1)
    aps = [nc.dram_tensor(f"in_{k}", v.shape, mybir.dt.from_np(v.dtype), kind="ExternalInput").ap()
           for k, v in arrays.items()]
    aps.append(nc.dram_tensor("out_x", (T, D), F32, kind="ExternalOutput").ap())
    build(nc, *aps)
    r = run_bass_kernel_spmd(nc, [{f"in_{k}": v for k, v in arrays.items()}], core_ids=[0])
    return r.results[0]["out_x"].reshape(1, T, D)
```

```python
from contextlib import ExitStack

import concourse.bass as bass
from concourse import mybir

F32 = mybir.dt.float32
F32R = mybir.dt.float32r
U8 = mybir.dt.uint8
I32 = mybir.dt.int32
ALU = mybir.AluOpType
ACT = mybir.ActivationFunctionType
AX_X = mybir.AxisListType.X

P = 128
D = 1024
T = 512
KC = D // P
TB = T // P
FFN = 2816
EPS = 1e-6
GN_EPS = 64e-5
DECAY = 0.6065306597126334
LAM_INIT = 0.2
TWO_PI = 6.283185307179586
TURN = (6.28125, 0.0019350051879882812, 3.0198680e-07)
ROUND = 12582912.0
LEVELS = 7

DA_Q, DA_K, DA_V, HG_F, HG_I, HG_Q, HG_G, RW_U, GATES = 0, 512, 1024, 1536, 2048, 2560, 3072, 3584, 5376

V_MU, V_W0, V_A0, V_KK, V_KA, V_RK, V_GNW, V_GNB, V_HGN, V_SUB, V_NM, V_NF, V_C, V_ADAB = (
    0, 14, 18, 22, 26, 30, 34, 38, 42, 43, 44, 52, 60, 68)
NVEC = 116

C_ID, C_PERM, C_ONES, C_BLK, C_MASK, C_MA, C_MB, C_LOW = 0, 128, 256, 384, 512, 1024, 1152, 1280
C_FREQ, C_EPS, C_GEPS, C_HPI, C_SEL, C_SELT = 1408, 1409, 1410, 1411, 1412, 1444
NCONST = C_SELT + 512

EARLY = [
    [("rw lora", 2), ("rw kk", 2), ("rw bonus", 4)] + [(("rw sums", n), 4) for n in range(5)]
    + [((what, c), n) for c in range(TB) for what, n in (("rw tok", 1), ("rw x", 2), ("rw r", 1), ("rw u", 2))]
    + [("rw mean", 2), ("rw var", 2), ("rw g", 4), ("rw past", 4), ("rw end", 0)],
    [(("hg z", 0), 4), (("hg z", 1), 4)] + [(("hg sc", lev), 2) for lev in range(1, LEVELS + 1)]
    + [("hg past", 2), ("hg left", 2)] + [(("hg tok", c), 1) for c in range(TB)] + [("hg ss", 2), ("hg end", 0)],
]
E_Z, E_HQ, E_HG, E_QK, E_GATES, E_RW, N_EARLY = 0, 4, 8, 12, 20, 44, 52


def early_parts():
    parts = [(u // 2, u, 4 * half, "h", half == 0, half == 1) for u in range(E_RW) for half in range(2)]
    return parts + [(u // 2, u, 0, "rw", True, True) for u in range(E_RW, N_EARLY)]


def stretch(place):
    total = 0
    for number, places in enumerate(EARLY):
        end = total + sum(n for _, n in places)
        for name, n in places:
            if name == place:
                return number, total, end
            total += n
    raise KeyError(place)


def panels_before(part):
    parts = early_parts()
    return parts[part][0] if part < len(parts) else N_EARLY // 2


ADA = (0, 4, 1, 5, 2, 6, 3, 7) + tuple(range(12, 20)) + tuple(range(8, 12)) + tuple(range(20, 24))
RAW = 3
RING = 2
BANKS = 8


def panel_stream(w_in, ada_w, wbr, w_out, f_in, f_out):
    def stationary(w, col, kc=KC):
        return w.rearrange("(k p) n -> p k n", p=P)[:, 0:kc, col:col + 256]

    def moving(w, half, col):
        return w.rearrange("(k p) n -> p k n", p=P)[:, 4 * half:4 * half + 4, col:col + 512]

    out = [("ada", stationary(ada_w, 256 * n)) for n in ADA[:8]]
    late = [("ada", stationary(ada_w, 256 * n)) for n in ADA[8:]]
    for n in range(7):
        out += [("w", stationary(w_in, RW_U + 256 * n)), late.pop(0)]
    early = [("w", stationary(w_in, base + 256 * n)) for base in (HG_F, HG_Q, HG_G) for n in range(2)]
    early += [("w", stationary(w_in, DA_Q + 256 * n)) for n in range(4)]
    early += [("w", stationary(w_in, GATES + D * g + 256 * j)) for j in range(4) for g in range(3)]
    early += [("w", stationary(wbr[2], 256 * j, 4)) for j in range(4)]
    at_hg = panels_before(stretch("rw end")[1])
    out += early[:at_hg]
    out += [("w", moving(w_in, half, HG_I)) for half in range(2)]
    out += early[at_hg:]
    out += [("w", moving(w_in, half, DA_V)) for half in range(2)]
    out += [late.pop(0) for _ in range(5)]
    out += [("w", stationary(w, 256 * j, 4)) for j in range(4) for w in wbr[:2]]
    out += [("w", moving(w_out, half, 512 * n)) for n in range(2) for half in range(2)]
    for j in range(FFN // 256):
        out.append(("w", stationary(f_in, 256 * j)))
        if late:
            out.append(late.pop(0))
        out.append(("w", stationary(f_in, FFN + 256 * j)))
    fo = f_out.rearrange("(k p) n -> p k n", p=P)
    out += [("w", fo[:, 2 * j:2 * j + 2, :]) for j in range(FFN // 256)]
    assert not late
    return out


class Banks:

    def __init__(self):
        self.of, self.count, self.next, self.used = {}, [0] * BANKS, 0, BANKS

    def rotate(self, n):
        self.used, self.next = n, 0

    def add(self, *name, bank=None):
        if bank is None:
            bank = self.next
            self.next = (bank + 1) % self.used
        self.of[name] = (bank, self.count[bank])
        self.count[bank] += 1


def bank_plan():
    b = Banks()
    b.add("vectors")
    for q in range(4):
        b.add("ada", q)
        b.add("ada", 4 + q)
        b.add("h", 0, 2 * q)
        b.add("h", 0, 2 * q + 1)
    late = list(ADA[8:])
    parts = early_parts()
    stretch_end = [0] + [stretch(place)[1] for place in ("rw end", "hg end")]

    def early(number):
        for part in parts[stretch_end[number]:stretch_end[number + 1]]:
            if part[4]:
                b.add("early", part[1], bank=6 + part[1] % 2)

    def late_ada(bank=None):
        if late:
            b.add("ada", late.pop(0), bank=bank)

    for n in range(7):
        b.add("rw", 2 * n)
        b.add("rw", 2 * n + 1)
        late_ada()
    early(0)
    b.rotate(6)
    for what in ("rw w", "rw a", "rw kk"):
        for c in range(4):
            b.add(what, c)
    b.add("rw bonus")
    for c in range(TB):
        for x in range(3):
            b.add("rw tok", c, x)
        for g in range(2):
            for hl in range(4):
                b.add("rw sc", c, g, hl)
            b.add("rw n", c, g)
        for i in range(1, LEVELS):
            for g in range(2):
                b.add("rw t", c, g, i)
            for g in range(2):
                if i < LEVELS - 1:
                    b.add("rw p", c, g, i)
                b.add("rw pt", c, g, i)
        for what in ("rw r", "rw u", "rw o") + (("rw m",) if c < TB - 1 else ()):
            for g in range(2):
                b.add(what, c, g)
    b.rotate(6)
    for what in ("rw mean", "rw bv", "rw var", "rw g"):
        for c in range(4):
            b.add(what, c)
    for tb in range(TB):
        b.add("hg v", tb, bank=4 + tb)
    early(1)
    b.rotate(6)
    for lev in range(LEVELS + 1):
        for c in range(TB):
            b.add("hg sc", lev, c)
    for c in range(TB):
        b.add("hg tok", c)
        b.add("hg o", c)
        if c < TB - 1:
            b.add("hg s", c)
    for h in range(4):
        b.add("hg ss", h)
    b.rotate(8)
    for tb in range(TB):
        b.add("da v", tb)
    for n in range(8):
        b.add("da rot", n)
    late_ada()
    b.rotate(4)
    for t in range(-2, 4 * TB + 3):
        if t >= 6 and t % 4 == 2:
            b.add("da ss", (t - 6) // 4, bank=5)
        if t + 2 < 4 * TB:
            for m in range(2):
                b.add("da s", t + 2, m)
        if t in range(3, 4 * TB, 4):
            late_ada(bank=5)
        if 0 <= t < 4 * TB:
            b.add("da pt", t, bank=4)
    for h in range(4):
        b.add("da o", h, bank=6 + h % 2)
    b.rotate(8)
    for j in range(4):
        for g in range(2):
            for m in range(2):
                b.add("branch", j, g, m)
    for n in range(2):
        for tb in range(TB):
            b.add("out", n, tb)
    for kc in range(KC):
        b.add("h", 1, kc)
    for j in range(FFN // 256):
        for which in range(2):
            for m in range(2):
                b.add("ffn", j, which, m)
            if which == 0:
                late_ada()
    for tb in range(TB):
        for n in range(2):
            b.add("down", tb, n)
    assert not late
    return b


def panel_ends():
    ends = [("bank", ("rw", 2 * n + 1)) for n in range(7)]
    early = [("bank", ("early", 2 * q + 1)) for q in range(N_EARLY // 2)]
    at_hg = panels_before(stretch("rw end")[1])
    ends += early[:at_hg] + [("panel used", 1), ("bank", ("hg v", TB - 1))]
    ends += early[at_hg:] + [("panel used", 2), ("bank", ("da v", TB - 1))]
    ends += [("bank", ("branch", j, g, 1)) for j in range(4) for g in range(2)]
    for n in range(2):
        ends += [("panel used", 3 + n), ("bank", ("out", n, TB - 1))]
    for j in range(FFN // 256):
        ends += [("bank", ("ffn", j, which, 1)) for which in range(2)]
    ends += [("down k", 2 * j + 2) for j in range(FFN // 256)]
    return ends


def build(nc, x, ada_w, w_in, wba, wbb, wbc, w_out, f_in, f_out, w2, a2, g2,
          vecs, consts, levels, gate_b, final_w, lam, positions, out):
    panels = panel_stream(w_in, ada_w, (wba, wbb, wbc), w_out, f_in, f_out)
    plan = bank_plan()
    with ExitStack() as ctx:
        def sb(name, shape, dt=F32):
            return ctx.enter_context(nc.sbuf_tensor(name, shape, dt))

        raw = sb("raw", [P, RAW, 2048])
        whi = sb("whi", [P, RING, 2048], F32R)
        wlo = sb("wlo", [P, RING, 2048], F32R)
        hhi = sb("hhi", [P, KC, T], F32R)
        hlo = sb("hlo", [P, KC, T], F32R)
        cst = sb("cst", [P, NCONST])
        lev_mask = sb("lev_mask", [P, 2 * LEVELS + 1, P], U8)
        vrow = sb("vrow", [NVEC, P])
        vc = sb("vc", [P, NVEC])
        ca = sb("ca", [P, KC])
        small = sb("small", [P, 160])
        ada_cols = sb("ada_cols", [P, 48])
        gmul = sb("gmul", [P, 2, KC])
        gate_row = sb("gate_row", [P, 2, D])
        ada_acc = sb("ada_acc", [P, 2, 2, 256])
        stage = gate_row[:, 1, :].rearrange("p (s t) -> p s t", s=2)
        early_out = nc.dram_tensor("early_out", (N_EARLY, P, T), F32, kind="Internal").ap()

        base = -(-nc.sbuf_base // 64) * 64
        size = (nc.sbuf_usable_end - base) // 64 * 64 - 64
        sb("arena_fence", [P, size // 4 - 16])

        def at(name, kb, shape, dt=F32):
            n = 2 if dt == U8 else 4
            for extent in shape[1:]:
                n *= extent
            assert kb * 1024 + n <= size, (name, kb + n / 1024, size / 1024)
            return nc.alloc_sbuf_tensor_at(name, shape, dt, offset=base + kb * 1024)

        x_in = at("x_in", 0, [P, TB, D])
        x_norm = at("x_norm", 16, [P, TB, D])
        h_tmp = at("h_tmp", 32, [P, 2, T])
        lev_f32 = at("lev_f32", 40, [P, 2 * LEVELS + 1, P])
        oc_hi = at("oc_hi", 0, [P, 4, T], F32R)
        oc_lo = at("oc_lo", 8, [P, 4, T], F32R)
        R = at("R", 16, [P, 4, T])
        K = at("K", 24, [P, 4, T])
        V = at("V", 32, [P, 4, T])
        A = at("A", 40, [P, 4, T])
        B = at("B", 48, [P, 4, T])
        gate_lo = at("gate_lo", 56, [P, T])
        bonus = at("bonus", 58, [8, T])
        lora_w = at("lora_w", 60, [P, 2, T])
        lora_in = at("lora_in", 64, [P, T])
        u_prev = at("u_prev", 66, [P, 2, T + 1])
        decay = at("decay", 71, [P, 4, T])
        cum = at("cum", 79, [P, 4, T])
        tmp = at("tmp", 87, [P, 4, T])
        tok = at("tok", 72, [P, 3, T])
        SC = [at("sc0", 78, [P, 4, T]), at("sc1", 0, [P, 4, T])]
        X = at("X", 8, [P, 2, T])
        XT = at("XT", 12, [P, 2, T])
        LX = at("LX", 86, [P, 2, T])
        rhs_u = at("rhs_u", 90, [P, 2, 256])
        U = at("U", 92, [P, 2, 256])
        M = at("M", 94, [P, 4, 64])
        epi = at("epi", 64, [P, 4, T])
        epi2 = at("epi2", 72, [P, 4, T])
        ob_hi = at("ob_hi", 16, [P, 4, T], F32R)
        ob_lo = at("ob_lo", 24, [P, 4, T], F32R)
        Z = at("Z", 40, [P, 4, T])
        Hb = at("Hb", 24, [P, 4, T])
        Hq = at("Hq", 32, [P, 4, T])
        Hg = at("Hg", 16, [P, 4, T])
        Hk = at("Hk", 48, [P, 4, T])
        Hv = at("Hv", 56, [P, TB, T])
        q_lev = at("q_lev", 64, [P, 4, T])
        k_lev = at("k_lev", 72, [P, 4, T])
        ST = at("ST", 80, [P, TB, 4, P])
        Hs = at("Hs", 88, [P, 4, P])
        k_tok = at("k_tok", 90, [P, T])
        oa_hi = at("oa_hi", 32, [P, 4, T], F32R)
        oa_lo = at("oa_lo", 40, [P, 4, T], F32R)
        qk = at("qk", 48, [P, 2, 4, T])
        v_tok = at("v_tok", 64, [P, TB, T])
        cos_sin = gate_row[:, 0, :].rearrange("p (s t) -> p s t", s=2)
        rot = at("rot", 76, [P, 4, T])
        prob = at("prob", 72, [P, 3, 2, T])
        probT = [at("probT0", 84, [P, T]), at("probT1", 90, [P, T])]
        turns = at("turns", 70, [P, T])
        pos_i = at("pos_i", 70, [P, T], I32)
        ang = at("ang", 64, [P, 3, T])
        att = at("att", 86, [P, T])
        att2 = at("att2", 88, [P, T])
        lam_in = at("lam_in", 95, [P, 256])
        sg = [at("sg0", 0, [P, 3, 2, T]), at("sg1", 48, [P, 3, 2, T])]
        br = [at(f"br{j}", (12, 72, 88, 12)[j], [P, 2, T]) for j in range(4)]
        mg_hi = at("mg_hi", 60, [P, KC, T], F32R)
        mg_lo = at("mg_lo", 76, [P, KC, T], F32R)
        mg = at("mg", 92, [P, 2, T])
        x1 = at("x1", 0, [P, TB, D])
        x1_norm = at("x1_norm", 16, [P, TB, D])
        h_tmp2 = at("h_tmp2", 32, [P, 2, T])
        hid = at("hid", 16, [P, FFN // P, T])
        d_hi = at("d_hi", 60, [P, 4, T], F32R)
        d_lo = at("d_lo", 68, [P, 4, T], F32R)
        f_tmp = at("f_tmp", 76, [P, 2, T])
        final_row = at("final_row", 92, [P, D])
        y = at("y", 16, [P, TB, D])

        psum = [ctx.enter_context(nc.psum_tensor(f"bank{b}", [P, T], F32)) for b in range(BANKS)]

        bank_full = [ctx.enter_context(nc.semaphore(f"bank{b}_full")) for b in range(BANKS)]
        bank_free = [ctx.enter_context(nc.semaphore(f"bank{b}_free")) for b in range(BANKS)]
        raw_loaded = [ctx.enter_context(nc.semaphore(f"raw{s}_loaded")) for s in range(RAW)]
        def sem(name):
            return ctx.enter_context(nc.semaphore(name))

        s_act_step = sem("act_step")
        s_ada_step = sem("ada_step")
        s_angles = sem("angles")
        s_c_act = sem("c_act")
        s_constants_in = sem("constants_in")
        s_cos_sin = sem("cos_sin")
        s_d_hi = sem("d_hi")
        s_d_lo = sem("d_lo")
        s_da_hi = sem("da_hi")
        s_da_lo = sem("da_lo")
        s_da_out = sem("da_out")
        s_da_p = sem("da_p")
        s_da_rstd = sem("da_rstd")
        s_da_sq = sem("da_sq")
        s_down_k = sem("down_k")
        s_dve_step = sem("dve_step")
        s_ffn_sig = sem("ffn_sig")
        s_rms = sem("rms")
        s_rstd = sem("rstd")
        s_final_weight_in = sem("final_weight_in")
        s_gate_bias_in = sem("gate_bias_in")
        s_gmul = sem("gmul")
        s_h_hi = sem("h_hi")
        s_h_lo = sem("h_lo")
        s_hg_neg_abs = sem("hg_neg_abs")
        s_hg_e_b = sem("hg_e_b")
        s_hg_e_last = sem("hg_e_last")
        s_hg_e_left = sem("hg_e_left")
        s_hg_e_rel = sem("hg_e_rel")
        s_hg_hi = sem("hg_hi")
        s_hg_k_left = sem("hg_k_left")
        s_hg_key = sem("hg_key")
        s_hg_last = sem("hg_last")
        s_hg_left = sem("hg_left")
        s_hg_lev = sem("hg_lev")
        s_hg_ln = sem("hg_ln")
        s_hg_ls_less_z = sem("hg_ls_less_z")
        s_hg_out = sem("hg_out")
        s_hg_rel = sem("hg_rel")
        s_hg_rstd = sem("hg_rstd")
        s_hg_split = sem("hg_split")
        s_hg_sq = sem("hg_sq")
        s_lam_dot = sem("lam_dot")
        s_lam_exp = sem("lam_exp")
        s_lambda_in = sem("lambda_in")
        s_lora_in = sem("lora_in")
        s_masks = sem("masks")
        s_masks_in = sem("masks_in")
        s_max = sem("max")
        s_merged = sem("merged")
        s_mg_hi = sem("mg_hi")
        s_mg_sum = sem("mg_sum")
        s_normed = sem("normed")
        s_panel_hi = sem("panel_hi")
        s_panel_taken = sem("panel_taken")
        s_panel_used = sem("panel_used")
        s_positions_in = sem("positions_in")
        s_roped = sem("roped")
        s_rw_e_a = sem("rw_e_a")
        s_rw_e_bk = sem("rw_e_bk")
        s_rw_e_r = sem("rw_e_r")
        s_rw_factor = sem("rw_factor")
        s_rw_hi = sem("rw_hi")
        s_rw_k_k = sem("rw_k_k")
        s_rw_kk2 = sem("rw_kk2")
        s_rw_lora = sem("rw_lora")
        s_rw_norm = sem("rw_norm")
        s_rw_prev = sem("rw_prev")
        s_rw_rkk = sem("rw_rkk")
        s_rw_rstd = sem("rw_rstd")
        s_rw_split = sem("rw_split")
        s_rw_sq = sem("rw_sq")
        s_rw_state = sem("rw_state")
        s_rw_sums = sem("rw_sums")
        s_rw_x = sem("rw_x")
        s_stored = sem("stored")
        s_spilled = [sem("spilled0"), sem("spilled1")]
        s_z_in, s_hq_in, s_hg_in, s_qk_in = sem("z_in"), sem("hq_in"), sem("hg_in"), sem("qk_in")
        s_hg_silu = sem("hg_silu")
        s_gates_in = [sem("gates_in0"), sem("gates_in1")]
        s_branch_in = [sem(f"branch_in{j}") for j in range(4)]
        s_gated = sem("gated")
        s_u_prev_zero = sem("u_prev_zero")
        s_vectors_in = sem("vectors_in")
        s_x_again = sem("x_again")
        s_x_in = [sem(f"x_in{tb}") for tb in range(TB)]
        s_x1_ready = sem("x1_ready")
        s_x2_ready = sem("x2_ready")
        s_y_ready = sem("y_ready")

        counts = {}

        def up(semaphore):
            counts[semaphore.name] = counts.get(semaphore.name, 0) + 1
            return counts[semaphore.name]

        def bank_of(*use):
            return psum[plan.of[use][0]]

        def full(*use):
            bank, k = plan.of[use]
            return bank_full[bank], k + 1

        def free_sem(*use):
            return bank_free[plan.of[use][0]]

        def freed(*use):
            bank, k = plan.of[use]
            return bank_free[bank], k + 1

        weights = [n for n, (kind, _) in enumerate(panels) if kind == "w"]
        ends = panel_ends()
        assert len(ends) == len(weights)

        def slot_released(eng, m):
            kind, what = ends[m]
            if kind == "bank":
                eng.wait_ge(*full(*what))
            else:
                eng.wait_ge({"panel used": s_panel_used, "down k": s_down_k}[kind], what)

        def ada_slot(n):
            return ADA.index(n) % 2

        def loaded(eng, n):
            eng.wait_ge(raw_loaded[n % RAW], 16 * (n // RAW + 1))
            a, cols = panels[n][1].shape[1:]
            return raw[:, n % RAW, 0:a * cols]

        def spilled(u):
            return s_spilled[u % 2], 16 * (u // 2 + 1)

        def split_by(place):
            number, part, end_ = stretch(place)
            return 8 + 2 * number + min(panels_before(part) + 1, panels_before(end_))

        def bcast(ap, *shape):
            return ap.to_broadcast(list(shape))

        def h_ring(k, kc):
            return (h_tmp2 if k else h_tmp)[:, kc % 2, :]

        def by_act(k, kc):
            return k == 0 or kc % 2 == 0

        def blocks(tile):
            return tile[:, :, :].rearrange("p a (b t) -> p (a b) t", t=P)

        ident = cst[:, C_ID:C_ID + P]
        ones = cst[:, C_ONES:C_ONES + P]
        pair_ones = cst[:, C_BLK:C_BLK + P]
        SS, RSTD, OM_MU, OM_KA, BREF, BLAST, FAC, HLAST, MX, RS, LR, NLAM, SUBW, NB, SUM = (
            0, 4, 8, 22, 26, 42, 58, 74, 90, 96, 98, 100, 101, 104, 110)

        def col(k, n=1):
            return small[:, k:k + n]

        def blk16(k):
            return small[:, k:k + 16]

        block = ctx.enter_context(nc.Block())

        @block.sync
        def _(sp):
            sp.dma_start(vrow[:, :], vecs).then_inc(s_vectors_in, 16)
            sp.dma_start(cst[:, :], consts).then_inc(s_constants_in, 16)
            for n, (kind, src) in enumerate(panels):
                if n >= RAW:
                    sp.wait_ge(s_panel_taken, n - RAW + 1)
                a, cols = src.shape[1:]
                dst = raw[:, n % RAW, 0:a * cols].rearrange("p (a n) -> p a n", a=a)
                sp.dma_start(dst, src).then_inc(raw_loaded[n % RAW], 16)

        @block.gpsimd
        def _(pool):
            for tb in range(TB):
                pool.dma_start(x_in[:, tb, :], x[tb * P:tb * P + P, :]).then_inc(s_x_in[tb], 16)
            pool.wait_ge(s_panel_taken, 7)
            pool.dma_start(lev_f32[:, :, :], levels.rearrange("p (l c) -> p l c", c=P)).then_inc(s_masks_in, 16)

            def gate_bias(g):
                pool.dma_start(gate_row[:, g, :], gate_b[3 * D * g + 2 * D:3 * D * g + 3 * D].rearrange(
                    "(a n) -> a n", a=1).to_broadcast([P, D])).then_inc(s_gate_bias_in, 16)

            pool.dma_start(lora_w[0:64, 0, :], w2).then_inc(s_lora_in, 16)
            pool.dma_start(lora_w[64:128, 0, :], a2).then_inc(s_lora_in, 16)
            pool.dma_start(lora_w[:, 1, :], g2).then_inc(s_lora_in, 16)
            pool.wait_ge(s_masks_in, 16)
            nc.gpsimd.tensor_copy(lev_mask[:, :, :], lev_f32[:, :, :]).then_inc(s_masks, 1)
            pool.wait_ge(s_masks, up(s_masks))
            pool.wait_ge(s_rw_state, 1)
            pool.dma_start(pos_i[:, :], positions.rearrange("(a n) -> a n", a=1).to_broadcast([P, T])
                           ).then_inc(s_positions_in, 16)
            pool.dma_start(lam_in[:, :], lam.rearrange("(a n) -> a n", a=1).to_broadcast([P, 256])
                           ).then_inc(s_lambda_in, 16)

            def reload(dst, u, n, arrived):
                pool.wait_ge(*spilled(u + n - 2))
                pool.wait_ge(*spilled(u + n - 1))
                pool.dma_start(dst, early_out[u:u + n].rearrange("u p t -> p u t")).then_inc(arrived, 16)

            pool.wait_ge(*full("rw o", TB - 1, 1))
            reload(Z[:, :, :], E_Z, 4, s_z_in)
            pool.wait_ge(*freed("rw bv", 3))
            reload(Hq[:, :, :], E_HQ, 4, s_hq_in)
            pool.wait_ge(*freed("rw g", 3))
            reload(Hg[:, :, :], E_HG, 4, s_hg_in)
            pool.wait_ge(s_hg_k_left, 1)
            pool.wait_ge(*full("hg o", TB - 1))
            reload(qk[:, :, :, :].rearrange("p a h t -> p (a h) t"), E_QK, 8, s_qk_in)
            pool.wait_ge(s_roped, 8)
            gate_bias(0)
            pool.wait_ge(*full("early", N_EARLY - 1))
            for j in range(4):
                if j == 1:
                    pool.wait_ge(s_da_lo, 4)
                elif j >= 2:
                    pool.wait_ge(s_mg_sum, 2 * j - 2)
                reload(br[j][:, :, :], E_RW + 2 * j, 2, s_branch_in[j])
                reload(sg[j % 2][:, :, :, :].rearrange("p g m t -> p (g m) t"), E_GATES + 6 * j, 6, s_gates_in[j % 2])
            gate_bias(1)
            pool.wait_ge(s_mg_sum, 8)
            pool.dma_start(x1[:, :, :], x.rearrange("(b p) d -> p b d", p=P)).then_inc(s_x_again, 16)
            pool.wait_ge(s_x1_ready, 2 * TB)
            pool.dma_start(final_row[:, :], final_w.rearrange("(a n) -> a n", a=1).to_broadcast([P, D])
                           ).then_inc(s_final_weight_in, 16)
            for tb in range(TB):
                pool.wait_ge(s_y_ready, tb + 1)
                pool.dma_start(out[tb * P:tb * P + P, :], y[:, tb, :]).then_inc(s_stored, 16)
            pool.wait_ge(s_stored, 16 * TB)

        @block.scalar
        def _(act):
            do = nc.scalar.activation
            split_next = [0]

            def split_hi():
                m = split_next[0]
                split_next[0] += 1
                if m >= len(weights):
                    return
                src = loaded(act, weights[m])
                if m >= RING:
                    slot_released(act, m - RING)
                do(whi[:, m % RING, 0:src.shape[1]], src, ACT.Copy).then_inc(s_panel_hi, 1)
                act.wait_ge(s_panel_hi, up(s_panel_hi))

            evicted = [0]

            def early(place):
                while split_next[0] < split_by(place):
                    split_hi()
                for part in early_parts()[:stretch(place)[1]]:
                    u = evicted[0]
                    if part[1] != u or not part[5]:
                        continue
                    evicted[0] += 1
                    act.wait_ge(*full("early", u))
                    if u >= 2:
                        act.wait_ge(*spilled(u - 2))
                    do(stage[:, u % 2, :], bank_of("early", u)[:, :], ACT.Copy).then_inc(free_sem("early", u), 1)
                    act.wait_ge(*freed("early", u))
                    act.dma_start(early_out[u], stage[:, u % 2, :]).then_inc(s_spilled[u % 2], 16)

            def norm(k, src, dst):
                for tb in range(TB):
                    if k:
                        act.wait_ge(s_x1_ready, TB + tb + 1)
                    else:
                        act.wait_ge(s_x_in[tb], 16)
                    do(dst[:, tb, :], src[:, tb, :], ACT.Square, accum_out=col(SS + tb)).then_inc(s_act_step, 1)
                    act.wait_ge(s_act_step, up(s_act_step))
                    do(col(RSTD + tb), col(SS + tb), ACT.Sqrt, scale=1.0 / D, bias=cst[:, C_EPS:C_EPS + 1])\
                        .then_inc(s_rms, 1)
                    act.wait_ge(s_rms, up(s_rms))
                    act.wait_ge(s_rstd, TB * k + tb + 1)
                    do(dst[:, tb, :], src[:, tb, :], ACT.Copy, scale=col(RSTD + tb)).then_inc(s_normed, 1)
                    act.wait_ge(s_normed, up(s_normed))
                for kc in range(KC):
                    if by_act(k, kc):
                        act.wait_ge(s_gmul, kc // 2 + 1 if k == 0 else 5)
                        act.wait_ge(*full("h", k, kc))
                        if kc >= 2:
                            act.wait_ge(s_h_lo, 8 * k + kc - 1)
                        do(h_ring(k, kc), bank_of("h", k, kc)[:, :], ACT.Identity, scale=gmul[:, k, kc:kc + 1],
                           bias=ada_cols[:, 24 * k + kc:24 * k + kc + 1]).then_inc(free_sem("h", k, kc), 1)
                    act.wait_ge(*freed("h", k, kc))
                    do(hhi[:, kc, :], h_ring(k, kc), ACT.Copy).then_inc(s_h_hi, 1)
                    act.wait_ge(s_h_hi, up(s_h_hi))

            act.wait_ge(*freed("vectors"))
            do(ca[:, :], vc[:, V_C:V_C + KC], ACT.Silu).then_inc(s_c_act, 1)
            act.wait_ge(s_c_act, up(s_c_act))
            act.wait_ge(s_constants_in, 16)
            norm(0, x_in, x_norm)
            split_hi()
            for n in range(7):
                split_hi()
                for b in (2 * n, 2 * n + 1):
                    act.wait_ge(*full("rw", b))
                    ps = bank_of("rw", b)
                    if b >= 2:
                        act.wait_ge(*freed("rw", b - 2))
                    elif b == 0:
                        act.wait_ge(s_u_prev_zero, 1)
                    do(u_prev[:, b % 2, 1:T + 1], ps[:, :], ACT.Copy, scale=vc[:, V_MU + b:V_MU + b + 1])\
                        .then_inc(s_rw_prev, 1)
                    act.wait_ge(s_rw_prev, up(s_rw_prev))
            act.wait_ge(*freed("rw", 13))
            do(lora_in[0:64, :], lora_in[0:64, :], ACT.Tanh).then_inc(s_rw_lora, 1)
            act.wait_ge(s_rw_lora, up(s_rw_lora))
            do(gate_lo[:, :], gate_lo[:, :], ACT.Sigmoid).then_inc(s_rw_lora, 1)
            act.wait_ge(s_rw_lora, up(s_rw_lora))
            early("rw lora")
            for c in range(4):
                act.wait_ge(*full("rw w", c))
                ps = bank_of("rw w", c)
                do(decay[:, c, :], ps[:, :], ACT.Sigmoid, bias=vc[:, V_W0 + c:V_W0 + c + 1]).then_inc(free_sem("rw w", c), 1)
                act.wait_ge(*freed("rw w", c))
            act.wait_ge(s_rw_k_k, 4)
            for c in range(4):
                act.wait_ge(*full("rw a", c))
                ps = bank_of("rw a", c)
                do(B[:, c, :], ps[:, :], ACT.Sigmoid, bias=vc[:, V_A0 + c:V_A0 + c + 1]).then_inc(free_sem("rw a", c), 1)
                act.wait_ge(*freed("rw a", c))
            early("rw kk")
            do(tmp[:, :, :], A[:, :, :], ACT.Square).then_inc(s_rw_kk2, 1)
            act.wait_ge(s_rw_kk2, up(s_rw_kk2))
            early("rw bonus")
            act.wait_ge(*freed("rw kk", 3))
            do(tmp[:, :, :], tmp[:, :, :], ACT.Sqrt).then_inc(s_rw_norm, 1)
            act.wait_ge(s_rw_norm, up(s_rw_norm))
            early(("rw sums", 0))
            early(("rw sums", 1))
            early(("rw sums", 2))
            early(("rw sums", 3))
            act.wait_ge(s_rw_sums, 1)
            do(tmp[:, :, :], cum[:, :, :], ACT.Exp, scale=-DECAY).then_inc(s_rw_e_r, 1)
            act.wait_ge(s_rw_e_r, up(s_rw_e_r))
            do(decay[:, :, :], decay[:, :, :], ACT.Exp, scale=-DECAY).then_inc(s_rw_e_a, 1)
            act.wait_ge(s_rw_e_a, up(s_rw_e_a))
            do(cum[:, :, :], cum[:, :, :], ACT.Exp, scale=DECAY).then_inc(s_rw_e_bk, 1)
            act.wait_ge(s_rw_e_bk, up(s_rw_e_bk))
            do(blk16(FAC), blk16(FAC), ACT.Exp, scale=-DECAY).then_inc(s_rw_factor, 1)
            act.wait_ge(s_rw_factor, up(s_rw_factor))
            early(("rw sums", 4))
            act.wait_ge(s_rw_state, 1)
            for c in range(TB):
                if c == 2:
                    act.wait_ge(s_angles, 2)
                    do(cos_sin[:, :, :], ang[:, 0:2, :], ACT.Sin).then_inc(s_cos_sin, 1)
                    act.wait_ge(s_cos_sin, up(s_cos_sin))
                    act.wait_ge(s_lam_dot, 2)
                    do(col(LR, 2), col(LR, 2), ACT.Exp).then_inc(s_lam_exp, 1)
                    act.wait_ge(s_lam_exp, up(s_lam_exp))
                for x_ in range(3):
                    act.wait_ge(*full("rw tok", c, x_))
                    ps = bank_of("rw tok", c, x_)
                    do(tok[:, x_, :], ps[:, :], ACT.Copy).then_inc(free_sem("rw tok", c, x_), 1)
                    act.wait_ge(*freed("rw tok", c, x_))
                early(("rw tok", c))
                for g in range(2):
                    act.wait_ge(*full("rw n", c, g))
                    ps = bank_of("rw n", c, g)
                    do(LX[:, g, :], ps[:, :], ACT.Copy, scale=-1.0).then_inc(free_sem("rw n", c, g), 1)
                    act.wait_ge(*freed("rw n", c, g))
                early(("rw x", c))
                for i in range(1, LEVELS):
                    for g in range(2):
                        act.wait_ge(*full("rw t", c, g, i))
                        ps = bank_of("rw t", c, g, i)
                        do(LX[:, g, :], ps[:, :], ACT.Copy).then_inc(free_sem("rw t", c, g, i), 1)
                        act.wait_ge(*freed("rw t", c, g, i))
                for what, dst in (("rw r", rhs_u), ("rw u", U)):
                    for g in range(2):
                        act.wait_ge(*full(what, c, g))
                        ps = bank_of(what, c, g)
                        do(dst[:, g, :], ps[:, 0:256], ACT.Copy, scale=-1.0 if dst is rhs_u else 1.0)\
                            .then_inc(free_sem(what, c, g), 1)
                        act.wait_ge(*freed(what, c, g))
                    early((what, c))
                for g in range(2):
                    act.wait_ge(*full("rw o", c, g))
                    ps = bank_of("rw o", c, g)
                    rows = slice(64 * g, 64 * g + 64)
                    do(R[rows, :, c * P:c * P + P], ps[rows, :].rearrange("p (b t) -> p b t", b=4), ACT.Copy)\
                        .then_inc(free_sem("rw o", c, g), 1)
                    act.wait_ge(*freed("rw o", c, g))
            early("rw mean")
            early("rw var")
            act.wait_ge(*freed("rw mean", 3))
            do(epi[:, :, :], R[:, :, :], ACT.Square).then_inc(s_rw_sq, 1)
            act.wait_ge(s_rw_sq, up(s_rw_sq))
            for c in range(4):
                act.wait_ge(*full("rw var", c))
                ps = bank_of("rw var", c)
                do(epi[:, c, :], ps[:, :], ACT.Ln, scale=1.0 / 64, bias=cst[:, C_GEPS:C_GEPS + 1])\
                    .then_inc(free_sem("rw var", c), 1)
                act.wait_ge(*freed("rw var", c))
            do(epi[:, :, :], epi[:, :, :], ACT.Exp, scale=-0.5).then_inc(s_rw_rstd, 1)
            act.wait_ge(s_rw_rstd, up(s_rw_rstd))
            early("rw g")
            act.wait_ge(*freed("rw g", 3))
            do(oc_hi[:, :, :], epi2[:, :, :], ACT.Copy).then_inc(s_rw_hi, 1)
            act.wait_ge(s_rw_hi, up(s_rw_hi))
            early("rw past")
            early("rw end")
            act.wait_ge(s_rw_split, 1)
            split_hi()
            act.wait_ge(s_hg_neg_abs, 1)
            do(q_lev[:, :, :], Hk[:, :, :], ACT.Exp).then_inc(s_act_step, 1)
            act.wait_ge(s_act_step, up(s_act_step))
            do(q_lev[:, :, :], q_lev[:, :, :], ACT.Ln, bias=1.0).then_inc(s_hg_ln, 1)
            act.wait_ge(s_hg_ln, up(s_hg_ln))
            act.wait_ge(s_hg_ls_less_z, 1)
            do(Hk[:, :, :], Hk[:, :, :], ACT.Exp).then_inc(s_hg_key, 1)
            act.wait_ge(s_hg_key, up(s_hg_key))
            split_hi()
            for tb in range(TB):
                act.wait_ge(*full("hg v", tb))
                ps = bank_of("hg v", tb)
                do(Hv[:, tb, :], ps[:, :], ACT.Copy).then_inc(free_sem("hg v", tb), 1)
                act.wait_ge(*freed("hg v", tb))
            early(("hg z", 0))
            early(("hg z", 1))
            act.wait_ge(s_hg_in, 16)
            do(Hg[:, :, :], Hg[:, :, :], ACT.Silu).then_inc(s_hg_silu, 1)
            act.wait_ge(s_hg_silu, up(s_hg_silu))
            act.wait_ge(s_hg_last, 1)
            do(blk16(HLAST), blk16(HLAST), ACT.Exp).then_inc(s_hg_e_last, 1)
            act.wait_ge(s_hg_e_last, up(s_hg_e_last))
            for i in range(LEVELS):
                act.wait_ge(s_hg_rel, i + 1)
                do(Z[:, :, :], Z[:, :, :], ACT.Abs).then_inc(s_act_step, 1)
                act.wait_ge(s_act_step, up(s_act_step))
                do(Z[:, :, :], Z[:, :, :], ACT.Exp, scale=-1.0).then_inc(s_hg_e_rel, 1)
                act.wait_ge(s_hg_e_rel, up(s_hg_e_rel))
                early(("hg sc", i + 1))
            act.wait_ge(s_hg_lev, LEVELS)
            do(Z[:, :, :], Hb[:, :, :], ACT.Exp).then_inc(s_hg_e_b, 1)
            act.wait_ge(s_hg_e_b, up(s_hg_e_b))
            early("hg past")
            early("hg left")
            act.wait_ge(s_hg_left, 1)
            do(Z[:, :, :], Z[:, :, :], ACT.Exp, scale=-1.0).then_inc(s_hg_e_left, 1)
            act.wait_ge(s_hg_e_left, up(s_hg_e_left))
            for c in range(TB):
                early(("hg tok", c))
                act.wait_ge(*full("hg tok", c))
                ps = bank_of("hg tok", c)
                do(k_tok[:, :], ps[:, :], ACT.Copy).then_inc(free_sem("hg tok", c), 1)
                act.wait_ge(*freed("hg tok", c))
                act.wait_ge(*full("hg o", c))
                ps = bank_of("hg o", c)
                do(q_lev[:, :, c * P:c * P + P], ps[:, :].rearrange("p (h t) -> p h t", h=4), ACT.Copy)\
                    .then_inc(free_sem("hg o", c), 1)
                act.wait_ge(*freed("hg o", c))
            do(k_lev[:, :, :], q_lev[:, :, :], ACT.Square).then_inc(s_hg_sq, 1)
            act.wait_ge(s_hg_sq, up(s_hg_sq))
            early("hg ss")
            for h in range(4):
                act.wait_ge(*full("hg ss", h))
                ps = bank_of("hg ss", h)
                do(Z[:, h, :], ps[:, :], ACT.Ln, scale=1.0 / P, bias=cst[:, C_EPS:C_EPS + 1])\
                    .then_inc(free_sem("hg ss", h), 1)
                act.wait_ge(*freed("hg ss", h))
            do(Z[:, :, :], Z[:, :, :], ACT.Exp, scale=-0.5).then_inc(s_hg_rstd, 1)
            act.wait_ge(s_hg_rstd, up(s_hg_rstd))
            act.wait_ge(s_hg_out, 4)
            for h in range(4):
                do(ob_hi[:, h, :], q_lev[:, h, :], ACT.Copy).then_inc(s_hg_hi, 1)
                act.wait_ge(s_hg_hi, up(s_hg_hi))
            early("hg end")
            act.wait_ge(s_hg_split, 4)
            split_hi()
            for tb in range(TB):
                act.wait_ge(*full("da v", tb))
                ps = bank_of("da v", tb)
                do(v_tok[:, tb, :], ps[:, :], ACT.Copy).then_inc(free_sem("da v", tb), 1)
                act.wait_ge(*freed("da v", tb))
            for t_ in range(4 * TB + 5):
                n = (t_ % TB + 1) * P
                h = t_ // 4 - 1
                if t_ == 4 * TB:
                    split_hi()
                if t_ < 4 * TB:
                    for m in range(2):
                        act.wait_ge(s_max, 2 * t_ + m + 1)
                        if t_ >= 3:
                            act.wait_ge(*full("da pt", t_ - 3))
                        ps = bank_of("da s", t_, m)
                        do(prob[:, t_ % 3, m, 0:n], ps[:, 0:n], ACT.Exp, scale=0.125, bias=col(NB + 2 * (t_ % 3) + m),
                           accum_out=col(SUM + 2 * (t_ % 3) + m)).then_inc(free_sem("da s", t_, m), 1)
                        act.wait_ge(*freed("da s", t_, m))
                if 1 <= t_ <= 4 * TB:
                    n = ((t_ - 1) % TB + 1) * P
                    act.wait_ge(*full("da pt", t_ - 1))
                    ps = bank_of("da pt", t_ - 1)
                    do(probT[(t_ - 1) % 2][:, 0:n], ps[:, 0:n], ACT.Copy).then_inc(free_sem("da pt", t_ - 1), 1)
                    act.wait_ge(*freed("da pt", t_ - 1))
                if h >= 0 and t_ % 4 == 1:
                    if h:
                        act.wait_ge(s_da_lo, h)
                    act.wait_ge(*full("da o", h))
                    ps = bank_of("da o", h)
                    do(att[:, :], ps[:, :], ACT.Copy).then_inc(free_sem("da o", h), 1)
                    act.wait_ge(*freed("da o", h))
                    do(att2[:, :], att[:, :], ACT.Square).then_inc(s_da_sq, 1)
                    act.wait_ge(s_da_sq, up(s_da_sq))
                elif h >= 0 and t_ % 4 == 2:
                    act.wait_ge(*full("da ss", h))
                    ps = bank_of("da ss", h)
                    do(att2[:, :], ps[:, :], ACT.Ln, scale=1.0 / P, bias=cst[:, C_EPS:C_EPS + 1])\
                        .then_inc(free_sem("da ss", h), 1)
                    act.wait_ge(*freed("da ss", h))
                    do(att2[:, :], att2[:, :], ACT.Exp, scale=-0.5).then_inc(s_da_rstd, 1)
                    act.wait_ge(s_da_rstd, up(s_da_rstd))
                h = t_ // 4 - 2
                if h >= 0 and t_ % 4 == 0:
                    act.wait_ge(s_da_out, h + 1)
                    do(oa_hi[:, h, :], att[:, :], ACT.Copy).then_inc(s_da_hi, 1)
                    act.wait_ge(s_da_hi, up(s_da_hi))
            act.wait_ge(s_da_lo, 4)
            for j in range(4):
                split_hi()
                split_hi()
                act.wait_ge(s_gates_in[j % 2], 16 * (j // 2 + 1))
                do(sg[j % 2][:, :, :, :], sg[j % 2][:, :, :, :], ACT.Sigmoid).then_inc(s_gated, 1)
                act.wait_ge(s_gated, up(s_gated))
                for m in range(2):
                    act.wait_ge(s_mg_sum, 2 * j + m + 1)
                    do(mg_hi[:, 2 * j + m, :], mg[:, m, :], ACT.Copy).then_inc(s_mg_hi, 1)
                    act.wait_ge(s_mg_hi, up(s_mg_hi))
            for n in range(4):
                split_hi()
            norm(1, x1, x1_norm)
            for j in range(FFN // 256):
                for which in range(2):
                    split_hi()
                    if which == 0:
                        for m in range(2):
                            act.wait_ge(*full("ffn", j, 0, m))
                            ps = bank_of("ffn", j, 0, m)
                            if j:
                                act.wait_ge(*freed("ffn", j - 1, 1, m))
                            do(f_tmp[:, m, :], ps[:, :], ACT.Sigmoid).then_inc(s_ffn_sig, 1)
                            act.wait_ge(s_ffn_sig, up(s_ffn_sig))
            for j in range(FFN // 256):
                for k in range(2):
                    kk = 2 * j + k
                    if kk >= 4:
                        act.wait_ge(s_down_k, kk - 3)
                    do(d_hi[:, kk % 4, :], hid[:, kk, :], ACT.Copy).then_inc(s_d_hi, 1)
                    act.wait_ge(s_d_hi, up(s_d_hi))
                split_hi()
            for tb in range(TB):
                act.wait_ge(s_x2_ready, 2 * tb + 2)
                do(y[:, tb, :], x1[:, tb, :], ACT.Square, accum_out=col(SS + tb)).then_inc(s_act_step, 1)
                act.wait_ge(s_act_step, up(s_act_step))
                do(col(RSTD + tb), col(SS + tb), ACT.Sqrt, scale=1.0 / D, bias=cst[:, C_EPS:C_EPS + 1])\
                    .then_inc(s_rms, 1)
                act.wait_ge(s_rms, up(s_rms))
            assert split_next[0] >= len(weights), (split_next, len(weights))

        @block.vector
        def _(dve):
            v = nc.vector
            stream_next, split_next, taken = [0], [0], [0]

            def tt(out_, a, b, op):
                return v.tensor_tensor(out_, a, b, op)

            def stt(out_, a, s_, b, op0, op1):
                return v.scalar_tensor_tensor(out=out_, in0=a, scalar=s_, in1=b, op0=op0, op1=op1)

            def ts(out_, a, s1, op0, s2=None, op1=None):
                if op1 is None:
                    return v.tensor_scalar(out_, a, s1, None, op0)
                return v.tensor_scalar(out_, a, s1, s2, op0, op1)

            def ada_sum(n, i):
                src = loaded(dve, i).rearrange("p (k n) -> p k n", k=KC)
                if ADA.index(n) >= 2:
                    dve.wait_ge(*full("ada", ADA[ADA.index(n) - 2]))
                for k in range(KC):
                    acc = ada_acc[:, ada_slot(n), k % 2, :]
                    if k < 2:
                        ts(acc, src[:, k, :], ca[:, k:k + 1], ALU.mult).then_inc(s_ada_step, 1)
                        step = up(s_ada_step)
                    elif k < KC - 1:
                        dve.wait_ge(s_ada_step, step - 1)
                        stt(acc, src[:, k, :], ca[:, k:k + 1], acc, ALU.mult, ALU.add).then_inc(s_ada_step, 1)
                        step = up(s_ada_step)
                    else:
                        dve.wait_ge(s_ada_step, step)
                        stt(acc, src[:, k, :], ca[:, k:k + 1], acc, ALU.mult, ALU.add).then_inc(s_panel_taken, 1)
                        dve.wait_ge(s_panel_taken, up(s_panel_taken))

            def ada_out(n):
                dve.wait_ge(*full("ada", n))
                ps = bank_of("ada", n)
                section = n // 4
                if section in (2, 5):
                    dve.wait_ge(s_gate_bias_in, 16 * (1 + section // 3))
                    row = gate_row[:, section // 3, (n % 4) * 256:(n % 4) * 256 + 256]
                    tt(row, ps[:, 0:256], row, ALU.add).then_inc(free_sem("ada", n), 1)
                    dve.wait_ge(*freed("ada", n))
                else:
                    tt(ada_cols[:, 2 * n:2 * n + 2], ps[:, 0:2], vc[:, V_ADAB + 2 * n:V_ADAB + 2 * n + 2], ALU.add)\
                        .then_inc(free_sem("ada", n), 1)
                    dve.wait_ge(*freed("ada", n))

            def take_panel():
                m = split_next[0]
                split_next[0] += 1
                if m >= len(weights):
                    return
                i = weights[m]
                src = loaded(dve, i)
                dve.wait_ge(s_panel_hi, m + 1)
                n = src.shape[1]
                tt(wlo[:, m % RING, 0:n], src, whi[:, m % RING, 0:n].bitcast(F32), ALU.subtract)\
                    .then_inc(s_panel_taken, 1)
                dve.wait_ge(s_panel_taken, up(s_panel_taken))
                if i + 1 < len(panels) and panels[i + 1][0] == "ada":
                    late_sum(i + 1)

            def late_sum(i):
                ada_sum(ADA[8 + taken[0]], i)
                taken[0] += 1

            def early(place):
                while split_next[0] < split_by(place):
                    take_panel()

            def row_rstd(k, tb):
                dve.wait_ge(s_rms, TB * k + tb + 1)
                v.reciprocal(col(RSTD + tb), col(RSTD + tb)).then_inc(s_rstd, 1)
                dve.wait_ge(s_rstd, up(s_rstd))

            def norm_scale(k, first, last):
                weight = V_NF if k else V_NM
                stt(gmul[:, k, first:last], ada_cols[:, 24 * k + 8 + first:24 * k + 8 + last], 1.0,
                    vc[:, weight + first:weight + last], ALU.add, ALU.mult).then_inc(s_gmul, 1)
                dve.wait_ge(s_gmul, up(s_gmul))

            def scaled_block(k, kc):
                if kc < KC and not by_act(k, kc):
                    dve.wait_ge(*full("h", k, kc))
                    if kc >= 2:
                        dve.wait_ge(s_h_hi, 8 * k + kc - 1)
                    ts(h_ring(k, kc), bank_of("h", k, kc)[:, :], gmul[:, k, kc:kc + 1], ALU.mult,
                       ada_cols[:, 24 * k + kc:24 * k + kc + 1], ALU.add).then_inc(free_sem("h", k, kc), 1)
                    dve.wait_ge(*freed("h", k, kc))

            def low_block(k, kc):
                dve.wait_ge(s_h_hi, 8 * k + kc + 1)
                tt(hlo[:, kc, :], h_ring(k, kc), hhi[:, kc, :].bitcast(F32), ALU.subtract).then_inc(s_h_lo, 1)
                dve.wait_ge(s_h_lo, up(s_h_lo))

            dve.wait_ge(*full("vectors"))
            ps = bank_of("vectors")
            v.tensor_copy(vc[:, :], ps[:, 0:NVEC]).then_inc(free_sem("vectors"), 1)
            dve.wait_ge(*freed("vectors"))
            ts(col(OM_MU, 14), vc[:, V_MU:V_MU + 14], -1.0, ALU.mult, 1.0, ALU.add).then_inc(s_dve_step, 1)
            dve.wait_ge(s_dve_step, up(s_dve_step))
            ts(col(OM_KA, 4), vc[:, V_KA:V_KA + 4], -1.0, ALU.mult, 1.0, ALU.add).then_inc(s_dve_step, 1)
            dve.wait_ge(s_dve_step, up(s_dve_step))
            ts(col(SUBW), vc[:, V_SUB:V_SUB + 1], 1.0 - LAM_INIT, ALU.mult).then_inc(s_dve_step, 1)
            dve.wait_ge(s_dve_step, up(s_dve_step))
            v.memset(u_prev[:, :, 0:1], 0.0).then_inc(s_u_prev_zero, 1)
            dve.wait_ge(s_u_prev_zero, up(s_u_prev_zero))
            dve.wait_ge(s_c_act, 1)
            for q in range(4):
                for half in range(2):
                    i = 2 * q + half
                    ada_sum(ADA[i], i)
                    if i:
                        ada_out(ADA[i - 1])
                    if q == 0:
                        row_rstd(0, 2 * half)
                        row_rstd(0, 2 * half + 1)
                    elif half == 0:
                        norm_scale(0, 2 * q - 2, 2 * q)
                    else:
                        low_block(0, 2 * q - 2)
                        low_block(0, 2 * q - 1)
            ada_out(7)
            norm_scale(0, 6, 8)
            low_block(0, 6)
            low_block(0, 7)
            take_panel()
            dve.wait_ge(s_masks, 1)
            for n in range(7):
                take_panel()
                for b in (2 * n, 2 * n + 1):
                    dve.wait_ge(s_rw_prev, b + 1)
                    ps = bank_of("rw", b)
                    dst = (R[:, b, :] if b < 4 else K[:, b - 4, :] if b < 8 else V[:, b - 8, :] if b < 12
                           else lora_in[:, :] if b == 12 else gate_lo[:, :])
                    stt(dst, ps[:, :], col(OM_MU + b), u_prev[:, b % 2, 0:T], ALU.mult, ALU.add)\
                        .then_inc(free_sem("rw", b), 1)
                    dve.wait_ge(*freed("rw", b))
                ada_out(ADA[8 + n])
            for c in range(4):
                ts(A[:, c, :], K[:, c, :], vc[:, V_KK + c:V_KK + c + 1], ALU.mult).then_inc(s_rw_k_k, 1)
                dve.wait_ge(s_rw_k_k, up(s_rw_k_k))
            early("rw lora")
            early("rw kk")
            for c in range(4):
                dve.wait_ge(*full("rw kk", c))
                ts(tmp[:, c, :], bank_of("rw kk", c)[:, :], 1e-24, ALU.max).then_inc(free_sem("rw kk", c), 1)
                dve.wait_ge(*freed("rw kk", c))
            early("rw bonus")
            dve.wait_ge(s_rw_norm, 1)
            v.reciprocal(tmp[:, :, :], tmp[:, :, :]).then_inc(s_dve_step, 1)
            dve.wait_ge(s_dve_step, up(s_dve_step))
            tt(A[:, :, :], A[:, :, :], tmp[:, :, :], ALU.mult).then_inc(s_dve_step, 1)
            dve.wait_ge(s_dve_step, up(s_dve_step))
            early(("rw sums", 0))
            for c in range(4):
                ts(cum[:, c, :], B[:, c, :], vc[:, V_KA + c:V_KA + c + 1], ALU.mult, col(OM_KA + c), ALU.add)\
                    .then_inc(s_dve_step, 1)
                dve.wait_ge(s_dve_step, up(s_dve_step))
            tt(K[:, :, :], K[:, :, :], cum[:, :, :], ALU.mult).then_inc(s_dve_step, 1)
            dve.wait_ge(s_dve_step, up(s_dve_step))
            early(("rw sums", 1))
            for c in range(4):
                stt(cum[:, c, :], R[:, c, :], vc[:, V_RK + c:V_RK + c + 1], K[:, c, :], ALU.mult, ALU.mult)\
                    .then_inc(s_rw_rkk, 1)
                dve.wait_ge(s_rw_rkk, up(s_rw_rkk))
            dve.wait_ge(*full("rw bonus"))
            v.tensor_copy(bonus[:, :], bank_of("rw bonus")[0:8, :]).then_inc(free_sem("rw bonus"), 1)
            dve.wait_ge(*freed("rw bonus"))
            early(("rw sums", 2))
            tt(B[:, :, :], A[:, :, :], B[:, :, :], ALU.mult).then_inc(s_dve_step, 1)
            dve.wait_ge(s_dve_step, up(s_dve_step))
            for n in range(16):
                v.tensor_tensor_scan(blocks(cum)[:, n, :], ones, blocks(decay)[:, n, :], 0.0, ALU.mult, ALU.add)\
                    .then_inc(s_dve_step, 1)
                dve.wait_ge(s_dve_step, up(s_dve_step))
            early(("rw sums", 3))
            v.tensor_copy(blk16(BREF), blocks(cum)[:, :, 63]).then_inc(s_dve_step, 1)
            dve.wait_ge(s_dve_step, up(s_dve_step))
            v.tensor_copy(blk16(BLAST), blocks(cum)[:, :, P - 1]).then_inc(s_dve_step, 1)
            dve.wait_ge(s_dve_step, up(s_dve_step))
            tt(decay[:, :, :], cum[:, :, :], decay[:, :, :], ALU.subtract).then_inc(s_dve_step, 1)
            dve.wait_ge(s_dve_step, up(s_dve_step))
            middle = bcast(blk16(BREF).unsqueeze(2), P, 16, P)
            tt(blocks(decay), blocks(decay), middle, ALU.subtract).then_inc(s_dve_step, 1)
            dve.wait_ge(s_dve_step, up(s_dve_step))
            tt(blocks(cum), blocks(cum), middle, ALU.subtract).then_inc(s_dve_step, 1)
            dve.wait_ge(s_dve_step, up(s_dve_step))
            tt(blk16(FAC), blk16(BLAST), blk16(BREF), ALU.subtract).then_inc(s_dve_step, 1)
            dve.wait_ge(s_dve_step, up(s_dve_step))
            fac = blk16(FAC).rearrange("p (a c) -> p a c", c=TB)
            ref = blk16(BREF).rearrange("p (a c) -> p a c", c=TB)
            tt(fac[:, :, 0:TB - 1], fac[:, :, 0:TB - 1], ref[:, :, 1:TB], ALU.add).then_inc(s_rw_sums, 1)
            dve.wait_ge(s_rw_sums, up(s_rw_sums))
            early(("rw sums", 4))
            dve.wait_ge(s_rw_e_r, 1)
            tt(R[:, :, :], R[:, :, :], tmp[:, :, :], ALU.mult).then_inc(s_dve_step, 1)
            dve.wait_ge(s_dve_step, up(s_dve_step))
            dve.wait_ge(s_rw_e_a, 1)
            tt(A[:, :, :], A[:, :, :], decay[:, :, :], ALU.mult).then_inc(s_dve_step, 1)
            dve.wait_ge(s_dve_step, up(s_dve_step))
            dve.wait_ge(s_rw_e_bk, 1)
            tt(B[:, :, :], B[:, :, :], cum[:, :, :], ALU.mult).then_inc(s_dve_step, 1)
            dve.wait_ge(s_dve_step, up(s_dve_step))
            tt(K[:, :, :], K[:, :, :], cum[:, :, :], ALU.mult).then_inc(s_dve_step, 1)
            dve.wait_ge(s_dve_step, up(s_dve_step))
            dve.wait_ge(s_rw_factor, 1)
            dve.wait_ge(s_masks, 1)
            v.memset(M[:, :, :], 0.0).then_inc(s_rw_state, 1)
            dve.wait_ge(s_rw_state, up(s_rw_state))

            def four(ap):
                return ap.rearrange("p (h t) -> p h t", h=4)

            def lmask(i, upper):
                return bcast(lev_mask[:, 2 * i + upper, :].unsqueeze(1), P, 4, P)

            def angles(x_):
                dst = ang[:, x_, :]
                if x_:
                    dve.wait_ge(s_positions_in, 16)
                    v.tensor_copy(ang[:, 2, :], pos_i[:, :]).then_inc(s_dve_step, 1)
                    dve.wait_ge(s_dve_step, up(s_dve_step))
                    ts(ang[:, 2, :], ang[:, 2, :], cst[:, C_FREQ:C_FREQ + 1], ALU.mult).then_inc(s_dve_step, 1)
                    dve.wait_ge(s_dve_step, up(s_dve_step))
                ts(turns[:, :], ang[:, 2, :], 1.0 / TWO_PI, ALU.mult, 0.0 if x_ else 0.25, ALU.add)\
                    .then_inc(s_dve_step, 1)
                dve.wait_ge(s_dve_step, up(s_dve_step))
                ts(turns[:, :], turns[:, :], ROUND, ALU.add).then_inc(s_dve_step, 1)
                dve.wait_ge(s_dve_step, up(s_dve_step))
                ts(turns[:, :], turns[:, :], ROUND, ALU.subtract).then_inc(s_dve_step, 1)
                dve.wait_ge(s_dve_step, up(s_dve_step))
                stt(dst, turns[:, :], -TURN[0], ang[:, 2, :], ALU.mult, ALU.add).then_inc(s_dve_step, 1)
                dve.wait_ge(s_dve_step, up(s_dve_step))
                stt(dst, turns[:, :], -TURN[1], dst, ALU.mult, ALU.add).then_inc(s_dve_step, 1)
                dve.wait_ge(s_dve_step, up(s_dve_step))
                stt(dst, turns[:, :], -TURN[2], dst, ALU.mult, ALU.add).then_inc(s_dve_step, 1)
                dve.wait_ge(s_dve_step, up(s_dve_step))
                ts(dst, dst, 0.0 if x_ else TWO_PI / 4, ALU.add).then_inc(s_dve_step, 1)
                dve.wait_ge(s_dve_step, up(s_dve_step))
                ts(dst, dst, 3.1415925, ALU.min, -3.1415925, ALU.max).then_inc(s_angles, 1)
                dve.wait_ge(s_angles, up(s_angles))

            id4 = bcast(ident.unsqueeze(1), P, 4, P)
            for c in range(TB):
                early(("rw tok", c))
                for g in range(2):
                    for hl in range(4):
                        dve.wait_ge(*full("rw sc", c, g, hl))
                        ps = bank_of("rw sc", c, g, hl)
                        tt(SC[g][:, hl, :], ps[:, :], cst[:, C_MASK:C_MASK + T], ALU.mult).then_inc(free_sem("rw sc", c, g, hl), 1)
                        dve.wait_ge(*freed("rw sc", c, g, hl))
                for g in range(2):
                    dve.wait_ge(*freed("rw n", c, g))
                    v.tensor_copy(four(X[:, g, :]), id4).then_inc(s_dve_step, 1)
                    dve.wait_ge(s_dve_step, up(s_dve_step))
                    v.tensor_copy(four(XT[:, g, :]), id4).then_inc(s_dve_step, 1)
                    dve.wait_ge(s_dve_step, up(s_dve_step))
                    v.copy_predicated(four(XT[:, g, :]), lmask(0, 1), SC[g][:, :, 0:P]).then_inc(s_dve_step, 1)
                    dve.wait_ge(s_dve_step, up(s_dve_step))
                    v.copy_predicated(four(X[:, g, :]), lmask(0, 0), four(LX[:, g, :])).then_inc(s_rw_x, 1)
                    dve.wait_ge(s_rw_x, up(s_rw_x))
                early(("rw x", c))
                for i in range(1, LEVELS):
                    for g in range(2):
                        if i < LEVELS - 1:
                            dve.wait_ge(*full("rw p", c, g, i))
                            ps = bank_of("rw p", c, g, i)
                            v.copy_predicated(four(X[:, g, :]), lmask(i, 0), four(ps[:, :])).then_inc(free_sem("rw p", c, g, i), 1)
                            dve.wait_ge(*freed("rw p", c, g, i))
                        dve.wait_ge(*full("rw pt", c, g, i))
                        ps = bank_of("rw pt", c, g, i)
                        v.copy_predicated(four(XT[:, g, :]), lmask(i, 1), four(ps[:, :])).then_inc(free_sem("rw pt", c, g, i), 1)
                        dve.wait_ge(*freed("rw pt", c, g, i))
                early(("rw r", c))
                early(("rw u", c))
                if c == 0:
                    angles(1)
                elif c == 1:
                    angles(0)
                    dve.wait_ge(s_lambda_in, 16)
                    for x_ in range(2):
                        pair = lam_in[:, 128 * x_:128 * x_ + 128].rearrange("p (a e) -> p a e", a=2)
                        tt(pair[:, 0, :], pair[:, 0, :], pair[:, 1, :], ALU.mult).then_inc(s_dve_step, 1)
                        dve.wait_ge(s_dve_step, up(s_dve_step))
                        v.reduce_sum(col(LR + x_), pair[:, 0, :], AX_X).then_inc(s_lam_dot, 1)
                        dve.wait_ge(s_lam_dot, up(s_lam_dot))
                elif c == 2:
                    dve.wait_ge(s_lam_exp, 1)
                    stt(col(NLAM), col(LR + 1), -LAM_INIT, col(LR), ALU.add, ALU.subtract).then_inc(s_dve_step, 1)
                    dve.wait_ge(s_dve_step, up(s_dve_step))
                if c < TB - 1:
                    for g in range(2):
                        dve.wait_ge(*full("rw m", c, g))
                        ps = bank_of("rw m", c, g)
                        rows = slice(64 * g, 64 * g + 64)
                        state = M[rows, :, :]
                        tt(state, state, ps[rows, 0:256].rearrange("p (b v) -> p b v", b=4), ALU.add)\
                            .then_inc(free_sem("rw m", c, g), 1)
                        dve.wait_ge(*freed("rw m", c, g))
                        tt(state, state, bcast(fac[rows, :, c:c + 1], 64, 4, 64), ALU.mult)\
                            .then_inc(s_rw_state, 1)
                        dve.wait_ge(s_rw_state, up(s_rw_state))
            early("rw mean")
            dve.wait_ge(*freed("rw o", TB - 1, 1))
            for c in range(4):
                dve.wait_ge(*full("rw mean", c))
                ps = bank_of("rw mean", c)
                stt(R[:, c, :], ps[:, :], -1.0 / 64, R[:, c, :], ALU.mult, ALU.add).then_inc(free_sem("rw mean", c), 1)
                dve.wait_ge(*freed("rw mean", c))
            for c in range(4):
                dve.wait_ge(*full("rw bv", c))
                ps = bank_of("rw bv", c)
                tt(epi2[:, c, :], V[:, c, :], ps[:, :], ALU.mult).then_inc(free_sem("rw bv", c), 1)
                dve.wait_ge(*freed("rw bv", c))
            early("rw var")
            dve.wait_ge(s_rw_rstd, 1)
            tt(R[:, :, :], R[:, :, :], epi[:, :, :], ALU.mult).then_inc(s_dve_step, 1)
            dve.wait_ge(s_dve_step, up(s_dve_step))
            for c in range(4):
                ts(R[:, c, :], R[:, c, :], vc[:, V_GNW + c:V_GNW + c + 1], ALU.mult, vc[:, V_GNB + c:V_GNB + c + 1], ALU.add)\
                    .then_inc(s_dve_step, 1)
                dve.wait_ge(s_dve_step, up(s_dve_step))
            early("rw g")
            tt(R[:, :, :], R[:, :, :], epi2[:, :, :], ALU.add).then_inc(s_dve_step, 1)
            dve.wait_ge(s_dve_step, up(s_dve_step))
            for c in range(4):
                dve.wait_ge(*full("rw g", c))
                ps = bank_of("rw g", c)
                tt(epi2[:, c, :], R[:, c, :], ps[:, :], ALU.mult).then_inc(free_sem("rw g", c), 1)
                dve.wait_ge(*freed("rw g", c))
            dve.wait_ge(s_rw_hi, 1)
            tt(oc_lo[:, :, :], epi2[:, :, :], oc_hi[:, :, :].bitcast(F32), ALU.subtract).then_inc(s_rw_split, 1)
            dve.wait_ge(s_rw_split, up(s_rw_split))
            early("rw past")
            early("rw end")
            take_panel()
            dve.wait_ge(s_z_in, 16)
            stt(Hk[:, :, :], Z[:, :, :], -1.0, Z[:, :, :], ALU.mult, ALU.min).then_inc(s_hg_neg_abs, 1)
            dve.wait_ge(s_hg_neg_abs, up(s_hg_neg_abs))
            dve.wait_ge(s_hg_ln, 1)
            stt(k_lev[:, :, :], Z[:, :, :], 0.0, q_lev[:, :, :], ALU.min, ALU.subtract).then_inc(s_dve_step, 1)
            dve.wait_ge(s_dve_step, up(s_dve_step))
            tt(Hk[:, :, :], k_lev[:, :, :], Z[:, :, :], ALU.subtract).then_inc(s_hg_ls_less_z, 1)
            dve.wait_ge(s_hg_ls_less_z, up(s_hg_ls_less_z))
            take_panel()
            for n in range(16):
                v.tensor_tensor_scan(blocks(Hb)[:, n, :], ones, blocks(k_lev)[:, n, :], 0.0, ALU.mult, ALU.add)\
                    .then_inc(s_dve_step, 1)
                dve.wait_ge(s_dve_step, up(s_dve_step))
            early(("hg z", 0))
            v.tensor_copy(blk16(HLAST), blocks(Hb)[:, :, P - 1]).then_inc(s_dve_step, 1)
            dve.wait_ge(s_dve_step, up(s_dve_step))
            v.tensor_copy(blk16(BLAST), blk16(HLAST)).then_inc(s_hg_last, 1)
            dve.wait_ge(s_hg_last, up(s_hg_last))
            v.memset(ST[:, :, :, :], 0.0).then_inc(s_dve_step, 1)
            dve.wait_ge(s_dve_step, up(s_dve_step))
            v.memset(q_lev[:, :, :], 0.0).then_inc(s_dve_step, 1)
            dve.wait_ge(s_dve_step, up(s_dve_step))
            v.memset(k_lev[:, :, :], 0.0).then_inc(s_dve_step, 1)
            dve.wait_ge(s_dve_step, up(s_dve_step))

            def halves(tile, s):
                return tile[:, :, :].rearrange("p a (n s) -> p (a n) s", s=2 * s)

            def rel(i):
                s = 1 << i
                hb = halves(Hb, s)
                tt(halves(Z, s), hb, bcast(hb[:, :, s - 1:s], P, 1024 // s, 2 * s), ALU.subtract)\
                    .then_inc(s_hg_rel, 1)
                dve.wait_ge(s_hg_rel, up(s_hg_rel))

            def gather(lev, mask):
                for c in range(TB):
                    dve.wait_ge(*full("hg sc", lev, c))
                    ps = bank_of("hg sc", lev, c)
                    v.copy_predicated(ST[:, c, :, :], bcast(mask.unsqueeze(1), P, 4, P), four(ps[:, :]))\
                        .then_inc(free_sem("hg sc", lev, c), 1)
                    dve.wait_ge(*freed("hg sc", lev, c))

            for i in range(LEVELS):
                s = 1 << i
                rel(i)
                if i == 0:
                    early(("hg z", 1))
                if i == 0:
                    dve.wait_ge(s_hg_key, 1)
                    gather(0, lev_mask[:, 2 * LEVELS, :])
                else:
                    gather(i, lev_mask[:, 2 * (i - 1) + 1, :])
                dve.wait_ge(s_hg_e_rel, i + 1)
                dve.wait_ge(s_hq_in, 16)
                z, q, k = halves(Z, s), halves(Hq, s), halves(Hk, s)
                tt(halves(q_lev, s)[:, :, s:], q[:, :, s:], z[:, :, s:], ALU.mult).then_inc(s_dve_step, 1)
                dve.wait_ge(s_dve_step, up(s_dve_step))
                tt(halves(k_lev, s)[:, :, :s], k[:, :, :s], z[:, :, :s], ALU.mult).then_inc(s_hg_lev, 1)
                dve.wait_ge(s_hg_lev, up(s_hg_lev))
                early(("hg sc", i + 1))
            gather(LEVELS, lev_mask[:, 2 * LEVELS - 1, :])
            dve.wait_ge(s_hg_e_b, 1)
            tt(Hq[:, :, :], Hq[:, :, :], Z[:, :, :], ALU.mult).then_inc(s_dve_step, 1)
            dve.wait_ge(s_dve_step, up(s_dve_step))
            tt(blocks(Z), blocks(Hb), bcast(blk16(BLAST).unsqueeze(2), P, 16, P), ALU.subtract)\
                .then_inc(s_hg_left, 1)
            dve.wait_ge(s_hg_left, up(s_hg_left))
            early("hg past")
            early("hg left")
            dve.wait_ge(s_hg_e_left, 1)
            tt(Hk[:, :, :], Hk[:, :, :], Z[:, :, :], ALU.mult).then_inc(s_hg_k_left, 1)
            dve.wait_ge(s_hg_k_left, up(s_hg_k_left))
            dve.wait_ge(s_hg_e_last, 1)
            for c in range(TB - 1):
                early(("hg tok", c))
                dve.wait_ge(*full("hg s", c))
                ps = bank_of("hg s", c)
                if c == 0:
                    v.tensor_copy(Hs[:, :, :], four(ps[:, :])).then_inc(free_sem("hg s", c), 1)
                    dve.wait_ge(*freed("hg s", c))
                else:
                    for h in range(4):
                        k = HLAST + 4 * h + c
                        stt(Hs[:, h, :], Hs[:, h, :], col(k), ps[:, h * P:h * P + P], ALU.mult, ALU.add)\
                            .then_inc(s_dve_step, 1)
                        dve.wait_ge(s_dve_step, up(s_dve_step))
                    v.tensor_copy(Hs[:, 0, 0:2], Hs[:, 0, 0:2]).then_inc(free_sem("hg s", c), 1)
                    dve.wait_ge(*freed("hg s", c))
            early(("hg tok", TB - 1))
            early("hg ss")
            early("hg end")
            dve.wait_ge(s_hg_rstd, 1)
            dve.wait_ge(s_hg_silu, 1)
            for h in range(4):
                tt(q_lev[:, h, :], q_lev[:, h, :], Z[:, h, :], ALU.mult).then_inc(s_dve_step, 1)
                dve.wait_ge(s_dve_step, up(s_dve_step))
                stt(q_lev[:, h, :], q_lev[:, h, :], vc[:, V_HGN:V_HGN + 1], Hg[:, h, :], ALU.mult, ALU.mult)\
                    .then_inc(s_hg_out, 1)
                dve.wait_ge(s_hg_out, up(s_hg_out))
            for h in range(4):
                dve.wait_ge(s_hg_hi, h + 1)
                tt(ob_lo[:, h, :], q_lev[:, h, :], ob_hi[:, h, :].bitcast(F32), ALU.subtract)\
                    .then_inc(s_hg_split, 1)
                dve.wait_ge(s_hg_split, up(s_hg_split))
            take_panel()
            dve.wait_ge(s_cos_sin, 1)
            for n in range(8):
                dve.wait_ge(*full("da rot", n))
                ps = bank_of("da rot", n)
                x_ = qk[:, n // 4, n % 4, :]
                tt(rot[:, n % 4, :], ps[:, :], cos_sin[:, 1, :], ALU.mult).then_inc(free_sem("da rot", n), 1)
                dve.wait_ge(*freed("da rot", n))
                tt(x_, x_, cos_sin[:, 0, :], ALU.mult).then_inc(s_dve_step, 1)
                dve.wait_ge(s_dve_step, up(s_dve_step))
                tt(x_, x_, rot[:, n % 4, :], ALU.add).then_inc(s_roped, 1)
                dve.wait_ge(s_roped, up(s_roped))
            ada_out(19)
            for t_ in range(4 * TB + 5):
                if t_ % 4 == 0 and 4 <= t_ <= 4 * TB:
                    ada_out(7 + t_ // 4)
                if 1 <= t_ <= 4 * TB:
                    n, r = ((t_ - 1) % TB + 1) * P, (t_ - 1) % 3
                    dve.wait_ge(*freed("da s", t_ - 1, 0))
                    dve.wait_ge(*freed("da s", t_ - 1, 1))
                    v.reciprocal(col(RS, 2), col(SUM + 2 * r, 2)).then_inc(s_dve_step, 1)
                    dve.wait_ge(s_dve_step, up(s_dve_step))
                    tt(col(LR), col(RS + 1), col(NLAM), ALU.mult).then_inc(s_dve_step, 1)
                    dve.wait_ge(s_dve_step, up(s_dve_step))
                    p0, p1 = prob[:, r, 0, 0:n], prob[:, r, 1, 0:n]
                    ts(p0, p0, col(RS), ALU.mult).then_inc(s_dve_step, 1)
                    dve.wait_ge(s_dve_step, up(s_dve_step))
                    stt(p0, p1, col(LR), p0, ALU.mult, ALU.add).then_inc(s_da_p, 1)
                    dve.wait_ge(s_da_p, up(s_da_p))
                if t_ < 4 * TB:
                    n, nb = (t_ % TB + 1) * P, NB + 2 * (t_ % 3)
                    for m in range(2):
                        dve.wait_ge(*full("da s", t_, m))
                        v.reduce_max(col(MX + m), bank_of("da s", t_, m)[:, 0:n], AX_X).then_inc(s_dve_step, 1)
                        dve.wait_ge(s_dve_step, up(s_dve_step))
                        ts(col(nb + m), col(MX + m), -0.125, ALU.mult).then_inc(s_max, 1)
                        dve.wait_ge(s_max, up(s_max))
                if t_ in range(2, 4 * TB, 4):
                    late_sum(weights[split_next[0]] - 4 + t_ // 4)
                elif t_ == 4 * TB - 1:
                    take_panel()
                h = t_ // 4 - 1
                if h >= 0 and t_ % 4 == 3:
                    dve.wait_ge(s_da_rstd, h + 1)
                    stt(att[:, :], att[:, :], col(SUBW), att2[:, :], ALU.mult, ALU.mult).then_inc(s_da_out, 1)
                    dve.wait_ge(s_da_out, up(s_da_out))
                h = t_ // 4 - 2
                if h >= 0 and t_ % 4 == 0:
                    dve.wait_ge(s_da_hi, h + 1)
                    tt(oa_lo[:, h, :], att[:, :], oa_hi[:, h, :].bitcast(F32), ALU.subtract).then_inc(s_da_lo, 1)
                    dve.wait_ge(s_da_lo, up(s_da_lo))
            for j in range(4):
                take_panel()
                take_panel()
                gates, other = sg[j % 2], br[j]
                dve.wait_ge(s_gated, j + 1)
                dve.wait_ge(s_branch_in[j], 16)
                tt(other[:, :, :], gates[:, 2, :, :], other[:, :, :], ALU.mult).then_inc(s_dve_step, 1)
                dve.wait_ge(s_dve_step, up(s_dve_step))
                for m in range(2):
                    dve.wait_ge(*full("branch", j, 0, m))
                    tt(mg[:, m, :], gates[:, 0, m, :], bank_of("branch", j, 0, m)[:, :], ALU.mult)\
                        .then_inc(free_sem("branch", j, 0, m), 1)
                    dve.wait_ge(*freed("branch", j, 0, m))
                    tt(mg[:, m, :], mg[:, m, :], other[:, m, :], ALU.add).then_inc(s_dve_step, 1)
                    dve.wait_ge(s_dve_step, up(s_dve_step))
                for m in range(2):
                    dve.wait_ge(*full("branch", j, 1, m))
                    tt(gates[:, 1, m, :], gates[:, 1, m, :], bank_of("branch", j, 1, m)[:, :], ALU.mult)\
                        .then_inc(free_sem("branch", j, 1, m), 1)
                    dve.wait_ge(*freed("branch", j, 1, m))
                    tt(mg[:, m, :], mg[:, m, :], gates[:, 1, m, :], ALU.add).then_inc(s_mg_sum, 1)
                    dve.wait_ge(s_mg_sum, up(s_mg_sum))
                for m in range(2):
                    dve.wait_ge(s_mg_hi, 2 * j + m + 1)
                    tt(mg_lo[:, 2 * j + m, :], mg[:, m, :], mg_hi[:, 2 * j + m, :].bitcast(F32), ALU.subtract)\
                        .then_inc(s_merged, 1)
                    dve.wait_ge(s_merged, up(s_merged))
            for n in range(3):
                take_panel()
            dve.wait_ge(s_x_again, 16)
            for n in range(2):
                if n:
                    take_panel()
                for tb in range(TB):
                    dve.wait_ge(*full("out", n, tb))
                    ps = bank_of("out", n, tb)
                    cols_ = slice(n * T, n * T + T)
                    tt(mg[:, 0, :], gate_row[:, 0, cols_], ps[:, :], ALU.mult).then_inc(free_sem("out", n, tb), 1)
                    dve.wait_ge(*freed("out", n, tb))
                    tt(x1[:, tb, cols_], x1[:, tb, cols_], mg[:, 0, :], ALU.add).then_inc(s_x1_ready, 1)
                    dve.wait_ge(s_x1_ready, up(s_x1_ready))
                    if n:
                        row_rstd(1, tb)
            norm_scale(1, 0, KC)
            for kc in range(KC):
                scaled_block(1, kc + 1)
                low_block(1, kc)
            for j in range(FFN // 256):
                take_panel()
                take_panel()
                for m in range(2):
                    dve.wait_ge(s_ffn_sig, 2 * j + m + 1)
                    tt(f_tmp[:, m, :], f_tmp[:, m, :], bank_of("ffn", j, 0, m)[:, :], ALU.mult)\
                        .then_inc(free_sem("ffn", j, 0, m), 1)
                    dve.wait_ge(*freed("ffn", j, 0, m))
                    dve.wait_ge(*full("ffn", j, 1, m))
                    ps = bank_of("ffn", j, 1, m)
                    tt(hid[:, 2 * j + m, :], f_tmp[:, m, :], ps[:, :], ALU.mult).then_inc(free_sem("ffn", j, 1, m), 1)
                    dve.wait_ge(*freed("ffn", j, 1, m))
                if j < 4:
                    ada_out(20 + j)
            for j in range(FFN // 256):
                for k in range(2):
                    kk = 2 * j + k
                    dve.wait_ge(s_d_hi, kk + 1)
                    tt(d_lo[:, kk % 4, :], hid[:, kk, :], d_hi[:, kk % 4, :].bitcast(F32), ALU.subtract)\
                        .then_inc(s_d_lo, 1)
                    dve.wait_ge(s_d_lo, up(s_d_lo))
                take_panel()
            dve.wait_ge(s_final_weight_in, 16)
            for tb in range(TB):
                for n in range(2):
                    dve.wait_ge(*full("down", tb, n))
                    ps = bank_of("down", tb, n)
                    cols_ = slice(n * T, n * T + T)
                    tt(f_tmp[:, n, :], gate_row[:, 1, cols_], ps[:, :], ALU.mult).then_inc(free_sem("down", tb, n), 1)
                    dve.wait_ge(*freed("down", tb, n))
                    tt(x1[:, tb, cols_], x1[:, tb, cols_], f_tmp[:, n, :], ALU.add).then_inc(s_x2_ready, 1)
                    dve.wait_ge(s_x2_ready, up(s_x2_ready))
                row_rstd(2, tb)
                stt(y[:, tb, :], x1[:, tb, :], col(RSTD + tb), final_row[:, :], ALU.mult, ALU.mult)\
                    .then_inc(s_y_ready, 1)
                dve.wait_ge(s_y_ready, up(s_y_ready))

        @block.tensor
        def _(pe):
            t = nc.tensor
            started = [0] * BANKS
            m_next = [0]
            late_next = [8]
            ada_at = [i for i, (kind, _) in enumerate(panels) if kind == "ada"]

            def begin(*use):
                bank, k = plan.of[use]
                assert k == started[bank], use
                started[bank] += 1
                if k:
                    pe.wait_ge(bank_free[bank], k)
                return psum[bank]

            def end(instruction, *use):
                instruction.then_inc(bank_full[plan.of[use][0]], 1)

            def mm(out_, lhsT, rhs, start=True, stop=True):
                return t.matmul(out_, lhsT, rhs, start=start, stop=stop, skip_group_check=True)

            def next_panel():
                m = m_next[0]
                m_next[0] += 1
                pe.wait_ge(s_panel_taken, weights[m] + 1)
                return m % RING

            def split3(ps, w, x_, first, last):
                mm(ps, w[0], x_[0], first, False)
                mm(ps, w[0], x_[1], False, False)
                return mm(ps, w[1], x_[0], False, last)

            def stationary_unit(slot, m, xs, kcs, *use, h_from=None):
                ps = begin(*use)
                for k in range(kcs):
                    if h_from is not None:
                        pe.wait_ge(s_h_lo, h_from + k + 1)
                    at_ = slice(256 * k + P * m, 256 * k + P * m + P)
                    last = split3(ps[:, :], (whi[:, slot, at_], wlo[:, slot, at_]),
                                  (xs[0][:, k, :], xs[1][:, k, :]), k == 0, k == kcs - 1)
                end(last, *use)

            def moving_units(xs, uses, between=None):
                tiles = [begin(*u) for u in uses]
                for half in range(2):
                    slot = next_panel()
                    for tb, ps in enumerate(tiles):
                        for k in range(4):
                            kk, cols_ = 4 * half + k, slice(T * k, T * k + T)
                            toks = slice(tb * P, tb * P + P)
                            last = split3(ps[:, :], (xs[0][:, kk, toks], xs[1][:, kk, toks]),
                                          (whi[:, slot, cols_], wlo[:, slot, cols_]), kk == 0, kk == KC - 1)
                        if half:
                            end(last, *uses[tb])
                    if not half:
                        last.then_inc(s_panel_used, 1)
                        if between:
                            between()

            def ada(n):
                pe.wait_ge(s_panel_taken, ada_at[ADA.index(n)] + 1)
                ps = begin("ada", n)
                acc = ada_acc[:, ada_slot(n), :, :]
                if n // 4 in (2, 5):
                    for x_ in range(2):
                        last = mm(ps[:, 0:256], ones, acc[:, x_, :], x_ == 0, x_ == 1)
                else:
                    for m in range(2):
                        for x_ in range(2):
                            last = mm(ps[:, m:m + 1], acc[:, x_, P * m:P * m + P], ones[:, 0:1], x_ == 0, x_ == 1)
                end(last, "ada", n)

            def late_ada():
                ada(ADA[late_next[0]])
                late_next[0] += 1

            def transposes(k, src, kcs):
                pe.wait_ge(s_normed, TB * (k + 1))
                for kc in kcs:
                    ps = begin("h", k, kc)
                    for tb in range(TB):
                        last = t.transpose(ps[:, tb * P:tb * P + P], src[:, tb, kc * P:kc * P + P], ident)
                    end(last, "h", k, kc)

            early_slot = [0]

            def early(place):
                inputs = {"h": (hhi, hlo), "rw": (oc_hi, oc_lo)}
                number, at, _ = stretch(place)
                for part in range(at, at + dict(EARLY[number])[place]):
                    panel, u, k0, source, begins, ends_ = early_parts()[part]
                    if part == 0 or panels_before(part - 1) != panel:
                        early_slot[0] = next_panel()
                    if u == E_RW:
                        pe.wait_ge(s_rw_split, 1)
                    ps, slot = begin("early", u) if begins else bank_of("early", u), early_slot[0]
                    for k in range(k0, k0 + 4):
                        at_ = slice(256 * k + P * (u % 2), 256 * k + P * (u % 2) + P)
                        last = split3(ps[:, :], (whi[:, slot, at_], wlo[:, slot, at_]),
                                      (inputs[source][0][:, k, :], inputs[source][1][:, k, :]),
                                      begins and k == k0, ends_ and k == k0 + 3)
                    if ends_:
                        end(last, "early", u)

            h_in = (hhi, hlo)
            pe.wait_ge(s_vectors_in, 16)
            pe.wait_ge(s_constants_in, 16)
            ps = begin("vectors")
            end(t.transpose(ps[:, 0:NVEC], vrow[:, :], cst[0:NVEC, C_ID:C_ID + NVEC]), "vectors")
            for q in range(4):
                ada(q)
                ada(4 + q)
                transposes(0, x_norm, (2 * q, 2 * q + 1))
            for n in range(7):
                slot = next_panel()
                for m in range(2):
                    stationary_unit(slot, m, h_in, KC, "rw", 2 * n + m, h_from=None if n or m else 0)
                late_ada()
            early("rw lora")
            pe.wait_ge(s_lora_in, 48)
            pe.wait_ge(s_rw_lora, 1)
            for c in range(4):
                ps = begin("rw w", c)
                end(mm(ps[:, :], lora_w[0:64, 0, c * P:c * P + P], lora_in[0:64, :]), "rw w", c)
            for c in range(4):
                ps = begin("rw a", c)
                end(mm(ps[:, :], lora_w[64:128, 0, c * P:c * P + P], lora_in[64:128, :]), "rw a", c)
            early("rw kk")
            pe.wait_ge(s_rw_kk2, 1)
            for c in range(4):
                ps = begin("rw kk", c)
                end(mm(ps[:, :], pair_ones, tmp[:, c, :]), "rw kk", c)
            early("rw bonus")
            early(("rw sums", 0))
            early(("rw sums", 1))
            pe.wait_ge(s_rw_rkk, 4)
            ps = begin("rw bonus")
            for c in range(4):
                last = mm(ps[0:8, :], cst[:, C_SEL + 8 * c:C_SEL + 8 * c + 8], cum[:, c, :], c == 0, c == 3)
            end(last, "rw bonus")
            for n in range(2, 5):
                early(("rw sums", n))
            pe.wait_ge(s_rw_state, 1)
            for c in range(TB):
                toks = slice(c * P, c * P + P)
                for x_, src in enumerate((V, K, B)):
                    ps = begin("rw tok", c, x_)
                    for b in range(4):
                        last = t.transpose(ps[:, b * P:b * P + P], src[:, b, toks], ident)
                    end(last, "rw tok", c, x_)
                early(("rw tok", c))
                for g in range(2):
                    rows = slice(64 * g, 64 * g + 64)
                    for hl in range(4):
                        ps = begin("rw sc", c, g, hl)
                        for n, (key, query) in enumerate(((B, A), (B, R), (K, A), (K, R))):
                            last = mm(ps[:, P * n:P * n + P], key[rows, hl, toks], query[rows, hl, toks])
                        end(last, "rw sc", c, g, hl)
                    ps = begin("rw n", c, g)
                    for hl in range(4):
                        last = mm(ps[:, hl * P:hl * P + P], A[rows, hl, toks], B[rows, hl, toks])
                    end(last, "rw n", c, g)
                early(("rw x", c))

                def heads(g):
                    return [(hl, slice(hl * P, hl * P + P)) for hl in range(4)]

                for i in range(1, LEVELS):
                    for g in range(2):
                        if i == 1:
                            pe.wait_ge(s_rw_x, 2 * c + g + 1)
                        else:
                            pe.wait_ge(*freed("rw pt", c, g, i - 1))
                        ps = begin("rw t", c, g, i)
                        for hl, at_ in heads(g):
                            last = mm(ps[:, at_], SC[g][:, hl, 0:P], X[:, g, at_])
                        end(last, "rw t", c, g, i)
                    for g in range(2):
                        pe.wait_ge(*freed("rw t", c, g, i))
                        if i < LEVELS - 1:
                            ps = begin("rw p", c, g, i)
                            for hl, at_ in heads(g):
                                last = mm(ps[:, at_], XT[:, g, at_], LX[:, g, at_])
                            end(last, "rw p", c, g, i)
                        ps = begin("rw pt", c, g, i)
                        for hl, at_ in heads(g):
                            last = mm(ps[:, at_], LX[:, g, at_], XT[:, g, at_])
                        end(last, "rw pt", c, g, i)
                for g in range(2):
                    pe.wait_ge(s_rw_state, 2 * c + g if c else 1)
                    for x_ in range(3) if g == 0 else ():
                        pe.wait_ge(*freed("rw tok", c, x_))
                    ps = begin("rw r", c, g)
                    rows = slice(64 * g, 64 * g + 64)
                    for hl in range(4):
                        cols_, head = slice(64 * hl, 64 * hl + 64), 2 * hl + g
                        mm(ps[:, cols_], A[rows, hl, toks], M[rows, hl, :], True, False)
                        last = mm(ps[:, cols_], SC[g][:, hl, 256:384], tok[:, 0, 64 * head:64 * head + 64], False, True)
                    end(last, "rw r", c, g)
                early(("rw r", c))
                for g in range(2):
                    pe.wait_ge(*freed("rw pt", c, g, LEVELS - 1))
                    pe.wait_ge(*freed("rw r", c, g))
                    ps = begin("rw u", c, g)
                    for hl, at_ in heads(g):
                        last = mm(ps[:, 64 * hl:64 * hl + 64], XT[:, g, at_], rhs_u[:, g, 64 * hl:64 * hl + 64])
                    end(last, "rw u", c, g)
                early(("rw u", c))
                for g in range(2):
                    pe.wait_ge(*freed("rw u", c, g))
                    ps = begin("rw o", c, g)
                    for hl in range(4):
                        head, rows = 2 * hl + g, slice(64 * g, 64 * g + 64)
                        o = ps[rows, P * hl:P * hl + P]
                        mm(o, tok[:, 0, 64 * head:64 * head + 64], SC[g][:, hl, 384:512], True, False)
                        mm(o, U[:, g, 64 * hl:64 * hl + 64], SC[g][:, hl, 128:256], False, False)
                        last = mm(o, M[rows, hl, :], R[rows, hl, toks], False, True)
                    end(last, "rw o", c, g)
                for g in range(2) if c < TB - 1 else ():
                    ps = begin("rw m", c, g)
                    for hl in range(4):
                        head = 2 * hl + g
                        o = ps[64 * g:64 * g + 64, 64 * hl:64 * hl + 64]
                        at_ = slice(64 * head, 64 * head + 64)
                        mm(o, tok[:, 1, at_], tok[:, 0, at_], True, False)
                        last = mm(o, tok[:, 2, at_], U[:, g, 64 * hl:64 * hl + 64], False, True)
                    end(last, "rw m", c, g)
            early("rw mean")
            pe.wait_ge(*freed("rw o", TB - 1, 1))
            for c in range(4):
                ps = begin("rw mean", c)
                end(mm(ps[:, :], pair_ones, R[:, c, :]), "rw mean", c)
            for c in range(4):
                ps = begin("rw bv", c)
                end(mm(ps[:, :], cst[0:8, C_SELT + P * c:C_SELT + P * c + P], bonus[:, :]), "rw bv", c)
            early("rw var")
            pe.wait_ge(s_rw_sq, 1)
            for c in range(4):
                ps = begin("rw var", c)
                end(mm(ps[:, :], pair_ones, epi[:, c, :]), "rw var", c)
            pe.wait_ge(s_rw_lora, 2)
            for c in range(4):
                ps = begin("rw g", c)
                end(mm(ps[:, :], lora_w[:, 1, c * P:c * P + P], gate_lo[:, :]), "rw g", c)
            early("rw g")
            early("rw past")
            moving_units(h_in, [("hg v", tb) for tb in range(TB)])
            early(("hg z", 0))
            early(("hg z", 1))
            pe.wait_ge(s_hg_key, 1)
            for lev in range(LEVELS + 1):
                if lev:
                    early(("hg sc", lev))
                    pe.wait_ge(s_hg_lev, lev)
                else:
                    pe.wait_ge(s_hq_in, 16)
                q, k_ = (q_lev, k_lev) if lev else (Hq, Hk)
                for c in range(TB):
                    ps = begin("hg sc", lev, c)
                    for h in range(4):
                        last = mm(ps[:, h * P:h * P + P], k_[:, h, c * P:c * P + P], q[:, h, c * P:c * P + P])
                    end(last, "hg sc", lev, c)
            early("hg past")
            early("hg left")
            pe.wait_ge(s_hg_k_left, 1)
            for c in range(TB):
                early(("hg tok", c))
                ps = begin("hg tok", c)
                for h in range(4):
                    last = t.transpose(ps[:, h * P:h * P + P], Hk[:, h, c * P:c * P + P], ident)
                end(last, "hg tok", c)
                if c:
                    pe.wait_ge(*freed("hg s", c - 1))
                ps = begin("hg o", c)
                for h in range(4):
                    o, v_ = ps[:, h * P:h * P + P], Hv[:, c, h * P:h * P + P]
                    last = mm(o, v_, ST[:, c, h, :], True, c == 0)
                    if c:
                        last = mm(o, Hs[:, h, :], Hq[:, h, c * P:c * P + P], False, True)
                end(last, "hg o", c)
                if c < TB - 1:
                    pe.wait_ge(*freed("hg tok", c))
                    ps = begin("hg s", c)
                    for h in range(4):
                        last = mm(ps[:, h * P:h * P + P], k_tok[:, h * P:h * P + P], Hv[:, c, h * P:h * P + P])
                    end(last, "hg s", c)
            early("hg ss")
            pe.wait_ge(s_hg_sq, 1)
            for h in range(4):
                ps = begin("hg ss", h)
                end(mm(ps[:, :], ones, k_lev[:, h, :]), "hg ss", h)
            def rotated(ns):
                for n in ns:
                    pe.wait_ge(s_qk_in, 16)
                    ps = begin("da rot", n)
                    end(mm(ps[:, :], cst[:, C_PERM:C_PERM + P], qk[:, n // 4, n % 4, :]), "da rot", n)

            moving_units(h_in, [("da v", tb) for tb in range(TB)], between=lambda: rotated(range(4)))
            rotated(range(4, 8))
            late_ada()
            pe.wait_ge(s_roped, 8)
            for tb in range(TB):
                pe.wait_ge(*freed("da v", tb))

            def scores(t_):
                h, i = divmod(t_, TB)
                n = (i + 1) * P
                for m in range(2):
                    rows = slice(64 * m, 64 * m + 64)
                    ps = begin("da s", t_, m)
                    mm(ps[:, 0:n], qk[rows, 0, h, i * P:i * P + P], qk[rows, 1, h, 0:n], True, False)
                    end(mm(ps[:, n - P:n], cst[rows, C_MA:C_MA + P], cst[rows, C_MB:C_MB + P], False, True),
                        "da s", t_, m)

            scores(0)
            scores(1)
            for t_ in range(4 * TB + 3):
                if t_ >= 6 and t_ % 4 == 2:
                    pe.wait_ge(s_da_sq, (t_ - 6) // 4 + 1)
                    ps = begin("da ss", (t_ - 6) // 4)
                    end(mm(ps[:, :], ones, att2[:, :]), "da ss", (t_ - 6) // 4)
                if t_ + 2 < 4 * TB:
                    scores(t_ + 2)
                if t_ in range(3, 4 * TB, 4):
                    late_ada()
                if 1 <= t_ <= 4 * TB:
                    h, i = divmod(t_ - 1, TB)
                    pe.wait_ge(*freed("da pt", t_ - 1))
                    if i == 0:
                        po = begin("da o", h)
                    for j in range(i + 1):
                        last = mm(po[:, i * P:i * P + P], v_tok[:, j, h * P:h * P + P],
                                  probT[(t_ - 1) % 2][:, j * P:j * P + P], j == 0, j == i)
                    if i == TB - 1:
                        end(last, "da o", h)
                if t_ < 4 * TB:
                    pe.wait_ge(s_da_p, t_ + 1)
                    ps = begin("da pt", t_)
                    for j in range(t_ % TB + 1):
                        last = t.transpose(ps[:, j * P:j * P + P], prob[:, t_ % 3, 0, j * P:j * P + P], ident)
                    end(last, "da pt", t_)
            pe.wait_ge(s_da_lo, 4)
            for j in range(4):
                for g, source in enumerate(((oa_hi, oa_lo), (ob_hi, ob_lo))):
                    slot = next_panel()
                    for m in range(2):
                        stationary_unit(slot, m, source, 4, "branch", j, g, m)
            pe.wait_ge(s_merged, KC)
            for n in range(2):
                moving_units((mg_hi, mg_lo), [("out", n, tb) for tb in range(TB)])
            transposes(1, x1_norm, range(KC))
            for j in range(FFN // 256):
                for which in range(2):
                    slot = next_panel()
                    for m in range(2):
                        stationary_unit(slot, m, h_in, KC, "ffn", j, which, m, h_from=None if j or which or m else KC)
                    if which == 0 and j < 4:
                        late_ada()
            tiles = [[begin("down", tb, n) for n in range(2)] for tb in range(TB)]

            def down(slot, kk, tb, n):
                toks, col0 = slice(tb * P, tb * P + P), D * (kk % 2) + T * n
                return split3(tiles[tb][n][:, :], (d_hi[:, kk % 4, toks], d_lo[:, kk % 4, toks]),
                              (whi[:, slot, col0:col0 + T], wlo[:, slot, col0:col0 + T]), kk == 0, kk == FFN // P - 1)

            for kk in range(FFN // P - 4):
                if kk % 2 == 0:
                    slot = next_panel()
                pe.wait_ge(s_d_lo, kk + 1)
                for tb in range(TB):
                    for n in range(2):
                        last = down(slot, kk, tb, n)
                last.then_inc(s_down_k, 1)
            slots = [next_panel(), next_panel()]
            pe.wait_ge(s_d_lo, FFN // P)
            for tb in range(TB):
                for n in range(2):
                    for kk in range(FFN // P - 4, FFN // P):
                        last = down(slots[(kk - (FFN // P - 4)) // 2], kk, tb, n)
                    end(last, "down", tb, n)


def constants():
    import numpy as np
    c = np.zeros((P, NCONST), np.float32)
    i = np.arange(P)
    c[:, C_ID:C_ID + P] = np.eye(P)
    for p in range(P):
        if p % 64 < 32:
            c[p + 32, C_PERM + p] = -1.0
        else:
            c[p - 32, C_PERM + p] = 1.0
    c[:, C_ONES:C_ONES + P] = 1.0
    c[:, C_BLK:C_BLK + P] = i[:, None] // 64 == i[None, :] // 64
    strict, incl = i[:, None] < i[None, :], i[:, None] <= i[None, :]
    for n, part in enumerate((-1.0 * strict, incl, strict, incl)):
        c[:, C_MASK + n * P:C_MASK + n * P + P] = part
    for row in (0, 64):
        c[row, C_MA:C_MA + 64] = 1.0
        c[row, C_MB + 64:C_MB + P] = -2.0 ** 100
    c[:, C_FREQ] = np.float32(10000.0) ** (-(2 * (i % 32)).astype(np.float32) / np.float32(64))
    c[:, C_EPS], c[:, C_GEPS], c[:, C_HPI] = EPS, GN_EPS, TWO_PI / 4
    for b in range(4):
        c[:, C_SEL + 8 * b + 2 * b] = i < 64
        c[:, C_SEL + 8 * b + 2 * b + 1] = i >= 64
        c[2 * b, C_SELT + P * b:C_SELT + P * b + 64] = 1.0
        c[2 * b + 1, C_SELT + P * b + 64:C_SELT + P * b + P] = 1.0
    lev = np.zeros((P, 2 * LEVELS + 1, P), np.float32)
    for n in range(LEVELS):
        s = 1 << n
        same = i[:, None] // (2 * s) == i[None, :] // (2 * s)
        upper = same & (i[:, None] % (2 * s) < s) & (i[None, :] % (2 * s) >= s)
        lev[:, 2 * n, :], lev[:, 2 * n + 1, :] = upper.T, upper
    lev[:, 2 * LEVELS, :] = np.eye(P)
    return c, lev.reshape(P, -1)


def kernel(**inputs):
    import numpy as np
    import concourse.bacc as bacc
    from concourse.bass_utils import run_bass_kernel_spmd

    a = {k: np.ascontiguousarray(v) for k, v in inputs.items()}
    names = ("rw_mu", "rw_w0", "rw_a0", "rw_k_k", "rw_k_a", "rw_r_k", "rw_gn_w", "rw_gn_b",
             "hg_norm_w", "da_subln_w", "norm_mix_w", "norm_ffn_w", "c", "ada_b")
    vecs = np.concatenate([a[n].reshape(-1, P) for n in names])
    consts, levels = constants()
    arrays = {
        "x": a["x"][0], "ada_w": a["ada_w"][0], "w_in": a["w_in"][0],
        "w_a": a["w_branch_a"][0], "w_b": a["w_branch_b"][0], "w_c": a["w_branch_c"][0],
        "w_out": a["w_out"][0], "f_in": a["ffn_w_in"][0], "f_out": a["ffn_w_out"][0],
        "w2": a["rw_w2"][0], "a2": a["rw_a2"][0], "g2": a["rw_g2"][0],
        "vecs": vecs, "consts": consts, "levels": levels,
        "gate_b": a["ada_b"][0], "final_w": a["final_norm_w"], "lam": a["da_lambda"].reshape(-1),
        "positions": a["positions"][0],
    }
    nc = bacc.Bacc("TRN2", target_bir_lowering=False, num_devices=1)
    aps = [nc.dram_tensor(f"in_{k}", v.shape, mybir.dt.from_np(v.dtype), kind="ExternalInput").ap()
           for k, v in arrays.items()]
    aps.append(nc.dram_tensor("out_x", (T, D), F32, kind="ExternalOutput").ap())
    build(nc, *aps)
    r = run_bass_kernel_spmd(nc, [{f"in_{k}": v for k, v in arrays.items()}], core_ids=[0])
    return r.results[0]["out_x"].reshape(1, T, D)
```
